# Optimizing a Trainium2 kernel written in Bass

```python
import jax
import jax.numpy as jnp
from jax import lax
import numpy as np

D_MODEL = 1024
BATCH = 1
SEQ = 512
DEPTH = 2

D_MIX = D_MODEL
D_FF = 4 * D_MODEL
NORM_EPS = 1e-5
SHORT_CONV = 4

ATT_HEAD_DIM = 64
ATT_Q_HEADS = (D_MIX // 2) // ATT_HEAD_DIM
ATT_KV_HEADS = ATT_Q_HEADS // 4
ATT_WINDOW = 128
ROPE_THETA = 500000.0
ROPE_DIM = ATT_HEAD_DIM // 4

ML_HEADS = 4
ML_V_DIM = (D_MIX // 2) // ML_HEADS
ML_QK_DIM = ML_V_DIM // 2
ML_CHUNK = 128
ML_NORM_EPS = 1e-6

SSM_HEAD_DIM = 64
SSM_HEADS = (D_MIX // 2) // SSM_HEAD_DIM
SSM_GROUPS = 2
SSM_STATE = 128
SSM_CHUNK = 128

RW_HEAD_DIM = 64
RW_HEADS = (D_MIX // 2) // RW_HEAD_DIM
RW_DECAY_LORA = 64
RW_AAA_LORA = 64
RW_GATE_LORA = 128
RW_LN_EPS = 64e-5

N_EVEN = (DEPTH + 1) // 2
N_ODD = DEPTH // 2

ATT_Q_W = ATT_Q_HEADS * ATT_HEAD_DIM
ATT_KV_W = ATT_KV_HEADS * ATT_HEAD_DIM
ML_QK_W = ML_HEADS * ML_QK_DIM
ML_V_W = ML_HEADS * ML_V_DIM
EVEN_IN = ATT_Q_W + 2 * ATT_KV_W + 2 * ML_QK_W + 2 * ML_V_W + 2 * ML_HEADS
EVEN_OUT = ATT_Q_W + ML_V_W

SSM_INNER = SSM_HEADS * SSM_HEAD_DIM
SSM_BC = SSM_GROUPS * SSM_STATE
SSM_CONV_W = SSM_INNER + 2 * SSM_BC
RW_W = RW_HEADS * RW_HEAD_DIM
RW_IN = 3 * RW_W + RW_DECAY_LORA + RW_AAA_LORA + RW_GATE_LORA
ODD_IN = SSM_INNER + SSM_CONV_W + SSM_HEADS + RW_IN
ODD_OUT = SSM_INNER + RW_W

F32 = jnp.float32

kernel_name = 'hybrid_swa_mlstm_ssd_rwkv7_trunk'

def rmsnorm(x, g):
    xf = x.astype(F32)
    y = xf * lax.rsqrt(jnp.mean(xf * xf, axis=-1, keepdims=True) + NORM_EPS)
    return (y * g.astype(F32)).astype(x.dtype)

def group_rmsnorm(x, g, groups):
    shp = x.shape
    xf = x.astype(F32).reshape(shp[:-1] + (groups, shp[-1] // groups))
    y = xf * lax.rsqrt(jnp.mean(xf * xf, axis=-1, keepdims=True) + NORM_EPS)
    return y.reshape(shp) * g.astype(F32)

def head_layernorm(x, eps):
    xf = x.astype(F32)
    mu = jnp.mean(xf, axis=-1, keepdims=True)
    var = jnp.mean(jnp.square(xf - mu), axis=-1, keepdims=True)
    return (xf - mu) * lax.rsqrt(var + eps)

def split_cols(p, sizes):
    idx = np.cumsum(np.array(sizes))[:-1].tolist()
    return jnp.split(p, idx, axis=-1)

def causal_conv(x, w, b):
    K = w.shape[0]
    T = x.shape[1]
    xp = jnp.pad(x, ((0, 0), (K - 1, 0), (0, 0)))
    out = b
    for tap in range(K):
        out = out + xp[:, tap:tap + T, :] * w[tap]
    return out

def token_shift(x):
    return jnp.pad(x, ((0, 0), (1, 0), (0, 0)))[:, :-1, :]

def partial_rope(x):
    T = x.shape[1]
    half = ROPE_DIM // 2
    inv_freq = ROPE_THETA ** (-jnp.arange(half, dtype=F32) * 2.0 / ROPE_DIM)
    ang = jnp.arange(T, dtype=F32)[:, None] * inv_freq[None, :]
    cos = jnp.cos(ang)[None, :, None, :]
    sin = jnp.sin(ang)[None, :, None, :]
    xf = x.astype(F32)
    x1 = xf[..., :half]
    x2 = xf[..., half:ROPE_DIM]
    rot = jnp.concatenate([x1 * cos - x2 * sin, x2 * cos + x1 * sin, xf[..., ROPE_DIM:]], axis=-1)
    return rot.astype(x.dtype)

def sliding_window_sink_attention(q, k, v, sinks):
    bsz, T, hq, dh = q.shape
    hkv = k.shape[2]
    grp = hq // hkv
    W = ATT_WINDOW
    nb = T // W
    qb = q.reshape(bsz, nb, W, hkv, grp, dh)

    def band(t):
        tp = jnp.pad(t, ((0, 0), (W, 0), (0, 0), (0, 0)))
        prev = tp[:, :T].reshape(bsz, nb, W, hkv, dh)
        cur = t.reshape(bsz, nb, W, hkv, dh)
        return jnp.concatenate([prev, cur], axis=2)

    kb = band(k)
    vb = band(v)
    s = jnp.einsum('bnqhgd,bnkhd->bhgnqk', qb, kb).astype(F32) * (dh ** -0.5)
    i = jnp.arange(W)[:, None]
    j = jnp.arange(2 * W)[None, :]
    blk = jnp.arange(nb)[:, None, None]
    mask = (j > i) & (j <= i + W) & (blk * W - W + j >= 0)
    s = jnp.where(mask, s, -jnp.inf)
    sink = sinks.astype(F32).reshape(hkv, grp, 1, 1, 1)
    m = jnp.maximum(jnp.max(s, axis=-1, keepdims=True), sink)
    p = jnp.exp(s - m)
    p = p / (jnp.sum(p, axis=-1, keepdims=True) + jnp.exp(sink - m))
    o = jnp.einsum('bhgnqk,bnkhd->bnqhgd', p.astype(v.dtype), vb)
    return o.reshape(bsz, T, hq * dh)

def mlstm_chunkwise(q, k, v, log_i, log_f):
    bsz, T, H, dk = q.shape
    dv = v.shape[-1]
    L = ML_CHUNK
    nc = T // L
    qc = q.astype(F32).reshape(bsz, nc, L, H, dk)
    kc = k.astype(F32).reshape(bsz, nc, L, H, dk) * (dk ** -0.5)
    vc = v.astype(F32).reshape(bsz, nc, L, H, dv)
    li = log_i.reshape(bsz, nc, L, H)
    b = jnp.cumsum(log_f.reshape(bsz, nc, L, H), axis=2)
    causal = jnp.tril(jnp.ones((L, L), dtype=bool))
    dlog = b[:, :, :, None, :] - b[:, :, None, :, :] + li[:, :, None, :, :]
    dlog = jnp.where(causal[None, None, :, :, None], dlog, -jnp.inf)
    bL = b[:, :, -1, :]
    a = bL[:, :, None, :] - b + li
    m_loc = jnp.max(a, axis=2)
    wgt = jnp.exp(a - m_loc[:, :, None, :])
    C_loc = jnp.einsum('bnlh,bnlhk,bnlhv->bnhkv', wgt, kc, vc)
    n_loc = jnp.einsum('bnlh,bnlhk->bnhk', wgt, kc)

    def step(carry, inp):
        C, n, m = carry
        Cl, nl, ml, gl = inp
        m_new = jnp.maximum(gl + m, ml)
        fa = jnp.exp(gl + m - m_new)
        fb = jnp.exp(ml - m_new)
        C_new = fa[..., None, None] * C + fb[..., None, None] * Cl
        n_new = fa[..., None] * n + fb[..., None] * nl
        return (C_new, n_new, m_new), (C, n, m)

    init = (jnp.zeros((bsz, H, dk, dv), F32), jnp.zeros((bsz, H, dk), F32), jnp.zeros((bsz, H), F32))
    xs = (jnp.moveaxis(C_loc, 1, 0), jnp.moveaxis(n_loc, 1, 0), jnp.moveaxis(m_loc, 1, 0), jnp.moveaxis(bL, 1, 0))
    _, (C_prev, n_prev, m_prev) = lax.scan(step, init, xs)
    C_prev = jnp.moveaxis(C_prev, 0, 1)
    n_prev = jnp.moveaxis(n_prev, 0, 1)
    m_prev = jnp.moveaxis(m_prev, 0, 1)
    inter_log = b + m_prev[:, :, None, :]
    m_t = jnp.maximum(inter_log, jnp.max(dlog, axis=3))
    w_intra = jnp.exp(dlog - m_t[:, :, :, None, :])
    w_inter = jnp.exp(inter_log - m_t)
    qk = jnp.einsum('bnthd,bnshd->bntsh', qc, kc) * w_intra
    num = jnp.einsum('bntsh,bnshv->bnthv', qk, vc) + w_inter[..., None] * jnp.einsum('bnthk,bnhkv->bnthv', qc, C_prev)
    den = jnp.sum(qk, axis=3) + w_inter * jnp.einsum('bnthk,bnhk->bnth', qc, n_prev)
    h = num / jnp.maximum(jnp.abs(den), jnp.exp(-m_t))[..., None]
    return h.reshape(bsz, T, H, dv)

def ssd_chunked(x, dt, A, Bm, Cm):
    bsz, T, H, P = x.shape
    G = Bm.shape[2]
    N = Bm.shape[-1]
    hg = H // G
    L = SSM_CHUNK
    nc = T // L
    xc = (x.astype(F32) * dt[..., None]).reshape(bsz, nc, L, G, hg, P)
    a_cum = jnp.cumsum((dt * A.astype(F32)).reshape(bsz, nc, L, G, hg), axis=2)
    Bc = Bm.astype(F32).reshape(bsz, nc, L, G, N)
    Cc = Cm.astype(F32).reshape(bsz, nc, L, G, N)
    causal = jnp.tril(jnp.ones((L, L), dtype=bool))[:, :, None, None]
    seg = a_cum[:, :, :, None] - a_cum[:, :, None, :]
    decay = jnp.exp(jnp.where(causal, seg, -jnp.inf))
    cb = jnp.einsum('bctgn,bcsgn->bctsg', Cc, Bc)
    y_diag = jnp.einsum('bctsgh,bcsghp->bctghp', cb[..., None] * decay, xc)
    decay_s = jnp.exp(a_cum[:, :, -1:] - a_cum)
    states = jnp.einsum('bclgn,bclgh,bclghp->bcghpn', Bc, decay_s, xc)
    chunk_decay = jnp.exp(a_cum[:, :, -1])

    def step(S, inp):
        st, dec = inp
        return S * dec[..., None, None] + st, S

    S0 = jnp.zeros((bsz, G, hg, P, N), F32)
    _, S_prev = lax.scan(step, S0, (jnp.moveaxis(states, 1, 0), jnp.moveaxis(chunk_decay, 1, 0)))
    S_prev = jnp.moveaxis(S_prev, 0, 1)
    y_off = jnp.einsum('bctgn,bcghpn->bctghp', Cc, S_prev) * jnp.exp(a_cum)[..., None]
    return (y_diag + y_off).reshape(bsz, T, H, P)

def rwkv7_scan(r, w, k, v, kk, kka):
    bsz, T, H, dh = r.shape

    def step(S, inp):
        r_t, w_t, k_t, v_t, kk_t, b_t = inp
        sa = jnp.einsum('bhvk,bhk->bhv', S, kk_t)
        S = S * w_t[:, :, None, :] - sa[..., None] * b_t[:, :, None, :] + v_t[..., None] * k_t[:, :, None, :]
        return S, jnp.einsum('bhvk,bhk->bhv', S, r_t)

    xs = (jnp.moveaxis(r, 1, 0), jnp.moveaxis(w, 1, 0), jnp.moveaxis(k, 1, 0), jnp.moveaxis(v, 1, 0), jnp.moveaxis(kk, 1, 0), jnp.moveaxis(kka, 1, 0))
    S0 = jnp.zeros((bsz, H, dh, dh), F32)
    _, y = lax.scan(step, S0, xs)
    return jnp.moveaxis(y, 0, 1)

def even_mixer(h, w_in, w_out, sinks, conv_w, conv_b, i_bias, f_bias, ml_norm):
    bsz, T, _ = h.shape
    p = h @ w_in
    q_a, k_a, v_a, qk_m, v_m, o_m, i_m, f_m = split_cols(p, (ATT_Q_W, ATT_KV_W, ATT_KV_W, 2 * ML_QK_W, ML_V_W, ML_V_W, ML_HEADS, ML_HEADS))
    q = partial_rope(q_a.reshape(bsz, T, ATT_Q_HEADS, ATT_HEAD_DIM))
    k = partial_rope(k_a.reshape(bsz, T, ATT_KV_HEADS, ATT_HEAD_DIM))
    v = v_a.reshape(bsz, T, ATT_KV_HEADS, ATT_HEAD_DIM)
    y_att = sliding_window_sink_attention(q, k, v, sinks)
    qk = jax.nn.silu(causal_conv(qk_m, conv_w, conv_b))
    q_m, k_m = jnp.split(qk, 2, axis=-1)
    log_f = jax.nn.log_sigmoid(f_m.astype(F32) + f_bias.astype(F32))
    log_i = i_m.astype(F32) + i_bias.astype(F32)
    hm = mlstm_chunkwise(q_m.reshape(bsz, T, ML_HEADS, ML_QK_DIM), k_m.reshape(bsz, T, ML_HEADS, ML_QK_DIM), v_m.reshape(bsz, T, ML_HEADS, ML_V_DIM), log_i, log_f)
    hm = head_layernorm(hm, ML_NORM_EPS).reshape(bsz, T, ML_V_W) * ml_norm.astype(F32)
    y_ml = (hm * jax.nn.sigmoid(o_m.astype(F32))).astype(h.dtype)
    return jnp.concatenate([y_att, y_ml], axis=-1) @ w_out

def odd_mixer(h, w_in, w_out, ssm_conv_w, ssm_conv_b, ssm_dt_bias, ssm_a_log, ssm_d, ssm_norm,
              rw_mu, rw_w0, rw_w2, rw_a0, rw_a2, rw_g2, rw_k_k, rw_k_a, rw_r_k, rw_ln_w, rw_ln_b):
    bsz, T, _ = h.shape
    p = h @ w_in
    z, xbc, dt_raw, rw = split_cols(p, (SSM_INNER, SSM_CONV_W, SSM_HEADS, RW_IN))
    xbc = jax.nn.silu(causal_conv(xbc, ssm_conv_w, ssm_conv_b))
    xs, Bm, Cm = split_cols(xbc, (SSM_INNER, SSM_BC, SSM_BC))
    dt = jax.nn.softplus(dt_raw.astype(F32) + ssm_dt_bias.astype(F32))
    A = -jnp.exp(ssm_a_log.astype(F32))
    xh = xs.reshape(bsz, T, SSM_HEADS, SSM_HEAD_DIM)
    y = ssd_chunked(xh, dt, A, Bm.reshape(bsz, T, SSM_GROUPS, SSM_STATE), Cm.reshape(bsz, T, SSM_GROUPS, SSM_STATE))
    y = y + ssm_d.astype(F32)[None, None, :, None] * xh.astype(F32)
    y = y.reshape(bsz, T, SSM_INNER) * jax.nn.silu(z.astype(F32))
    y_ssm = group_rmsnorm(y, ssm_norm, SSM_GROUPS).astype(h.dtype)
    rw = rw + (token_shift(rw) - rw) * rw_mu
    r, k, v, wd, ad, gd = split_cols(rw, (RW_W, RW_W, RW_W, RW_DECAY_LORA, RW_AAA_LORA, RW_GATE_LORA))
    w_log = -jax.nn.softplus(-(rw_w0 + jnp.tanh(wd) @ rw_w2).astype(F32)) - 0.5
    decay = jnp.exp(-jnp.exp(w_log))
    a = jax.nn.sigmoid((rw_a0 + ad @ rw_a2).astype(F32))
    g = (jax.nn.sigmoid(gd) @ rw_g2).astype(F32)
    hd = (bsz, T, RW_HEADS, RW_HEAD_DIM)
    rh = r.astype(F32).reshape(hd)
    kh = k.astype(F32).reshape(hd)
    vh = v.astype(F32).reshape(hd)
    ah = a.reshape(hd)
    kk = kh * rw_k_k.astype(F32).reshape(RW_HEADS, RW_HEAD_DIM)
    kk = kk / jnp.maximum(jnp.sqrt(jnp.sum(kk * kk, axis=-1, keepdims=True)), 1e-12)
    kh = kh * (1.0 + (ah - 1.0) * rw_k_a.astype(F32).reshape(RW_HEADS, RW_HEAD_DIM))
    yr = rwkv7_scan(rh, decay.reshape(hd), kh, vh, kk, kk * ah)
    yr = head_layernorm(yr, RW_LN_EPS).reshape(bsz, T, RW_W) * rw_ln_w.astype(F32) + rw_ln_b.astype(F32)
    bonus = (jnp.sum(rh * kh * rw_r_k.astype(F32), axis=-1, keepdims=True) * vh).reshape(bsz, T, RW_W)
    y_rw = ((yr + bonus) * g).astype(h.dtype)
    return jnp.concatenate([y_ssm, y_rw], axis=-1) @ w_out

def squared_relu_mlp(h, w_up, w_down):
    return jnp.square(jax.nn.relu(h @ w_up)) @ w_down

def setup_inputs(seed: int = 0) -> dict:
    key = jax.random.key(seed)
    keys = iter(jax.random.split(key, 48))

    def normal(shape, scale):
        return jax.random.normal(next(keys), shape, F32) * scale

    def gain(shape):
        return 1.0 + normal(shape, 0.05)

    def unif(shape, lo, hi):
        return jax.random.uniform(next(keys), shape, F32, lo, hi)

    E, O, L = N_EVEN, N_ODD, DEPTH
    x = normal((BATCH, SEQ, D_MODEL), 1.0)
    mix_norm = gain((L, D_MODEL))
    mlp_norm = gain((L, D_MODEL))
    w_up = normal((L, D_MODEL, D_FF), D_MODEL ** -0.5)
    w_down = normal((L, D_FF, D_MODEL), D_FF ** -0.5)
    e_w_in = normal((E, D_MODEL, EVEN_IN), D_MODEL ** -0.5)
    e_w_out = normal((E, EVEN_OUT, D_MODEL), EVEN_OUT ** -0.5)
    att_sinks = normal((E, ATT_Q_HEADS), 1.0)
    ml_conv_w = normal((E, SHORT_CONV, 2 * ML_QK_W), SHORT_CONV ** -0.5)
    ml_conv_b = normal((E, 2 * ML_QK_W), 0.02)
    ml_i_bias = normal((E, ML_HEADS), 0.1)
    ml_f_bias = jnp.linspace(3.0, 6.0, ML_HEADS)[None, :] + normal((E, ML_HEADS), 0.1)
    ml_norm = gain((E, ML_V_W))
    o_w_in = normal((O, D_MODEL, ODD_IN), D_MODEL ** -0.5)
    o_w_out = normal((O, ODD_OUT, D_MODEL), ODD_OUT ** -0.5)
    ssm_conv_w = normal((O, SHORT_CONV, SSM_CONV_W), SHORT_CONV ** -0.5)
    ssm_conv_b = normal((O, SSM_CONV_W), 0.02)
    dt0 = jnp.exp(unif((O, SSM_HEADS), float(np.log(1e-3)), float(np.log(1e-1))))
    ssm_dt_bias = dt0 + jnp.log(-jnp.expm1(-dt0))
    ssm_a_log = jnp.log(unif((O, SSM_HEADS), 1.0, 16.0))
    ssm_d = gain((O, SSM_HEADS))
    ssm_norm = gain((O, SSM_INNER))
    rw_mu = unif((O, RW_IN), 0.0, 1.0)
    rw_w0 = jnp.tile(jnp.linspace(-6.0, -0.5, RW_HEAD_DIM), RW_HEADS)[None, :] + normal((O, RW_W), 0.1)
    rw_w2 = normal((O, RW_DECAY_LORA, RW_W), 0.1)
    rw_a0 = normal((O, RW_W), 0.1)
    rw_a2 = normal((O, RW_AAA_LORA, RW_W), 0.1)
    rw_g2 = normal((O, RW_GATE_LORA, RW_W), RW_GATE_LORA ** -0.5)
    rw_k_k = 0.85 + normal((O, RW_W), 0.05)
    rw_k_a = gain((O, RW_W))
    rw_r_k = normal((O, RW_HEADS, RW_HEAD_DIM), 0.1)
    rw_ln_w = gain((O, RW_W))
    rw_ln_b = normal((O, RW_W), 0.02)
    final_norm = gain((D_MODEL,))
    return {'x': x, 'mix_norm': mix_norm, 'mlp_norm': mlp_norm, 'w_up': w_up, 'w_down': w_down,
            'e_w_in': e_w_in, 'e_w_out': e_w_out, 'att_sinks': att_sinks, 'ml_conv_w': ml_conv_w,
            'ml_conv_b': ml_conv_b, 'ml_i_bias': ml_i_bias, 'ml_f_bias': ml_f_bias, 'ml_norm': ml_norm,
            'o_w_in': o_w_in, 'o_w_out': o_w_out, 'ssm_conv_w': ssm_conv_w, 'ssm_conv_b': ssm_conv_b,
            'ssm_dt_bias': ssm_dt_bias, 'ssm_a_log': ssm_a_log, 'ssm_d': ssm_d, 'ssm_norm': ssm_norm,
            'rw_mu': rw_mu, 'rw_w0': rw_w0, 'rw_w2': rw_w2, 'rw_a0': rw_a0, 'rw_a2': rw_a2, 'rw_g2': rw_g2,
            'rw_k_k': rw_k_k, 'rw_k_a': rw_k_a, 'rw_r_k': rw_r_k, 'rw_ln_w': rw_ln_w, 'rw_ln_b': rw_ln_b,
            'final_norm': final_norm}

def reference(x, mix_norm, mlp_norm, w_up, w_down, e_w_in, e_w_out, att_sinks, ml_conv_w, ml_conv_b,
              ml_i_bias, ml_f_bias, ml_norm, o_w_in, o_w_out, ssm_conv_w, ssm_conv_b, ssm_dt_bias,
              ssm_a_log, ssm_d, ssm_norm, rw_mu, rw_w0, rw_w2, rw_a0, rw_a2, rw_g2, rw_k_k, rw_k_a,
              rw_r_k, rw_ln_w, rw_ln_b, final_norm):
    h = x
    for layer in range(DEPTH):
        hn = rmsnorm(h, mix_norm[layer])
        if layer % 2 == 0:
            e = layer // 2
            h = h + even_mixer(hn, e_w_in[e], e_w_out[e], att_sinks[e], ml_conv_w[e], ml_conv_b[e],
                               ml_i_bias[e], ml_f_bias[e], ml_norm[e])
        else:
            o = layer // 2
            h = h + odd_mixer(hn, o_w_in[o], o_w_out[o], ssm_conv_w[o], ssm_conv_b[o], ssm_dt_bias[o],
                              ssm_a_log[o], ssm_d[o], ssm_norm[o], rw_mu[o], rw_w0[o], rw_w2[o],
                              rw_a0[o], rw_a2[o], rw_g2[o], rw_k_k[o], rw_k_a[o], rw_r_k[o],
                              rw_ln_w[o], rw_ln_b[o])
        h = h + squared_relu_mlp(rmsnorm(h, mlp_norm[layer]), w_up[layer], w_down[layer])
    return rmsnorm(h, final_norm)


_drawn_inputs = setup_inputs


def setup_inputs(seed=0):
    import zlib

    import numpy as np

    out = dict(_drawn_inputs(seed))
    spreads = {}
    factors = {'att_sinks': 6.26,
     'ml_conv_b': 4.911,
     'ml_i_bias': 8.0,
     'ssm_conv_b': 5.465,
     'ssm_d': 5.597,
     'ssm_norm': 2.798,
     'rw_w2': 3.574,
     'rw_a0': 6.334,
     'rw_ln_w': 4.568,
     'rw_ln_b': 8.0}
    for name, (base, spread) in spreads.items():
        noise = np.random.default_rng([zlib.crc32(name.encode()), seed]).standard_normal(out[name].shape)
        drawn = base * np.exp(spread * noise) if base else spread * noise
        out[name] = jnp.asarray(drawn.astype(out[name].dtype))
    for name, factor in factors.items():
        out[name] = (out[name] * factor).astype(out[name].dtype)
    return out
```

```python
from contextlib import ExitStack

import numpy as np
import concourse.bass as bass
from concourse import mybir

F32 = mybir.dt.float32
ALU = mybir.AluOpType
ACT = mybir.ActivationFunctionType
AX = mybir.AxisListType

P = 128
T = 512
NT = T // P
D = 1024
KT = D // P
FF = 4096
FT = FF // P
SW = 256
RING = 4
NBANK = 8
BANK = 512
NEG = -1.0e30
HUGE = 1.0e38
DECAY_K = float(np.exp(np.float32(-0.5)))

_i = np.arange(P)
_row, _col = _i[:, None], _i[None, :]


def _const_columns():
    half = 8
    inv = np.float32(500000.0) ** (-np.arange(half, dtype=np.float32) * np.float32(2.0) / np.float32(16))
    ang = (np.arange(T, dtype=np.float32)[:, None] * inv[None, :]).astype(np.float32)
    cos, sin = np.ones((P, T), np.float32), np.zeros((P, T), np.float32)
    rot = np.zeros((P, P), np.float32)
    for base in (0, 64):
        for j in range(half):
            cos[base + j] = cos[base + half + j] = np.cos(ang[:, j])
            sin[base + j] = sin[base + half + j] = np.sin(ang[:, j])
            rot[base + half + j, base + j] = -1.0
            rot[base + j, base + half + j] = 1.0
    dup = np.zeros((P, 2, P), np.float32)
    for g in range(2):
        for m in range(P):
            dup[64 * g + m % 64, g, m] = 1.0
    k = np.arange(2 * P)[None, :]
    band = np.where((k > _row) & (k <= _row + P), 0.0, NEG)
    first = np.where((k > _row) & (k <= _row + P) & (k >= P), 0.0, NEG)
    even = [("cos", cos), ("sin", sin), ("rot", rot), ("dup", dup.reshape(P, -1)), ("band", band), ("first", first)]
    common = [
        ("ident", np.eye(P)), ("ones", np.ones((P, P))),
        ("upper", _row <= _col),
        ("blocks", (_row // 64) == (_col // 64)),
        ("add_st", np.where(_row <= _col, 0.0, NEG)),
        ("add_ts", np.where(_col <= _row, 0.0, NEG)),
        ("eps", np.repeat(np.array([[1e-5, 1e-6, 64e-5, 0.0]]), P, 0)),
    ]
    levels = []
    for b in (1, 2, 4, 8, 16, 32, 64):
        levels.append(((_col // b) % 2 == 1) & ((_row // b) == (_col // b) - 1))
    reset = np.ones((P, T))
    reset[:, ::P] = 0.0
    odd = [
        ("levels", np.concatenate(levels, 1)),
        ("four", np.concatenate([_col < _row, _row < _col, _row <= _col, _row <= _col], 1)),
        ("reset", reset),
        ("heads", np.stack([_i // 64 == 0, _i // 64 == 1], 1)),
    ]
    return common + odd, even


def _offsets(cols):
    at, out = 0, {}
    for name, a in cols:
        out[name] = (at, a.shape[1])
        at += a.shape[1]
    return out, at


MAIN_COLS, EVEN_COLS = _const_columns()
MAIN_AT, MAIN_W = _offsets(MAIN_COLS)
EVEN_AT, EVEN_W = _offsets(EVEN_COLS)

STACK_A = [("mix_norm", 16), ("mlp_norm", 16), ("final_norm", 8), ("ml_conv_w", 16), ("ml_conv_b", 4),
           ("ssm_conv_w", 32), ("ssm_conv_b", 8)]
STACK_B = [("rw_mu", 14), ("rw_w0", 4), ("rw_a0", 4), ("rw_k_k", 4), ("rw_k_a", 4), ("rw_r_k", 4)]
ROWS = [("att_sinks", 8), ("ml_i_bias", 4), ("ml_f_bias", 4), ("ssm_dt_bias", 8), ("ssm_a_log", 8), ("ssm_d", 8),
        ("ml_norm", 512), ("ssm_norm", 512), ("rw_ln_w", 512), ("rw_ln_b", 512)]


def _starts(spec):
    at, out = 0, {}
    for name, n in spec:
        out[name] = at
        at += n
    return out, at


A_AT, A_N = _starts(STACK_A)
B_AT, B_N = _starts(STACK_B)
R_AT, R_N = _starts(ROWS)

E_GATES, E_Q, E_KV, E_QK, E_V, E_O = 2304, 0, 512, 768, 1280, 1792
EVEN_SLOTS = [(E_GATES, 8, "gates"), (0, SW, "q"), (SW, SW, "q"), (E_KV, SW, "kv"), (E_QK, SW, "qk"), (E_QK + SW, SW, "qk"),
              (E_V, SW, "v"), (E_V + SW, SW, "v"), (E_O, SW, "o"), (E_O + SW, SW, "o")]
O_Z, O_XBC, O_DT, O_RW = 0, 512, 1536, 1544
ODD_SLOTS = ([(O_DT, 8, "dt"), (O_Z, SW, "z"), (O_Z + SW, SW, "z")] + [(O_XBC + SW * j, SW, "xbc") for j in range(4)]
             + [(O_RW + SW * j, SW, "rw") for j in range(7)])
LEVELS = 7
STAGE_AT = 21120
ARENA = STAGE_AT + 2 * P


class Plan:

    def __init__(self):
        self.turns = [0] * NBANK
        self.at = {}
        self.next = 0

    def put(self, *key, bank=None, times=1):
        if bank is None:
            bank = self.next
            self.next = (self.next + 1) % NBANK
        assert key not in self.at, key
        self.at[key] = (bank, self.turns[bank])
        self.turns[bank] += times


def make_plan():
    plan = Plan()
    put = plan.put
    put("stack_a")
    put("stack_b")
    for k in range(KT):
        put("x", k)
    for layer in range(2):
        put("norm", 2 * layer)
        if layer == 0:
            put("gates")
            for i in range(4):
                put("q", i)
            put("k")
            put("v_att")
            for i in range(4):
                put("qk", i)
            for half in range(2):
                for pair in range(2):
                    put("v", half, pair)
            for half in range(2):
                for pair in range(2):
                    put("o", half, pair)
            for i in range(5):
                put("rope", i)
            for g in range(2):
                put("dup", g)
            for u in range(8 + 2):
                if u < 8:
                    put("score", u, 0)
                    put("score", u, 1)
                if 1 <= u < 9:
                    put("turn", u - 1, 0)
                    put("turn", u - 1, 1)
                if u >= 2:
                    put("att", u - 2)
            put("cum")
            for n in range(NT):
                put("g_row", n)
            for a in range(2):
                put("k_tok", a)
            for n in range(NT):
                put("m_row", n)
            for n in range(NT):
                for par in range(2):
                    put("qk_st", n, par)
                if n < NT - 1:
                    for a in range(2):
                        put("c_loc", n, a)
                for a in range(2):
                    put("num", n, a)
                if n:
                    for par in range(2):
                        put("inter", n, par)
            for f in range(4):
                put("y_ml", f)
        else:
            put("dt")
            for half in range(2):
                for pair in range(2):
                    put("z", half, pair)
            for i in range(8):
                put("xbc", i)
            for i in range(14):
                put("rw", i)
            put("a_cum")
            for n in range(NT):
                put("x_tok", n)
                put("b_tok", n)
                put("a_row", n, 0)
                put("a_row", n, 1)
                put("cb", n)
                put("y_diag", n)
                if n:
                    put("y_off", n)
                if n < NT - 1:
                    put("s_loc", n)
            for f in range(4):
                put("y_ssm", f)
            for f in range(4):
                put("decay", f)
                put("a", f)
                put("kk_sum", f)
            for n in range(NT):
                put("g_tok", n)
            for n in range(NT):
                put("rv_tok", n)
            put("bonus")
            for n in range(NT):
                put("rk_tok", n)
                put("rb_tok", n)
                for f in range(4):
                    for par in range(2):
                        put("mats", n, f, par)
                for level in range(LEVELS):
                    put("pt", n, level, 0)
                    put("pt", n, level, 1)
                    for half in range(2):
                        if level < LEVELS - 1:
                            put("d", n, level, half)
                        put("dt_", n, level, half)
                put("rhs", n)
                put("u", n)
                put("y", n)
                if n < NT - 1:
                    put("s_rw", n)
            for f in range(4):
                put("y_rw", f)
        for j in range(4):
            put("out", layer, j, bank=j, times=2)
        put("norm", 2 * layer + 1)
        for j in range(8):
            put("up", layer, j, bank=j, times=4)
        for j in range(2):
            put("down", layer, j, bank=j, times=4)
    put("norm", 4)
    for t in range(NT):
        for half in range(2):
            put("result", t, half)
    return plan


def trunk(nc, dram, out):
    PLAN = make_plan()
    with ExitStack() as ctx:
        def sb(name, width):
            return ctx.enter_context(nc.sbuf_tensor(name, [P, width], F32))

        def sem(name):
            return ctx.enter_context(nc.semaphore(name))

        def cut(tile, at, *shape):
            n = int(np.prod(shape))
            v = tile[:, at:at + n]
            if len(shape) == 2:
                v = v.rearrange("p (a b) -> p a b", b=shape[1])
            if len(shape) == 3:
                v = v.rearrange("p (a b c) -> p a b c", b=shape[1], c=shape[2])
            return v

        ps = ctx.enter_context(nc.psum_tensor("ps", [P, NBANK, BANK], F32))
        h_t = sb("h", KT * T)
        hn_t = sb("hn", KT * T)
        ring_t = sb("ring", RING * KT * SW)
        main_t = sb("main", MAIN_W)
        cols_t = sb("cols", A_N + B_N)
        rows_t = sb("rows", R_N)
        small = sb("small", 640)
        rwkv_raw = sb("rwkv_raw", 14 * (T + 1))
        arena = sb("arena", ARENA)
        rms_t = sb("rms", T)[:, :]
        relu_t = sb("relu", 2 * T)[:, :].rearrange("p (a t) -> p a t", a=2)
        lora = sb("lora", 512 * 2)

        h = cut(h_t, 0, KT, T)
        hn = cut(hn_t, 0, KT, T)
        y_mix = hn
        ring = ring_t[:, :].rearrange("p (r k c) -> p r k c", r=RING, c=SW)

        def const(name):
            at, w = MAIN_AT[name]
            return main_t[:, at:at + w]

        ident, ones, upper, blocks = const("ident"), const("ones"), const("upper"), const("blocks")
        eps = const("eps")

        def col_a(name, i):
            return cols_t[:, A_AT[name] + i:A_AT[name] + i + 1]

        def col_b(name, i):
            return cols_t[:, A_N + B_AT[name] + i:A_N + B_AT[name] + i + 1]

        def row(name, width):
            return rows_t[:, R_AT[name]:R_AT[name] + width]

        def over(ap, axis, n):
            v = ap.unsqueeze(axis)
            shape = list(v.shape)
            shape[axis] = n
            return v.to_broadcast(shape)

        bank_full = [sem(f"bank_full{b}") for b in range(NBANK)]
        bank_free = [sem(f"bank_free{b}") for b in range(NBANK)]
        w_full = [sem(f"w_full{r}") for r in range(RING)]
        w_used = sem("w_used")
        x_in = sem("x_in")
        main_in = sem("main_in")
        even_in = sem("even_in")
        stack_in = sem("stack_in")
        rows_in = sem("rows_in")
        lora_in = sem("lora_in")
        out_done = sem("out_done")
        dve_step = sem("dve_step")
        act_step = sem("act_step")
        stack_zero = sem("stack_zero")
        squared = sem("squared")
        rms_root = sem("rms_root")
        normed = sem("normed")
        scaled = sem("scaled")

        def bank(key):
            return ps[:, PLAN.at[key][0], :]

        def free(eng, *key):
            b, turn = PLAN.at[key]
            if turn:
                eng.wait_ge(bank_free[b], turn)
            return ps[:, b, :]

        def full(eng, *key):
            b, turn = PLAN.at[key]
            eng.wait_ge(bank_full[b], turn + 1)
            return ps[:, b, :]

        def drained(eng, *key):
            b, turn = PLAN.at[key]
            eng.wait_ge(bank_free[b], turn + 1)

        def full_sem(*key):
            return bank_full[PLAN.at[key][0]]

        def free_sem(*key):
            return bank_free[PLAN.at[key][0]]

        EIN = 0
        base = {}
        n_slots = 0
        for layer in range(2):
            base["in", layer] = n_slots
            n_slots += len(EVEN_SLOTS) if layer == 0 else len(ODD_SLOTS)
            base["out", layer] = n_slots
            n_slots += 4
            base["up", layer] = n_slots
            n_slots += 16
            base["down", layer] = n_slots
            n_slots += 16

        w_in = [dram["e_w_in"][0], dram["o_w_in"][0]]
        w_out = [dram["e_w_out"][0], dram["o_w_out"][0]]

        pos = [0]

        def take(*shape):
            at = pos[0]
            pos[0] += int(np.prod(shape))
            assert pos[0] <= STAGE_AT, pos[0]
            return cut(arena, at, *shape)

        even_t = take(EVEN_W)

        def even_const(name):
            at, w = EVEN_AT[name]
            return even_t[:, at:at + w]

        x_tok_in = rwkv_raw[:, 0:NT * D].rearrange("p (n d) -> p n d", n=NT)
        qk_raw = rwkv_raw[:, 4096:4096 + 5 * T].rearrange("p (a t) -> p a t", a=5)
        q_rot = take(4, T)
        k_rot = take(T)
        k_dup = take(2, P + T)
        v_dup = take(NT + 1, 2, P)
        conv_in = take(4, T + 3)
        conv_out = take(4, T)
        v_ml = take(NT, 4, 129)
        o_gate = take(NT, 512)
        att_p = take(2, 4, 256)
        att_pt = take(2, 2, 512)
        k_w = take(NT, 256)
        k_keep = cut(rwkv_raw, 0, 2, 512)
        w_ml = cut(arena, EVEN_W, 4, 4, P)
        dg = cut(rwkv_raw, 1024, 2, 4 * P)
        mtmp = cut(rwkv_raw, 2048, 2, 4 * P)
        qkw = cut(rwkv_raw, 3072, 2, 4 * P)
        n_sb = cut(rwkv_raw, 4096, 2, 2, 129 * 2)
        c_state = cut(rwkv_raw, 4096 + 1032, NT, 2, 129)
        c_tmp = cut(rwkv_raw, 4096 + 1032 + 1032, 2, 129)
        sm_at = [0]

        def tiny(*shape):
            at = sm_at[0]
            sm_at[0] += int(np.prod(shape))
            assert sm_at[0] <= 640
            return cut(small, at, *shape)

        a_mx, a_nm, a_se, a_rs, a_es, a_l = (tiny(2, 4) for _ in range(6))
        gt = tiny(NT, 8)
        fg, af, lf, li, gg, gmax, cmx, mx, marr, mm, dfa, dfb, wi_arg, em_arg = (tiny(NT, 4) for _ in range(14))
        cumb = tiny(2, 16)
        wgt_arg = tiny(NT, 4)
        dn = tiny(2, 4)
        st6 = tiny(6)
        mv = tiny(16, 2)

        hid = cut(arena, 0, FT, T)

        raw = cut(rwkv_raw, 0, 14, T + 1)
        pos[0] = 0
        z_tok = take(NT, 512)
        xbc_in = take(8, T + 3)
        xbc = take(8, T)
        xs_tok = take(2, 512)
        xdt = take(2, 512)
        xds = take(2, 512)
        b_tok = take(2, 256)
        s_dg = take(2, 512)
        s_w = take(2, 512)
        s_m = take(2, 8 * P)
        s_state = take(2, 512)
        s_y = hn_t[:, 4 * T:].rearrange("p (n c) -> p n c", n=NT)
        s_t = take(2, 512)
        pos[0] = 0
        kk_s = take(4, T)
        b_s = take(4, T)
        t1, t8 = take(T), take(T)
        inv_at = pos[0]
        inv_d = take(8, P)
        inv_t = take(8, P)
        inv_p = take(8, P)
        t2, t3, t4, t5, t6, t7 = (cut(arena, inv_at + j * T, T) for j in range(6))
        v_tok = take(NT, 512)
        g_tok = s_y
        y_rw = take(NT, 512)
        k_tok = take(2, 512)
        bb_tok = take(2, 512)
        mats_at = pos[0]
        mats = take(8, 4, P)
        mats_rk = cut(arena, mats_at, 4, T)
        s_sum = take(512)
        rhs_sb = take(512)
        neg_u = take(512)
        s_rw = take(2, 512)
        wa2 = lora[:, 0:512]
        g2 = lora[:, 512:1024]
        sm_at[0] = 0
        dtr, dta, dte, dtt, dA = (tiny(NT, 8) for _ in range(5))
        acum = tiny(2, 32)
        nacum, dsx, ea, ds_, dec = (tiny(32) for _ in range(5))
        expa = tiny(8)
        gss = tiny(8)
        bon = tiny(NT, 8)
        e_s = tiny(4, NT)
        e_a = tiny(4, NT)
        omka = tiny(4)
        lnm = tiny(NT, 8)
        lnv = tiny(NT, 8)

        names = ("att_max att_exp att_probs halo rope_done kd_v v_ones conv_ready silu_done soft_e soft_l lf_ready "
                 "g_diag g_ready m_diag m_ready wl_ready mexp k_scaled qkw_ready c_ready n_keep hm_done ln_var ln_root "
                 "o_sig y_ml_ready ssm_conv ssm_silu s_soft_e s_soft_l da_ready acum_args acum_exps s_diag s_masked "
                 "s_decay s_m_ready xdt_ready s_new xs_kept s_yprod z_silu s_sq s_root y_ssm_ready mixed tanh_done "
                 "gd_sig sgm a_sig cum_args cum_exps kk_sq kk_root rk_ready scales_arg scales tilde mats_ready "
                 "inv_step urhs_ready s_rw_ready ln2_sq ln2_var ln2_root y_rw_ready x_out slot_read kkraw").split()
        S = {n: sem(n) for n in names}

        block = ctx.enter_context(nc.Block())

        @block.sync
        def _(sp):
            sp.dma_start(x_tok_in, dram["x"][0].rearrange("(n p) d -> p n d", p=P)).then_inc(x_in, 16)

            def slot(n, src, width):
                if n >= RING:
                    sp.wait_ge(w_used, n - RING + 1)
                sp.dma_start(ring[:, n % RING, :, 0:width], src).then_inc(w_full[n % RING], 16)

            for layer in range(2):
                for j, (c0, width, _) in enumerate(EVEN_SLOTS if layer == 0 else ODD_SLOTS):
                    slot(base["in", layer] + j,
                         w_in[layer][:, c0:c0 + width].rearrange("(k p) c -> p k c", p=P), width)
                for j in range(4):
                    slot(base["out", layer] + j,
                         w_out[layer][:, j * SW:(j + 1) * SW].rearrange("(k p) c -> p k c", p=P), SW)
                up = dram["w_up"][layer].rearrange("(k p) c -> p k c", p=P)
                b0 = base["up", layer]
                with sp.Fori(0, 4) as i:
                    for j in range(4):
                        sp.wait_ge(w_used, i * 4 + (b0 + j - RING + 1))
                        sp.dma_start(ring[:, (b0 + j) % RING], up[:, :, bass.ds(i * (4 * SW) + j * SW, SW)]
                                     ).then_inc(w_full[(b0 + j) % RING], 16)
                down = dram["w_down"][layer].rearrange("(g k p) c -> p g k c", p=P, k=KT)
                b0 = base["down", layer]
                with sp.Fori(0, 4) as i:
                    for j in range(4):
                        sp.wait_ge(w_used, i * 4 + (b0 + j - RING + 1))
                        sp.dma_start(ring[:, (b0 + j) % RING], down[:, j, :, bass.ds(i * SW, SW)]
                                     ).then_inc(w_full[(b0 + j) % RING], 16)
            for t in range(NT):
                sp.wait_ge(S["x_out"], 2 * (t + 1))
                sp.dma_start(out[0, t * P:(t + 1) * P, :], arena[:, t * D:(t + 1) * D]).then_inc(out_done, 16)
            sp.wait_ge(out_done, 16 * NT)

        @block.gpsimd
        def _(pool):
            pool.dma_start(main_t[:, :], dram["main_const"]).then_inc(main_in, 16)
            n_stack = 0
            nc.gpsimd.memset(arena[:, STAGE_AT:STAGE_AT + 2 * P], 0.0).then_inc(stack_zero, 1)
            pool.wait_ge(stack_zero, 1)
            stage = {"a": (arena[:, STAGE_AT:STAGE_AT + P], STACK_A, A_AT), "b": (arena[:, STAGE_AT + P:STAGE_AT + 2 * P], STACK_B, B_AT)}
            for key in "ab":
                tile, spec, at = stage[key]
                for name, n in spec:
                    a = dram[name]
                    flat = a.rearrange(" ".join("abcd"[:len(a.shape)]) + " -> (" + " ".join("abcd"[:len(a.shape)]) + ")") \
                        if len(a.shape) > 1 else a
                    pool.dma_start(tile[at[name]:at[name] + n, :], flat.rearrange("(n p) -> n p", p=P)
                                   ).then_inc(stack_in, 16)
                    n_stack += 1
            pool.dma_start(even_t, dram["even_const"]).then_inc(even_in, 16)
            for name, n in ROWS:
                pool.dma_start(row(name, n), dram[name][0:1, :].to_broadcast([P, n])).then_inc(rows_in, 16)
            pool.dma_start(wa2[0:64, :], dram["rw_w2"][0]).then_inc(lora_in, 16)
            pool.dma_start(wa2[64:128, :], dram["rw_a2"][0]).then_inc(lora_in, 16)
            pool.dma_start(g2, dram["rw_g2"][0]).then_inc(lora_in, 16)

        N_STACK = len(STACK_A) + len(STACK_B)
        stage_a, stage_b = arena[:, STAGE_AT:STAGE_AT + P], arena[:, STAGE_AT + P:STAGE_AT + 2 * P]

        @block.tensor
        def _(pe):
            mm = nc.tensor.matmul

            def close(ins, *key):
                ins.then_inc(full_sem(*key), 1)

            def turn(key, parts):
                o = free(pe, *key)
                for j, src in enumerate(parts):
                    ins = nc.tensor.transpose(o[:, j * P:(j + 1) * P], src, ident)
                close(ins, *key)

            def norm(i):
                o = free(pe, "norm", i)
                for k in range(KT):
                    pe.wait_ge(squared, KT * i + k + 1)
                    ins = mm(o, ones, hn[:, k, :], start=(k == 0), stop=(k == KT - 1))
                close(ins, "norm", i)

            def slot_ready(n):
                pe.wait_ge(w_full[n % RING], 16 * (n // RING + 1))
                return ring[:, n % RING]

            def feature_tile(o, w, c, ready=0):
                for k in range(KT):
                    if ready:
                        pe.wait_ge(normed, ready + k + 1)
                    ins = mm(o, w[:, k, c:c + P], hn[:, k, :], start=(k == 0), stop=(k == KT - 1))
                return ins

            def token_tile(o, w, c, width, t):
                for k in range(KT):
                    ins = mm(o, hn[:, k, t * P:(t + 1) * P], w[:, k, c:c + width], start=(k == 0), stop=(k == KT - 1))
                return ins

            def project_in(layer):
                slots = EVEN_SLOTS if layer == 0 else ODD_SLOTS
                pe.wait_ge(normed, KT * (2 * layer + 1))
                count = {}
                for j, (c0, width, kind) in enumerate(slots):
                    w = slot_ready(base["in", layer] + j)
                    i = count.get(kind, 0)
                    count[kind] = i + 1
                    if kind in ("gates", "dt"):
                        o = free(pe, kind)
                        for t in range(NT):
                            ins = token_tile(o[:, t * 8:t * 8 + 8], w, 0, 8, t)
                        ins = close(ins, kind)
                    elif kind in ("q", "qk", "xbc", "rw"):
                        for c in range(2):
                            ins = feature_tile(free(pe, kind, 2 * i + c), w, c * P)
                            close(ins, kind, 2 * i + c)
                    elif kind == "kv":
                        close(feature_tile(free(pe, "k"), w, 0), "k")
                        o = free(pe, "v_att")
                        for t in range(NT):
                            ins = token_tile(o[:, t * P:(t + 1) * P], w, P, P, t)
                        close(ins, "v_att")
                    else:
                        for pair in range(2):
                            o = free(pe, kind, i, pair)
                            for t in range(2):
                                ins = token_tile(o[:, t * SW:(t + 1) * SW], w, 0, SW, 2 * pair + t)
                            close(ins, kind, i, pair)
                    pe.wait_ge(full_sem(*last_key[layer, j]), PLAN.at[last_key[layer, j]][1] + 1)
                    pe.sem_inc(w_used, 1)

            last_key = {}
            for layer, slots in ((0, EVEN_SLOTS), (1, ODD_SLOTS)):
                count = {}
                for j, (_, _, kind) in enumerate(slots):
                    i = count.get(kind, 0)
                    count[kind] = i + 1
                    last_key[layer, j] = {"gates": ("gates",), "dt": ("dt",), "kv": ("v_att",)}.get(
                        kind, (kind, 2 * i + 1) if kind in ("q", "qk", "xbc", "rw") else (kind, i, 1))

            def weights_loop(b0, j, i):
                pe.wait_ge(w_full[(b0 + j) % RING], i * 16 + 16 * ((b0 + j) // RING + 1))
                return ring[:, (b0 + j) % RING]

            def project_out(layer):
                b0 = base["out", layer]
                for i in range(2):
                    for s in range(2):
                        w = slot_ready(b0 + 2 * i + s)
                        for c in range(2):
                            b, turn0 = PLAN.at["out", layer, 2 * s + c]
                            pe.wait_ge(bank_free[b], turn0 + i)
                            for k in range(KT):
                                ins = mm(ps[:, b, :], w[:, k, c * P:(c + 1) * P], y_mix[:, k, :],
                                         start=(k == 0), stop=(k == KT - 1))
                            ins.then_inc(bank_full[b], 1)
                        pe.wait_ge(bank_full[b], turn0 + i + 1)
                        pe.sem_inc(w_used, 1)

            def mlp(layer):
                pe.wait_ge(normed, KT * (2 * layer + 2))
                b0 = base["up", layer]
                with pe.Fori(0, 4) as i:
                    for j in range(4):
                        w = weights_loop(b0, j, i)
                        for c in range(2):
                            b, turn0 = PLAN.at["up", layer, 2 * j + c]
                            pe.wait_ge(bank_free[b], i + turn0)
                            for k in range(KT):
                                ins = mm(ps[:, b, :], w[:, k, c * P:(c + 1) * P], hn[:, k, :],
                                         start=(k == 0), stop=(k == KT - 1))
                            ins.then_inc(bank_full[b], 1)
                        pe.wait_ge(bank_full[b], i + (turn0 + 1))
                        pe.sem_inc(w_used, 1)
                for j in range(8):
                    b, turn0 = PLAN.at["up", layer, j]
                    pe.wait_ge(bank_free[b], turn0 + 4)
                b0 = base["down", layer]
                with pe.Fori(0, 4) as i:
                    for c in range(2):
                        b, turn0 = PLAN.at["down", layer, c]
                        pe.wait_ge(bank_free[b], i + turn0)
                    for j in range(4):
                        w = weights_loop(b0, j, i)
                        for c in range(2):
                            b, turn0 = PLAN.at["down", layer, c]
                            for k in range(KT):
                                ins = mm(ps[:, b, :], w[:, k, c * P:(c + 1) * P], hid[:, j * KT + k, :],
                                         start=(j == 0 and k == 0), stop=(j == 3 and k == KT - 1))
                            if j == 3 and c == 0:
                                ins.then_inc(bank_full[b], 1)
                        ins.then_inc(bank_full[b] if j == 3 else S["slot_read"], 1)
                        if j == 3:
                            pe.wait_ge(bank_full[b], i + (turn0 + 1))
                        else:
                            pe.wait_ge(S["slot_read"], i * 3 + (12 * layer + j + 1))
                        pe.sem_inc(w_used, 1)

            def even():
                for i in range(5):
                    drained(pe, *(("q", i) if i < 4 else ("k",)))
                    pe.wait_ge(even_in, 16)
                    close(mm(free(pe, "rope", i), even_const("rot"), qk_raw[:, i, :], start=True, stop=True), "rope", i)
                pe.wait_ge(S["rope_done"], 5)
                dup = even_const("dup").rearrange("p (g m) -> p g m", g=2)
                for g in range(2):
                    close(mm(free(pe, "dup", g), dup[:, g, :], k_rot, start=True, stop=True), "dup", g)
                drained(pe, "dup", 1)
                drained(pe, "dup", 0)
                pe.wait_ge(S["halo"], 3)
                drained(pe, "v_att")
                for u in range(8 + 2):
                    if u < 8:
                        n, g = u // 2, u % 2
                        for par in range(2):
                            o = free(pe, "score", u, par)
                            r = slice(64 * par, 64 * par + 64)
                            for a in range(2):
                                ins = mm(o[:, a * 256:(a + 1) * 256], q_rot[r, 2 * g + a, n * P:(n + 1) * P],
                                         k_dup[r, g, n * P:n * P + 256], start=True, stop=True)
                            close(ins, "score", u, par)
                    if 1 <= u < 9:
                        v = u - 1
                        pe.wait_ge(S["att_probs"], v + 1)
                        for blk in range(2):
                            turn(("turn", v, blk), [att_p[:, v % 2, j, blk * P:(blk + 1) * P] for j in range(4)])
                    if u >= 2:
                        v = u - 2
                        n, g = v // 2, v % 2
                        o = free(pe, "att", v)
                        for blk in range(2):
                            drained(pe, "turn", v, blk)
                            ins = mm(o, v_dup[:, n + blk, g, :], att_pt[:, v % 2, blk, :], start=(blk == 0), stop=(blk == 1))
                        close(ins, "att", v)
                pe.wait_ge(S["lf_ready"], 1)
                o = free(pe, "cum")
                lf_ = lf.rearrange("p a b -> p (a b)")
                mm(o[:, 0:16], upper, lf_, start=True, stop=True)
                close(mm(o[:, 16:32], ones, lf_, start=True, stop=True), "cum")
                for n in range(NT):
                    pe.wait_ge(S["g_diag"], n + 1)
                    close(mm(free(pe, "g_row", n), ones, dg[:, n % 2, :], start=True, stop=True), "g_row", n)
                pe.wait_ge(S["silu_done"], 4)
                for a in range(2):
                    turn(("k_tok", a), [conv_out[:, 2 + a, n * P:(n + 1) * P] for n in range(NT)])
                for n in range(NT):
                    pe.wait_ge(S["m_diag"], n + 1)
                    close(mm(free(pe, "m_row", n), ones, dg[:, n % 2, :], start=True, stop=True), "m_row", n)
                drained_v = [("v", a, b) for a in range(2) for b in range(2)]
                for key in drained_v:
                    drained(pe, *key)
                pe.wait_ge(S["v_ones"], 1)
                for n in range(NT):
                    tok = slice(n * P, (n + 1) * P)
                    for par in range(2):
                        o = free(pe, "qk_st", n, par)
                        r = slice(64 * par, 64 * par + 64)
                        for a in range(2):
                            ins = mm(o[:, a * P:(a + 1) * P], conv_out[r, 2 + a, tok], conv_out[r, a, tok],
                                     start=True, stop=True)
                        close(ins, "qk_st", n, par)
                    if n < NT - 1:
                        pe.wait_ge(S["k_scaled"], n + 1)
                        for a in range(2):
                            o = free(pe, "c_loc", n, a)
                            for par in range(2):
                                ins = mm(o[:, par * 129:(par + 1) * 129], k_w[:, n, a * P:(a + 1) * P],
                                         v_ml[:, n, 2 * a + par, :], start=True, stop=True)
                            close(ins, "c_loc", n, a)
                    pe.wait_ge(S["qkw_ready"], n + 1)
                    for a in range(2):
                        o = free(pe, "num", n, a)
                        for par in range(2):
                            hh = 2 * a + par
                            ins = mm(o[:, par * 129:(par + 1) * 129], qkw[:, n % 2, hh * P:(hh + 1) * P],
                                     v_ml[:, n, hh, :], start=True, stop=True)
                        close(ins, "num", n, a)
                    if n:
                        pe.wait_ge(S["c_ready"], n)
                        for par in range(2):
                            o = free(pe, "inter", n, par)
                            r = slice(64 * par, 64 * par + 64)
                            for a in range(2):
                                ins = mm(o[:, a * 129:(a + 1) * 129], conv_out[r, a, tok], c_state[r, n, a, :],
                                         start=True, stop=True)
                            close(ins, "inter", n, par)
                pe.wait_ge(S["y_ml_ready"], 1)
                for f in range(4):
                    turn(("y_ml", f), [o_gate[:, n, f * P:(f + 1) * P] for n in range(NT)])
                for f in range(4):
                    drained(pe, "y_ml", f)
                for u in range(8):
                    drained(pe, "att", u)

            def odd():
                pe.wait_ge(S["da_ready"], 1)
                o = free(pe, "a_cum")
                da_ = dA.rearrange("p a b -> p (a b)")
                mm(o[:, 0:32], upper, da_, start=True, stop=True)
                close(mm(o[:, 32:64], ones, da_, start=True, stop=True), "a_cum")
                pe.wait_ge(S["ssm_silu"], 8)
                for n in range(NT):
                    tok = slice(n * P, (n + 1) * P)
                    turn(("x_tok", n), [xbc[:, i, tok] for i in range(4)])
                    turn(("b_tok", n), [xbc[:, 4 + g, tok] for g in range(2)])
                    for half in range(2):
                        pe.wait_ge(S["s_diag"], 2 * n + half + 1)
                        close(mm(free(pe, "a_row", n, half), ones, s_dg[:, half, :], start=True, stop=True),
                              "a_row", n, half)
                    o = free(pe, "cb", n)
                    for g in range(2):
                        ins = mm(o[:, g * P:(g + 1) * P], xbc[:, 4 + g, tok], xbc[:, 6 + g, tok], start=True, stop=True)
                    close(ins, "cb", n)
                    pe.wait_ge(S["s_m_ready"], n + 1)
                    pe.wait_ge(S["xdt_ready"], n + 1)
                    o = free(pe, "y_diag", n)
                    for hh in range(8):
                        c = slice(hh * 64, hh * 64 + 64)
                        ins = mm(o[:, c], s_m[:, n % 2, hh * P:(hh + 1) * P], xdt[:, n % 2, c], start=True, stop=True)
                    close(ins, "y_diag", n)
                    if n:
                        pe.wait_ge(S["s_new"], n)
                        o = free(pe, "y_off", n)
                        for g in range(2):
                            c = slice(g * 256, g * 256 + 256)
                            ins = mm(o[:, c], xbc[:, 6 + g, tok], s_state[:, n % 2, c], start=True, stop=True)
                        close(ins, "y_off", n)
                    if n < NT - 1:
                        drained(pe, "b_tok", n)
                        o = free(pe, "s_loc", n)
                        for g in range(2):
                            c = slice(g * 256, g * 256 + 256)
                            ins = mm(o[:, c], b_tok[:, n % 2, g * P:(g + 1) * P], xds[:, n % 2, c], start=True, stop=True)
                        close(ins, "s_loc", n)
                pe.wait_ge(S["y_ssm_ready"], 1)
                for f in range(4):
                    turn(("y_ssm", f), [s_y[:, n, f * P:(f + 1) * P] for n in range(NT)])
                pe.wait_ge(S["tanh_done"], 1)
                pe.wait_ge(lora_in, 48)
                for f in range(4):
                    close(mm(free(pe, "decay", f), wa2[0:64, f * P:(f + 1) * P], raw[0:64, 12, 1:], start=True, stop=True),
                          "decay", f)
                    close(mm(free(pe, "a", f), wa2[64:128, f * P:(f + 1) * P], raw[64:128, 12, 1:], start=True, stop=True),
                          "a", f)
                    pe.wait_ge(S["kk_sq"], f + 1)
                    close(mm(free(pe, "kk_sum", f), blocks, t8, start=True, stop=True), "kk_sum", f)
                pe.wait_ge(S["gd_sig"], 1)
                for n in range(NT):
                    close(mm(free(pe, "g_tok", n), raw[:, 13, 1 + n * P:1 + (n + 1) * P], g2, start=True, stop=True),
                          "g_tok", n)
                for n in range(NT):
                    turn(("rv_tok", n), [raw[:, 8 + f, 1 + n * P:1 + (n + 1) * P] for f in range(4)])
                pe.wait_ge(S["rk_ready"], 4)
                o = free(pe, "bonus")
                heads = const("heads")
                for n in range(NT):
                    for f in range(4):
                        ins = mm(o[:, n * 8 + 2 * f:n * 8 + 2 * f + 2], mats_rk[:, f, n * P:(n + 1) * P], heads,
                                 start=True, stop=True)
                close(ins, "bonus")
                pe.wait_ge(S["tilde"], 4)
                for n in range(NT):
                    tok = slice(n * P, (n + 1) * P)
                    rtok = slice(1 + n * P, 1 + (n + 1) * P)
                    turn(("rk_tok", n), [raw[:, 4 + f, rtok] for f in range(4)])
                    turn(("rb_tok", n), [b_s[:, f, tok] for f in range(4)])
                    for f in range(4):
                        for par in range(2):
                            r = slice(64 * par, 64 * par + 64)
                            o = free(pe, "mats", n, f, par)
                            mm(o[:, 0:P], kk_s[r, f, tok], b_s[r, f, tok], start=True, stop=True)
                            mm(o[:, P:2 * P], raw[r, 4 + f, rtok], kk_s[r, f, tok], start=True, stop=True)
                            mm(o[:, 2 * P:3 * P], raw[r, 4 + f, rtok], raw[r, f, rtok], start=True, stop=True)
                            close(mm(o[:, 3 * P:4 * P], b_s[r, f, tok], raw[r, f, rtok], start=True, stop=True),
                                  "mats", n, f, par)
                    for f in range(4):
                        for par in range(2):
                            drained(pe, "mats", n, f, par)
                    for level in range(LEVELS):
                        last = level == LEVELS - 1
                        for half in range(2):
                            if level:
                                drained(pe, "dt_", n, level - 1, half)
                            o = free(pe, "pt", n, level, half)
                            for j in range(4):
                                hh = 4 * half + j
                                ins = mm(o[:, j * P:(j + 1) * P], mats[:, hh, 0, :], inv_t[:, hh, :] if level else ident,
                                         start=True, stop=True)
                            close(ins, "pt", n, level, half)
                        for half in range(2):
                            drained(pe, "pt", n, level, half)
                            if not last:
                                o = free(pe, "d", n, level, half)
                                for j in range(4):
                                    hh = 4 * half + j
                                    ins = mm(o[:, j * P:(j + 1) * P], inv_p[:, hh, :],
                                             inv_d[:, hh, :] if level else ident, start=True, stop=True)
                                close(ins, "d", n, level, half)
                            o = free(pe, "dt_", n, level, half)
                            for j in range(4):
                                hh = 4 * half + j
                                ins = mm(o[:, j * P:(j + 1) * P], inv_d[:, hh, :] if level else ident,
                                         inv_p[:, hh, :], start=True, stop=True)
                            close(ins, "dt_", n, level, half)
                    for half in range(2):
                        drained(pe, "dt_", n, LEVELS - 1, half)
                    drained(pe, "rv_tok", n)
                    if n:
                        pe.wait_ge(S["s_rw_ready"], n)
                    o = free(pe, "rhs", n)
                    for f in range(4):
                        c = slice(f * P, (f + 1) * P)
                        if n:
                            mm(o[:, c], kk_s[:, f, tok], s_rw[:, n % 2, c], start=True, stop=True,
                               skip_group_check=True)
                        for par in range(2):
                            hh = 2 * f + par
                            c = slice(hh * 64, hh * 64 + 64)
                            ins = mm(o[:, c], mats[:, hh, 1, :], v_tok[:, n, c], start=(n == 0), stop=True,
                                     skip_group_check=True)
                    close(ins, "rhs", n)
                    drained(pe, "rhs", n)
                    o = free(pe, "u", n)
                    for hh in range(8):
                        c = slice(hh * 64, hh * 64 + 64)
                        ins = mm(o[:, c], inv_t[:, hh, :], rhs_sb[:, c], start=True, stop=True)
                    close(ins, "u", n)
                    drained(pe, "u", n)
                    o = free(pe, "y", n)
                    for f in range(4):
                        c = slice(f * P, (f + 1) * P)
                        if n:
                            mm(o[:, c], raw[:, f, rtok], s_rw[:, n % 2, c], start=True, stop=True,
                               skip_group_check=True)
                        for par in range(2):
                            hh = 2 * f + par
                            c = slice(hh * 64, hh * 64 + 64)
                            mm(o[:, c], mats[:, hh, 2, :], v_tok[:, n, c], start=(n == 0), stop=True,
                               skip_group_check=True)
                            ins = mm(o[:, c], mats[:, hh, 3, :], neg_u[:, c], start=False, stop=True,
                                     skip_group_check=True)
                    close(ins, "y", n)
                    if n < NT - 1:
                        drained(pe, "rk_tok", n)
                        drained(pe, "rb_tok", n)
                        o = free(pe, "s_rw", n)
                        for f in range(4):
                            c = slice(f * P, (f + 1) * P)
                            mm(o[:, c], k_tok[:, n % 2, c], v_tok[:, n, c], start=True, stop=False)
                            ins = mm(o[:, c], bb_tok[:, n % 2, c], neg_u[:, c], start=False, stop=True)
                        close(ins, "s_rw", n)
                pe.wait_ge(S["y_rw_ready"], NT)
                for f in range(4):
                    turn(("y_rw", f), [y_rw[:, n, f * P:(f + 1) * P] for n in range(NT)])
                for f in range(4):
                    drained(pe, "y_ssm", f)
                    drained(pe, "y_rw", f)

            pe.wait_ge(main_in, 16)
            pe.wait_ge(stack_in, 16 * N_STACK)
            for key, tile in (("stack_a", stage_a), ("stack_b", stage_b)):
                close(nc.tensor.transpose(free(pe, key)[:, 0:P], tile, ident), key)
            pe.wait_ge(x_in, 16)
            for k in range(KT):
                turn(("x", k), [x_tok_in[:, n, k * P:(k + 1) * P] for n in range(NT)])
            for layer in range(2):
                norm(2 * layer)
                project_in(layer)
                (even if layer == 0 else odd)()
                project_out(layer)
                norm(2 * layer + 1)
                mlp(layer)
            norm(4)
            pe.wait_ge(normed, KT * 5)
            for t in range(NT):
                for half in range(2):
                    turn(("result", t, half), [hn[:, 4 * half + j, t * P:(t + 1) * P] for j in range(4)])

        @block.scalar
        def _(act):
            steps = [0]
            A = nc.scalar.activation

            def link(ins):
                steps[0] += 1
                ins.then_inc(act_step, 1)
                act.wait_ge(act_step, steps[0])

            def drain(dst, *key, src=None, scale=1.0):
                o = full(act, *key)
                A(dst, o if src is None else src, ACT.Copy, scale=scale).then_inc(free_sem(*key), 1)

            def norm(i, ready):
                for k in range(KT):
                    ready(act, k)
                    A(hn[:, k, :], h[:, k, :], ACT.Square).then_inc(squared, 1)
                o = full(act, "norm", i)
                if i:
                    act.wait_ge(normed, KT * i)
                A(rms_t, o, ACT.Sqrt, scale=1.0 / D, bias=eps[:, 0:1]).then_inc(free_sem("norm", i), 1)

            act.wait_ge(main_in, 16)
            for key, at, n in (("stack_a", 0, A_N), ("stack_b", A_N, B_N)):
                o = full(act, key)
                A(cols_t[:, at:at + n], o[:, 0:n], ACT.Copy).then_inc(free_sem(key), 1)
            for k in range(KT):
                drain(h[:, k, :], "x", k)

            def x_ready(eng, k):
                drained(eng, "x", k)

            norm(0, x_ready)

            def pair_view(tile, half, pair):
                return tile[:, 2 * pair:2 * pair + 2, half * SW:(half + 1) * SW]

            for i in range(4):
                drain(qk_raw[:, i, :], "q", i)
            drain(qk_raw[:, 4, :], "k")
            o = full(act, "v_att").rearrange("p (n g d) -> p n g d", n=NT, g=2)
            for j in range(2):
                for g in range(2):
                    ins = A(v_dup[:, 1:NT + 1, g, 64 * j:64 * j + 64], o[:, :, g, :], ACT.Copy)
                    if j and g:
                        ins.then_inc(free_sem("v_att"), 1)
            for i in range(4):
                drain(conv_in[:, i, 3:], "qk", i)
            for half in range(2):
                for pair in range(2):
                    o = full(act, "v", half, pair).rearrange("p (n a d) -> p n a d", n=2, a=2)
                    for t in range(2):
                        ins = A(v_ml[:, 2 * pair + t, 2 * half:2 * half + 2, 0:P], o[:, t], ACT.Copy)
                    ins.then_inc(free_sem("v", half, pair), 1)
            for half in range(2):
                for pair in range(2):
                    o = full(act, "o", half, pair)
                    A(pair_view(o_gate, half, pair), o.rearrange("p (n c) -> p n c", n=2), ACT.Sigmoid
                      ).then_inc(free_sem("o", half, pair), 1)
            for i in range(4):
                act.wait_ge(S["conv_ready"], i + 1)
                A(conv_out[:, i, :], conv_out[:, i, :], ACT.Silu).then_inc(S["silu_done"], 1)
            act.wait_ge(S["halo"], 3)
            for g in range(2):
                drain(k_dup[:, g, P:], "dup", g)
            for u in range(8 + 2):
                if u < 8:
                    b = u % 2
                    act.wait_ge(S["att_max"], u + 1)
                    for j in range(4):
                        A(att_p[:, b, j, :], att_p[:, b, j, :], ACT.Exp, bias=a_nm[:, b, j:j + 1],
                          accum_out=a_rs[:, b, j:j + 1])
                    A(a_es[:, b, :], a_se[:, b, :], ACT.Exp).then_inc(S["att_exp"], 1)
                if 1 <= u < 9:
                    for blk in range(2):
                        drain(att_pt[:, (u - 1) % 2, blk, :], "turn", u - 1, blk)
                if u >= 2:
                    v = u - 2
                    n, g = v // 2, v % 2
                    o = full(act, "att", v)
                    for par in range(2):
                        r = slice(64 * par, 64 * par + 64)
                        ins = A(y_mix[r, 2 * g:2 * g + 2, n * P:(n + 1) * P],
                                o[r, par * 256:par * 256 + 256].rearrange("p (a t) -> p a t", a=2), ACT.Copy)
                    ins.then_inc(free_sem("att", v), 1)
            act.wait_ge(S["soft_e"], 1)
            link(A(af, af, ACT.Exp, scale=-1.0))
            A(af, af, ACT.Ln, bias=1.0).then_inc(S["soft_l"], 1)
            for a in range(2):
                drain(k_keep[:, a, :], "k_tok", a)
            act.wait_ge(S["m_ready"], 1)
            for ap in (dfa, dfb, wi_arg, em_arg, wgt_arg):
                ins = A(ap, ap, ACT.Exp)
            ins.then_inc(S["mexp"], 1)
            for n in range(NT):
                act.wait_ge(S["wl_ready"], n + 1)
                for j in range(4):
                    ins = A(w_ml[:, n, j, :], mtmp[:, n % 2, j * P:(j + 1) * P], ACT.Exp, bias=gg[:, n, j:j + 1])
                ins.then_inc(S["n_keep"], 1)
            for n in range(NT):
                for a in range(2):
                    if n >= 2:
                        act.wait_ge(S["hm_done"], n - 1)
                    drain(n_sb[:, n % 2, a, :], "num", n, a, src=bank(("num", n, a))[:, 0:258])
            act.wait_ge(S["ln_var"], 1)
            A(mv[:, :, 1], mv[:, :, 1], ACT.Sqrt, bias=eps[:, 1:2]).then_inc(S["ln_root"], 1)
            for f in range(4):
                drain(y_mix[:, 4 + f, :], "y_ml", f)

            def residual(i):
                def ready(eng, k):
                    if i % 2 == 1:
                        b, t0 = PLAN.at["out", i // 2, k % 4]
                        eng.wait_ge(bank_free[b], t0 + k // 4 + 1)
                    else:
                        b, t0 = PLAN.at["down", i // 2 - 1, k % 2]
                        eng.wait_ge(bank_free[b], t0 + k // 2 + 1)
                return ready

            def squares_free(i):
                key = ("out", i // 2, 3) if i % 2 == 1 else ("up", i // 2 - 1, 7)
                b, t0 = PLAN.at[key]
                act.wait_ge(bank_full[b], t0 + (2 if i % 2 == 1 else 4))

            squares_free(1)
            norm(1, residual(1))
            squares_free(2)
            norm(2, residual(2))

            for half in range(2):
                for pair in range(2):
                    o = full(act, "z", half, pair)
                    A(pair_view(z_tok, half, pair), o.rearrange("p (n c) -> p n c", n=2), ACT.Silu
                      ).then_inc(free_sem("z", half, pair), 1)
            for i in range(8):
                drain(xbc_in[:, i, 3:], "xbc", i)
            for i in range(14):
                drain(raw[:, i, 1:], "rw", i)
            for i in range(8):
                act.wait_ge(S["ssm_conv"], i + 1)
                A(xbc[:, i, :], xbc[:, i, :], ACT.Silu).then_inc(S["ssm_silu"], 1)
            act.wait_ge(rows_in, 16 * len(ROWS))
            A(expa, row("ssm_a_log", 8), ACT.Exp)
            act.wait_ge(S["s_soft_e"], 1)
            link(A(dta, dta, ACT.Exp, scale=-1.0))
            A(dta, dta, ACT.Ln, bias=1.0).then_inc(S["s_soft_l"], 1)
            act.wait_ge(S["acum_args"], 1)
            A(ea, acum[:, 0, :], ACT.Exp)
            A(dec, acum[:, 1, :], ACT.Exp)
            A(ds_, dsx, ACT.Exp).then_inc(S["acum_exps"], 1)
            for n in range(NT):
                if n >= 2:
                    act.wait_ge(S["s_yprod"], n - 1)
                    if n < NT:
                        pe_key = ("s_loc", n - 2)
                        full(act, *pe_key)
                drain(xs_tok[:, n % 2, :], "x_tok", n)
                drain(b_tok[:, n % 2, :], "b_tok", n, src=bank(("b_tok", n))[:, 0:256])
                for half in range(2):
                    act.wait_ge(S["s_masked"], 2 * n + half + 1)
                    for j in range(4):
                        c = 8 * n + 4 * half + j
                        ins = A(s_w[:, half, j * P:(j + 1) * P], s_t[:, half, j * P:(j + 1) * P], ACT.Exp,
                                bias=nacum[:, c:c + 1])
                    ins.then_inc(S["s_decay"], 1)
            for n in range(NT):
                act.wait_ge(S["z_silu"], n + 1)
                for g in range(2):
                    ins = A(xbc_in[:, 2 * n + g, 0:256], s_y[:, n, g * 256:(g + 1) * 256], ACT.Square,
                            accum_out=gss[:, 2 * n + g:2 * n + g + 1])
                    if n == NT - 1 and g == 1:
                        link(ins)
            A(gss, gss, ACT.Sqrt, scale=1.0 / 256, bias=eps[:, 0:1]).then_inc(S["s_root"], 1)
            for f in range(4):
                drain(y_mix[:, f, :], "y_ssm", f)
            act.wait_ge(S["mixed"], 1)
            A(raw[0:64, 12, 1:], raw[0:64, 12, 1:], ACT.Tanh).then_inc(S["tanh_done"], 1)
            A(raw[:, 13, 1:], raw[:, 13, 1:], ACT.Sigmoid).then_inc(S["gd_sig"], 1)
            for f in range(4):
                if f:
                    act.wait_ge(S["tilde"], f)
                o = full(act, "decay", f)
                A(t1, o, ACT.Sigmoid, bias=col_b("rw_w0", f)).then_inc(free_sem("decay", f), 1)
                o = full(act, "a", f)
                A(t2, o, ACT.Sigmoid, bias=col_b("rw_a0", f)).then_inc(free_sem("a", f), 1)
                act.wait_ge(S["kkraw"], f + 1)
                A(t8, t7, ACT.Square).then_inc(S["kk_sq"], 1)
                o = full(act, "kk_sum", f)
                A(t6, o, ACT.Sqrt).then_inc(free_sem("kk_sum", f), 1)
                act.wait_ge(S["cum_args"], f + 1)
                A(t5, t3, ACT.Exp, scale=-DECAY_K)
                A(t4, t4, ACT.Exp, scale=-DECAY_K)
                A(t3, t3, ACT.Exp, scale=DECAY_K).then_inc(S["cum_exps"], 1)
            A(e_s, e_a, ACT.Exp, scale=-DECAY_K).then_inc(S["scales"], 1)
            for n in range(NT):
                drain(g_tok[:, n, :], "g_tok", n)
            for n in range(NT):
                drain(v_tok[:, n, :], "rv_tok", n)
            for n in range(NT):
                if n >= 2:
                    full(act, "s_rw", n - 2)
                drain(k_tok[:, n % 2, :], "rk_tok", n)
                drain(bb_tok[:, n % 2, :], "rb_tok", n)
                drain(rhs_sb, "rhs", n)
                if n:
                    full(act, "s_rw", n - 1)
                drain(neg_u, "u", n, scale=-1.0)
                drain(y_rw[:, n, :], "y", n)
            act.wait_ge(S["ln2_var"], 1)
            A(lnv, lnv, ACT.Sqrt, scale=1.0 / 64, bias=eps[:, 2:3]).then_inc(S["ln2_root"], 1)
            for f in range(4):
                drain(y_mix[:, 4 + f, :], "y_rw", f)
            squares_free(3)
            norm(3, residual(3))
            squares_free(4)
            norm(4, residual(4))
            for t in range(NT):
                for half in range(2):
                    o = full(act, "result", t, half)
                    A(arena[:, t * D + half * 512:t * D + half * 512 + 512], o, ACT.Copy).then_inc(S["x_out"], 1)

        @block.vector
        def _(dve):
            steps = [0]
            V = nc.vector

            def link(ins):
                steps[0] += 1
                ins.then_inc(dve_step, 1)
                dve.wait_ge(dve_step, steps[0])

            def norm(i):
                gains = {0: ("mix_norm", 0), 1: ("mlp_norm", 0), 2: ("mix_norm", 8), 3: ("mlp_norm", 8),
                         4: ("final_norm", 0)}[i]
                drained(dve, "norm", i)
                link(V.reciprocal(rms_t, rms_t))
                for k in range(KT):
                    V.scalar_tensor_tensor(out=hn[:, k, :], in0=h[:, k, :], scalar=col_a(gains[0], gains[1] + k),
                                           in1=rms_t, op0=ALU.mult, op1=ALU.mult).then_inc(normed, 1)

            def project_out(layer):
                for i in range(2):
                    for j in range(4):
                        b, t0 = PLAN.at["out", layer, j]
                        dve.wait_ge(bank_full[b], t0 + i + 1)
                        m = 4 * i + j
                        V.tensor_tensor(h[:, m, :], h[:, m, :], ps[:, b, :], ALU.add).then_inc(bank_free[b], 1)

            def mlp(layer):
                with dve.Fori(0, 4) as i:
                    for j in range(8):
                        b, t0 = PLAN.at["up", layer, j]
                        dve.wait_ge(bank_full[b], i + (t0 + 1))
                        V.tensor_scalar(relu_t[:, j % 2, :], ps[:, b, :], 0.0, None, ALU.max).then_inc(scaled, 1)
                        dve.wait_ge(scaled, i * 8 + (32 * layer + j + 1))
                        V.tensor_tensor(arena[:, bass.ds(i * (8 * T) + j * T, T)],
                                        relu_t[:, j % 2, :], ps[:, b, :], ALU.mult).then_inc(bank_free[b], 1)
                with dve.Fori(0, 4) as i:
                    for j in range(2):
                        b, t0 = PLAN.at["down", layer, j]
                        dve.wait_ge(bank_full[b], i + (t0 + 1))
                        hd = h_t[:, bass.ds(i * (2 * T) + j * T, T)]
                        V.tensor_tensor(hd, hd, ps[:, b, :], ALU.add).then_inc(bank_free[b], 1)

            def conv(dst, src, w, b, i, tiles, signal):
                link(V.tensor_scalar(dst, src[:, 0:T], col_a(w, i), col_a(b, i), ALU.mult, ALU.add))
                for tap in range(1, 4):
                    ins = V.scalar_tensor_tensor(out=dst, in0=src[:, tap:tap + T], scalar=col_a(w, tap * tiles + i),
                                                 in1=dst, op0=ALU.mult, op1=ALU.add)
                    if tap < 3:
                        link(ins)
                    else:
                        ins.then_inc(signal, 1)

            drained(dve, "stack_a")
            drained(dve, "stack_b")
            drained(dve, "x", KT - 1)
            for k in range(KT):
                drained(dve, "x", k)
            norm(0)
            V.memset(k_dup[:, :, 0:P], 0.0).then_inc(S["halo"], 1)
            V.memset(v_dup[:, 0, :, :], 0.0).then_inc(S["halo"], 1)
            V.memset(conv_in[:, :, 0:3], 0.0).then_inc(S["halo"], 1)
            V.memset(v_ml[:, :, :, 128:129], 1.0).then_inc(S["v_ones"], 1)
            dve.wait_ge(rows_in, 16 * len(ROWS))
            g_ps = full(dve, "gates")[:, 0:32].rearrange("p (n c) -> p n c", n=NT)
            link(V.tensor_tensor(li, g_ps[:, :, 0:4], over(row("ml_i_bias", 4), 1, NT), ALU.add))
            V.tensor_tensor(fg, g_ps[:, :, 4:8], over(row("ml_f_bias", 4), 1, NT), ALU.add).then_inc(free_sem("gates"), 1)
            drained(dve, "gates")
            V.scalar_tensor_tensor(out=af, in0=fg, scalar=-1.0, in1=fg, op0=ALU.mult, op1=ALU.max
                                   ).then_inc(S["soft_e"], 1)
            dve.wait_ge(even_in, 16)
            cos, sin = even_const("cos"), even_const("sin")
            for i in range(5):
                dst = q_rot[:, i, :] if i < 4 else k_rot
                drained(dve, *(("q", i) if i < 4 else ("k",)))
                link(V.tensor_tensor(dst, qk_raw[:, i, :], cos, ALU.mult))
                o = full(dve, "rope", i)
                V.tensor_tensor(relu_t[:, i % 2, :], o, sin, ALU.mult).then_inc(free_sem("rope", i), 1)
                drained(dve, "rope", i)
                V.tensor_tensor(dst, dst, relu_t[:, i % 2, :], ALU.add).then_inc(S["rope_done"], 1)
            dve.wait_ge(S["halo"], 3)
            for i in range(4):
                drained(dve, "qk", i)
                conv(conv_out[:, i, :], conv_in[:, i, :], "ml_conv_w", "ml_conv_b", i, 4, S["conv_ready"])
            sinks = row("att_sinks", 8)
            band, first = even_const("band"), even_const("first")

            def att_scores(u):
                n, g = u // 2, u % 2
                b = u % 2
                if u >= 2:
                    full(dve, "turn", u - 2, 0)
                    full(dve, "turn", u - 2, 1)
                for par in range(2):
                    o = full(dve, "score", u, par).rearrange("p (a k) -> p a k", a=2)
                    V.scalar_tensor_tensor(out=att_p[:, b, 2 * par:2 * par + 2, :], in0=o, scalar=0.125,
                                           in1=over(band if n else first, 1, 2), op0=ALU.mult, op1=ALU.add
                                           ).then_inc(free_sem("score", u, par), 1)
                drained(dve, "score", u, 0)
                drained(dve, "score", u, 1)
                sk = sinks[:, 4 * g:4 * g + 4].rearrange("p (a par) -> p par a", par=2)
                v2 = lambda ap: ap.rearrange("p (par a) -> p par a", par=2)
                link(V.tensor_reduce(a_mx[:, b, :], att_p[:, b], AX.X, ALU.max))
                link(V.tensor_tensor(v2(a_mx[:, b, :]), v2(a_mx[:, b, :]), sk, ALU.max))
                link(V.tensor_scalar(a_nm[:, b, :], a_mx[:, b, :], -1.0, None, ALU.mult))
                V.tensor_tensor(v2(a_se[:, b, :]), v2(a_nm[:, b, :]), sk, ALU.add).then_inc(S["att_max"], 1)

            def att_norm(u):
                b = u % 2
                dve.wait_ge(S["att_exp"], u + 1)
                link(V.tensor_tensor(a_l[:, b, :], a_rs[:, b, :], a_es[:, b, :], ALU.add))
                link(V.reciprocal(a_l[:, b, :], a_l[:, b, :]))
                V.tensor_tensor(att_p[:, b], att_p[:, b], over(a_l[:, b, :], 2, 256), ALU.mult
                                ).then_inc(S["att_probs"], 1)

            for u in range(9):
                if u < 8:
                    att_scores(u)
                if u:
                    att_norm(u - 1)
            dve.wait_ge(S["soft_l"], 1)
            V.scalar_tensor_tensor(out=lf, in0=fg, scalar=0.0, in1=af, op0=ALU.min, op1=ALU.subtract
                                   ).then_inc(S["lf_ready"], 1)
            o = full(dve, "cum")
            V.tensor_copy(cumb, o[:, 0:32].rearrange("p (a b) -> p a b", a=2)).then_inc(free_sem("cum"), 1)
            drained(dve, "cum")
            b_ = cumb[:, 0, :].rearrange("p (n c) -> p n c", n=NT)
            bl = cumb[:, 1, :].rearrange("p (n c) -> p n c", n=NT)
            link(V.tensor_tensor(gg, li, b_, ALU.subtract))

            def diag(dst, col, signal):
                V.tensor_tensor(dst.rearrange("p (a t) -> p a t", a=4), over(ident, 1, 4), over(col, 2, P), ALU.mult
                                ).then_inc(signal, 1)

            full(dve, "att", 7)
            for n in range(2):
                diag(dg[:, n % 2, :], gg[:, n, :], S["g_diag"])
            for n in range(NT):
                o = full(dve, "g_row", n).rearrange("p (a t) -> p a t", a=4)
                link(V.tensor_reduce(gmax[:, n, :], o, AX.X, ALU.max))
                V.tensor_tensor(mtmp[:, n % 2, :].rearrange("p (a t) -> p a t", a=4), o, over(const("add_ts"), 1, 4),
                                ALU.add).then_inc(free_sem("g_row", n), 1)
                drained(dve, "g_row", n)
                link(V.tensor_reduce(cmx[:, n, :], mtmp[:, n % 2, :].rearrange("p (a t) -> p a t", a=4), AX.X, ALU.max))
                if n + 2 < NT:
                    diag(dg[:, n % 2, :], gg[:, n + 2, :], S["g_diag"])
            link(V.memset(marr[:, 0, :], 0.0))
            for n in range(NT):
                link(V.tensor_tensor(mx[:, n, :], marr[:, n, :], gmax[:, n, :], ALU.max))
                if n < NT - 1:
                    link(V.tensor_tensor(marr[:, n + 1, :], bl[:, n, :], mx[:, n, :], ALU.add))
            mm_ = mm
            link(V.tensor_tensor(mm_, marr, cmx, ALU.max))
            V.tensor_tensor(dfa, marr, mx, ALU.subtract)
            V.tensor_tensor(dfb, gmax, mx, ALU.subtract)
            V.tensor_tensor(wi_arg, marr, mm_, ALU.subtract)
            V.tensor_tensor(wgt_arg, gg, gmax, ALU.subtract)
            link(V.tensor_tensor(em_arg, b_, mm_, ALU.add))
            V.tensor_scalar(em_arg, em_arg, -1.0, None, ALU.mult).then_inc(S["m_ready"], 1)
            for n in range(2):
                diag(dg[:, n % 2, :], mm_[:, n, :], S["m_diag"])
            for n in range(NT):
                o = full(dve, "m_row", n).rearrange("p (a t) -> p a t", a=4)
                if n >= 2:
                    dve.wait_ge(S["n_keep"], n - 1)
                V.tensor_tensor(mtmp[:, n % 2, :].rearrange("p (a t) -> p a t", a=4), over(const("add_st"), 1, 4), o,
                                ALU.subtract).then_inc(free_sem("m_row", n), 1)
                drained(dve, "m_row", n)
                dve.sem_inc(S["wl_ready"], 1)
                if n + 2 < NT:
                    diag(dg[:, n % 2, :], mm_[:, n + 2, :], S["m_diag"])
            dve.wait_ge(S["mexp"], 1)
            for a in range(2):
                drained(dve, "k_tok", a)
            kk4 = k_keep.rearrange("p a (n f) -> p n a f", n=NT)
            for n in range(NT):
                for a in range(2):
                    ins = V.scalar_tensor_tensor(
                        out=k_w[:, n, a * P:(a + 1) * P].rearrange("p (b d) -> p b d", b=2),
                        in0=kk4[:, n, a, :].rearrange("p (b d) -> p b d", b=2), scalar=0.125,
                        in1=over(wgt_arg[:, n, 2 * a:2 * a + 2], 2, 64), op0=ALU.mult, op1=ALU.mult)
                    if a == 0:
                        link(ins)
                    else:
                        ins.then_inc(S["k_scaled"], 1)
            for n in range(NT):
                dve.wait_ge(S["n_keep"], n + 1)
                for par in range(2):
                    o = full(dve, "qk_st", n, par)[:, 0:256].rearrange("p (a t) -> p a t", a=2)
                    wv = w_ml[:, n].rearrange("p (a b) t -> p b a t", b=2)[:, par]
                    qv = qkw[:, n % 2, :].rearrange("p (a b t) -> p b a t", a=2, b=2)[:, par]
                    if n >= 2 and par == 0:
                        full(dve, "num", n - 2, 1)
                    V.scalar_tensor_tensor(out=qv, in0=o, scalar=0.125, in1=wv, op0=ALU.mult, op1=ALU.mult
                                           ).then_inc(free_sem("qk_st", n, par), 1)
                drained(dve, "qk_st", n, 0)
                drained(dve, "qk_st", n, 1)
                dve.sem_inc(S["qkw_ready"], 1)
                if n < NT - 1:
                    for a in range(2):
                        o = full(dve, "c_loc", n, a)[:, 0:258].rearrange("p (b v) -> p b v", b=2)
                        for par in range(2):
                            r = slice(64 * par, 64 * par + 64)
                            hh = 2 * a + par
                            dst = c_state[r, n + 1, a, :]
                            if n:
                                link(V.tensor_scalar(c_tmp[r, a, :], c_state[r, n, a, :], dfa[r, n, hh:hh + 1], None,
                                                     ALU.mult))
                                ins = V.scalar_tensor_tensor(out=dst, in0=o[r, par, :], scalar=dfb[r, n, hh:hh + 1],
                                                             in1=c_tmp[r, a, :], op0=ALU.mult, op1=ALU.add)
                            else:
                                ins = V.tensor_scalar(dst, o[r, par, :], dfb[r, n, hh:hh + 1], None, ALU.mult)
                            if par:
                                ins.then_inc(free_sem("c_loc", n, a), 1)
                            else:
                                link(ins)
                    drained(dve, "c_loc", n, 0)
                    drained(dve, "c_loc", n, 1)
                    dve.sem_inc(S["c_ready"], 1)
                drained(dve, "num", n, 0)
                drained(dve, "num", n, 1)
                nn = n_sb[:, n % 2].rearrange("p a (b v) -> p a b v", b=2)
                if n:
                    for par in range(2):
                        o = full(dve, "inter", n, par)[:, 0:258].rearrange("p (a v) -> p a v", a=2)
                        for a in range(2):
                            hh = 2 * a + par
                            ins = V.scalar_tensor_tensor(out=nn[:, a, par, :], in0=o[:, a, :],
                                                         scalar=wi_arg[:, n, hh:hh + 1], in1=nn[:, a, par, :],
                                                         op0=ALU.mult, op1=ALU.add)
                            if a:
                                ins.then_inc(free_sem("inter", n, par), 1)
                    drained(dve, "inter", n, 0)
                    drained(dve, "inter", n, 1)
                den = nn[:, :, :, 128:129].rearrange("p a b v -> p a (b v)")
                d2 = dn[:, n % 2, :].rearrange("p (a b) -> p a b", a=2)
                em = em_arg[:, n, :].rearrange("p (a b) -> p a b", a=2)
                link(V.tensor_scalar(d2, den, -1.0, None, ALU.mult))
                link(V.tensor_tensor(d2, d2, den, ALU.max))
                link(V.tensor_tensor(d2, d2, em, ALU.max))
                link(V.reciprocal(dn[:, n % 2, :], dn[:, n % 2, :]))
                for hh in range(4):
                    link(V.tensor_scalar(w_ml[:, n, hh, :], nn[:, hh // 2, hh % 2, 0:P], dn[:, n % 2, hh:hh + 1], None,
                                         ALU.mult))
                    link(V.bn_stats(st6, w_ml[:, n, hh, :]))
                    ins = V.bn_aggr(mv[:, 4 * n + hh, :], st6)
                    if hh < 3:
                        link(ins)
                    else:
                        ins.then_inc(S["hm_done"], 1)
                        dve.wait_ge(S["hm_done"], n + 1)
            dve.sem_inc(S["ln_var"], 1)
            for key in [(a, b) for a in range(2) for b in range(2)]:
                drained(dve, "o", *key)
            link(V.tensor_tensor(o_gate, o_gate, over(row("ml_norm", 512), 1, NT), ALU.mult))
            dve.wait_ge(S["ln_root"], 1)
            link(V.reciprocal(mv[:, :, 1], mv[:, :, 1]))
            for n in range(NT):
                for hh in range(4):
                    j = 4 * n + hh
                    link(V.tensor_scalar(w_ml[:, n, hh, :], w_ml[:, n, hh, :], mv[:, j, 0:1], mv[:, j, 1:2],
                                         ALU.subtract, ALU.mult))
            V.tensor_tensor(o_gate, o_gate, w_ml.rearrange("p n h t -> p n (h t)"), ALU.mult
                            ).then_inc(S["y_ml_ready"], 1)
            project_out(0)
            norm(1)
            mlp(0)
            norm(2)

            V.memset(xbc_in[:, :, 0:3], 0.0).then_inc(S["halo"], 1)
            V.memset(raw[:, :, 0:1], 0.0).then_inc(S["halo"], 1)
            d_ps = full(dve, "dt")[:, 0:32].rearrange("p (n c) -> p n c", n=NT)
            V.tensor_tensor(dtr, d_ps, over(row("ssm_dt_bias", 8), 1, NT), ALU.add).then_inc(free_sem("dt"), 1)
            drained(dve, "dt")
            V.scalar_tensor_tensor(out=dta, in0=dtr, scalar=-1.0, in1=dtr, op0=ALU.mult, op1=ALU.max
                                   ).then_inc(S["s_soft_e"], 1)
            dve.wait_ge(S["halo"], 5)
            for i in range(8):
                drained(dve, "xbc", i)
                conv(xbc[:, i, :], xbc_in[:, i, :], "ssm_conv_w", "ssm_conv_b", i, 8, S["ssm_conv"])
            for i in range(14):
                drained(dve, "rw", i)
                link(V.tensor_tensor(relu_t[:, i % 2, :], raw[:, i, 0:T], raw[:, i, 1:], ALU.subtract))
                ins = V.scalar_tensor_tensor(out=raw[:, i, 1:], in0=relu_t[:, i % 2, :], scalar=col_b("rw_mu", i),
                                             in1=raw[:, i, 1:], op0=ALU.mult, op1=ALU.add)
                if i < 13:
                    link(ins)
                else:
                    ins.then_inc(S["mixed"], 1)
            dve.wait_ge(S["s_soft_l"], 1)
            link(V.scalar_tensor_tensor(out=dtt, in0=dtr, scalar=0.0, in1=dta, op0=ALU.max, op1=ALU.add))
            V.scalar_tensor_tensor(out=dA, in0=dtt, scalar=-1.0, in1=over(expa, 1, NT), op0=ALU.mult, op1=ALU.mult
                                   ).then_inc(S["da_ready"], 1)
            o = full(dve, "a_cum")
            V.tensor_copy(acum, o[:, 0:64].rearrange("p (a b) -> p a b", a=2)).then_inc(free_sem("a_cum"), 1)
            drained(dve, "a_cum")
            link(V.tensor_tensor(dsx, acum[:, 1, :], acum[:, 0, :], ALU.subtract))
            V.tensor_scalar(nacum, acum[:, 0, :], -1.0, None, ALU.mult).then_inc(S["acum_args"], 1)
            dve.wait_ge(S["acum_exps"], 1)
            a4 = acum[:, 0, :].rearrange("p (n b c) -> p n b c", n=NT, b=2)
            h8 = lambda ap: ap.rearrange("p (c d) -> p c d", d=64)

            def ssd_front(n):
                b = n % 2
                for half in range(2):
                    diag(s_dg[:, half, :], a4[:, n, half, :], S["s_diag"])
                for half in range(2):
                    o = full(dve, "a_row", n, half).rearrange("p (a t) -> p a t", a=4)
                    V.tensor_tensor(s_t[:, half, :].rearrange("p (a t) -> p a t", a=4), o, over(const("add_st"), 1, 4),
                                    ALU.add).then_inc(free_sem("a_row", n, half), 1)
                    drained(dve, "a_row", n, half)
                    dve.sem_inc(S["s_masked"], 1)
                drained(dve, "x_tok", n)
                dt_n = dtt[:, n, :]
                if n >= 2:
                    full(dve, "y_diag", n - 2)
                    full(dve, "s_loc", n - 2)
                link(V.tensor_tensor(h8(xdt[:, b, :]), h8(xs_tok[:, b, :]), over(dt_n, 2, 64), ALU.mult))
                V.tensor_tensor(h8(xds[:, b, :]), h8(xdt[:, b, :]), over(ds_[:, 8 * n:8 * n + 8], 2, 64), ALU.mult
                                ).then_inc(S["xdt_ready"], 1)
                o = full(dve, "cb", n)[:, 0:256].rearrange("p (g t) -> p g t", g=2)
                for half in range(2):
                    dve.wait_ge(S["s_decay"], 2 * n + half + 1)
                    ins = V.tensor_tensor(s_m[:, b, half * 512:(half + 1) * 512].rearrange("p (a t) -> p a t", a=4),
                                          s_w[:, half, :].rearrange("p (a t) -> p a t", a=4), over(o[:, half, :], 1, 4),
                                          ALU.mult)
                    if half == 0:
                        link(ins)
                    else:
                        ins.then_inc(free_sem("cb", n), 1)
                drained(dve, "cb", n)
                dve.sem_inc(S["s_m_ready"], 1)

            for n in range(NT):
                b = n % 2
                ssd_front(n)
                y = s_y[:, n, :]
                link(V.tensor_tensor(h8(y), h8(xs_tok[:, b, :]), over(row("ssm_d", 8), 2, 64), ALU.mult))
                o = full(dve, "y_diag", n)
                V.tensor_tensor(y, y, o, ALU.add).then_inc(free_sem("y_diag", n), 1)
                drained(dve, "y_diag", n)
                if n:
                    o = full(dve, "y_off", n)
                    V.tensor_tensor(h8(relu_t[:, 0, :]), h8(o), over(ea[:, 8 * n:8 * n + 8], 2, 64), ALU.mult
                                    ).then_inc(free_sem("y_off", n), 1)
                    drained(dve, "y_off", n)
                    link(V.tensor_tensor(y, y, relu_t[:, 0, :], ALU.add))
                if n == 0:
                    for key in [(p, q) for p in range(2) for q in range(2)]:
                        drained(dve, "z", *key)
                V.tensor_tensor(y, y, z_tok[:, n, :], ALU.mult).then_inc(S["z_silu"], 1)
                dve.wait_ge(S["z_silu"], n + 1)
                dve.sem_inc(S["s_yprod"], 1)
                if n < NT - 1:
                    o = full(dve, "s_loc", n)
                    nxt = s_state[:, (n + 1) % 2, :]
                    if n:
                        link(V.tensor_tensor(h8(nxt), h8(s_state[:, b, :]), over(dec[:, 8 * n:8 * n + 8], 2, 64), ALU.mult))
                        V.tensor_tensor(nxt, nxt, o, ALU.add).then_inc(free_sem("s_loc", n), 1)
                    else:
                        V.tensor_copy(nxt, o).then_inc(free_sem("s_loc", n), 1)
                    drained(dve, "s_loc", n)
                    dve.sem_inc(S["s_new"], 1)
            dve.wait_ge(S["s_root"], 1)
            link(V.reciprocal(gss, gss))
            for n in range(NT):
                for g in range(2):
                    c = slice(g * 256, g * 256 + 256)
                    ins = V.scalar_tensor_tensor(out=s_y[:, n, c], in0=s_y[:, n, c], scalar=gss[:, 2 * n + g:2 * n + g + 1],
                                                 in1=row("ssm_norm", 512)[:, c], op0=ALU.mult, op1=ALU.mult)
                    if (n, g) == (NT - 1, 1):
                        ins.then_inc(S["y_ssm_ready"], 1)
                    else:
                        link(ins)
            for f in range(4):
                drained(dve, "y_ssm", f)
            link(V.tensor_scalar(omka, cols_t[:, A_N + B_AT["rw_k_a"]:A_N + B_AT["rw_k_a"] + 4], -1.0, 1.0,
                                 ALU.mult, ALU.add))
            for f in range(4):
                r_, k_ = raw[:, f, 1:], raw[:, 4 + f, 1:]
                if f:
                    dve.wait_ge(S["kk_sq"], f)
                V.tensor_scalar(t7, k_, col_b("rw_k_k", f), None, ALU.mult).then_inc(S["kkraw"], 1)
                drained(dve, "decay", f)
                link(V.tensor_tensor_scan(t3, const("reset"), t1, 0.0, ALU.mult, ALU.add))
                t3c = t3.rearrange("p (n t) -> p n t", n=NT)
                mid = t3[:, P // 2 - 1::P]
                end = t3[:, P - 1::P]
                link(V.tensor_tensor(e_a[:, f, :], end, mid, ALU.subtract))
                link(V.tensor_tensor(e_a[:, f, 0:NT - 1], e_a[:, f, 0:NT - 1], mid[:, 1:NT], ALU.add))
                link(V.tensor_copy(lnm[:, f, 0:NT], mid))
                link(V.tensor_tensor(t3c, t3c, over(lnm[:, f, 0:NT], 2, P), ALU.subtract))
                V.tensor_tensor(t4, t3, t1, ALU.subtract).then_inc(S["cum_args"], 1)
                drained(dve, "kk_sum", f)
                link(V.tensor_scalar(t6, t6, 1e-12, None, ALU.max))
                link(V.reciprocal(t6, t6))
                link(V.tensor_tensor(t7, t7, t6, ALU.mult))
                drained(dve, "a", f)
                link(V.tensor_scalar(t6, t2, col_b("rw_k_a", f), omka[:, f:f + 1], ALU.mult, ALU.add))
                link(V.tensor_tensor(k_, k_, t6, ALU.mult))
                V.scalar_tensor_tensor(out=mats_rk[:, f, :], in0=r_, scalar=col_b("rw_r_k", f), in1=k_, op0=ALU.mult,
                                       op1=ALU.mult).then_inc(S["rk_ready"], 1)
                link(V.tensor_tensor(t2, t2, t7, ALU.mult))
                dve.wait_ge(S["cum_exps"], f + 1)
                dve.wait_ge(S["rk_ready"], f + 1)
                link(V.tensor_tensor(b_s[:, f, :], t2, t3, ALU.mult))
                link(V.tensor_tensor(k_, k_, t3, ALU.mult))
                link(V.tensor_tensor(kk_s[:, f, :], t7, t4, ALU.mult))
                V.tensor_tensor(r_, r_, t5, ALU.mult).then_inc(S["tilde"], 1)
            dve.wait_ge(S["tilde"], 4)
            o = full(dve, "bonus")
            V.tensor_copy(bon, o[:, 0:32].rearrange("p (n c) -> p n c", n=NT)).then_inc(free_sem("bonus"), 1)
            dve.wait_ge(S["scales"], 1)
            lv = const("levels")
            for n in range(NT):
                for f in range(4):
                    for par in range(2):
                        o = full(dve, "mats", n, f, par)
                        V.scalar_tensor_tensor(out=mats[:, 2 * f + par].rearrange("p a b -> p (a b)"), in0=o, scalar=HUGE,
                                               in1=const("four"), op0=ALU.min, op1=ALU.mult
                                               ).then_inc(free_sem("mats", n, f, par), 1)
                for level in range(LEVELS):
                    mask = over(lv[:, level * P:(level + 1) * P], 1, 4)
                    for half in range(2):
                        hs = slice(4 * half, 4 * half + 4)
                        o = full(dve, "pt", n, level, half).rearrange("p (a t) -> p a t", a=4)
                        V.tensor_tensor(inv_p[:, hs, :], o, mask, ALU.mult).then_inc(free_sem("pt", n, level, half), 1)
                    for half in range(2):
                        hs = slice(4 * half, 4 * half + 4)
                        eye = over(ident, 1, 4)
                        if level < LEVELS - 1:
                            o = full(dve, "d", n, level, half).rearrange("p (a t) -> p a t", a=4)
                            full(dve, "dt_", n, level, half)
                            if level:
                                drained(dve, "d", n, level - 1, half)
                            V.tensor_tensor(inv_d[:, hs, :], inv_d[:, hs, :] if level else eye, o, ALU.subtract
                                            ).then_inc(free_sem("d", n, level, half), 1)
                        o = full(dve, "dt_", n, level, half).rearrange("p (a t) -> p a t", a=4)
                        if level:
                            drained(dve, "dt_", n, level - 1, half)
                        V.tensor_tensor(inv_t[:, hs, :], inv_t[:, hs, :] if level else eye, o, ALU.subtract
                                        ).then_inc(free_sem("dt_", n, level, half), 1)
                if n < NT - 1:
                    o = full(dve, "s_rw", n)
                    if n:
                        link(V.tensor_tensor(s_sum, s_rw[:, n % 2, :], o, ALU.add))
                    else:
                        link(V.tensor_copy(s_sum, o))
                    for f in range(4):
                        c = slice(f * P, (f + 1) * P)
                        ins = V.scalar_tensor_tensor(out=s_rw[:, (n + 1) % 2, c], in0=s_sum[:, c],
                                                     scalar=e_s[:, f, n:n + 1], in1=blocks, op0=ALU.mult, op1=ALU.mult)
                        if f < 3:
                            link(ins)
                        else:
                            ins.then_inc(free_sem("s_rw", n), 1)
                    drained(dve, "s_rw", n)
                    dve.sem_inc(S["s_rw_ready"], 1)
            for n in range(NT):
                drained(dve, "y", n)
                y8 = h8(y_rw[:, n, :])
                link(V.tensor_reduce(lnm[:, n, :], y8, AX.X, ALU.add))
                link(V.tensor_scalar(lnm[:, n, :], lnm[:, n, :], 1.0 / 64, None, ALU.mult))
                link(V.tensor_tensor(y8, y8, over(lnm[:, n, :], 2, 64), ALU.subtract))
                link(V.tensor_tensor(t1, y_rw[:, n, :], y_rw[:, n, :], ALU.mult))
                ins = V.tensor_reduce(lnv[:, n, :], h8(t1), AX.X, ALU.add)
                if n < NT - 1:
                    link(ins)
                else:
                    ins.then_inc(S["ln2_var"], 1)
            dve.wait_ge(S["ln2_root"], 1)
            link(V.reciprocal(lnv, lnv))
            for n in range(NT):
                drained(dve, "g_tok", n)
                drained(dve, "rv_tok", n)
                y = y_rw[:, n, :]
                link(V.tensor_tensor(h8(y), h8(y), over(lnv[:, n, :], 2, 64), ALU.mult))
                link(V.tensor_tensor(y, y, row("rw_ln_w", 512), ALU.mult))
                link(V.tensor_tensor(y, y, row("rw_ln_b", 512), ALU.add))
                link(V.tensor_tensor(h8(t1), h8(v_tok[:, n, :]), over(bon[:, n, :], 2, 64), ALU.mult))
                link(V.tensor_tensor(y, y, t1, ALU.add))
                V.tensor_tensor(y, y, g_tok[:, n, :], ALU.mult).then_inc(S["y_rw_ready"], 1)
            project_out(1)
            norm(3)
            mlp(1)
            norm(4)


PARAMS = ["x", "w_up", "w_down", "e_w_in", "e_w_out", "o_w_in", "o_w_out", "rw_w2", "rw_a2", "rw_g2"]


def kernel(**inputs):
    import concourse.bacc as bacc
    from concourse.bass_utils import run_bass_kernel_spmd

    nc = bacc.Bacc("TRN2", target_bir_lowering=False, num_devices=1)
    arrays, dram = {}, {}
    names = PARAMS + [n for n, _ in STACK_A + STACK_B + ROWS]
    data = {n: np.ascontiguousarray(inputs[n]) for n in names}
    data["main_const"] = np.concatenate([np.asarray(a, np.float32) for _, a in MAIN_COLS], 1)
    data["even_const"] = np.concatenate([np.asarray(a, np.float32) for _, a in EVEN_COLS], 1)
    for name, a in data.items():
        arrays[f"in_{name}"] = a
        dram[name] = nc.dram_tensor(f"in_{name}", a.shape, mybir.dt.from_np(a.dtype), kind="ExternalInput").ap()
    out = nc.dram_tensor("out_0", (1, T, D), F32, kind="ExternalOutput").ap()
    trunk(nc, dram, out)
    r = run_bass_kernel_spmd(nc, [arrays], core_ids=[0])
    return r.results[0]["out_0"]
```

```python
from contextlib import ExitStack

import numpy as np
import concourse.bass as bass
from concourse import mybir

F32 = mybir.dt.float32
F32R = mybir.dt.float32r
ALU = mybir.AluOpType
ACT = mybir.ActivationFunctionType
AX = mybir.AxisListType

P = 128
T = 512
NT = T // P
D = 1024
KT = D // P
FF = 4096
FT = FF // P
SW = P
RING = 4
CUT = 2
NBANK = 8
BANK = 512
NEG = -1.0e30
HUGE = 1.0e38
DECAY_K = float(np.exp(np.float32(-0.5)))

SUB = 32
LEVEL_SIZES = (32, 64)
LEVELS = len(LEVEL_SIZES)

_i = np.arange(P)
_row, _col = _i[:, None], _i[None, :]


def _const_columns():
    half = 8
    inv = np.float32(500000.0) ** (-np.arange(half, dtype=np.float32) * np.float32(2.0) / np.float32(16))
    ang = (np.arange(T, dtype=np.float32)[:, None] * inv[None, :]).astype(np.float32)
    cos, sin = np.ones((P, T), np.float32), np.zeros((P, T), np.float32)
    rot = np.zeros((P, P), np.float32)
    for base in (0, 64):
        for j in range(half):
            cos[base + j] = cos[base + half + j] = np.cos(ang[:, j])
            sin[base + j] = sin[base + half + j] = np.sin(ang[:, j])
            rot[base + half + j, base + j] = -1.0
            rot[base + j, base + half + j] = 1.0
    dup = np.zeros((P, 2, P), np.float32)
    for g in range(2):
        for m in range(P):
            dup[64 * g + m % 64, g, m] = 1.0
    k = np.arange(2 * P)[None, :]
    band = np.where((k > _row) & (k <= _row + P), 0.0, NEG)
    first = np.where((k > _row) & (k <= _row + P) & (k >= P), 0.0, NEG)
    even = [("cos", cos), ("sin", sin), ("rot", rot), ("dup", dup.reshape(P, -1)), ("band", band), ("first", first)]
    common = [
        ("ident", np.eye(P)), ("ones", np.ones((P, P))),
        ("upper", _row <= _col),
        ("blocks", (_row // 64) == (_col // 64)),
        ("add_st", np.where(_row <= _col, 0.0, NEG)),
        ("add_ts", np.where(_col <= _row, 0.0, NEG)),
        ("eps", np.repeat(np.array([[1e-5, 1e-6, 64e-5, 0.0]]), P, 0)),
    ]
    levels = []
    for b in LEVEL_SIZES:
        levels.append(((_col // b) % 2 == 1) & ((_row // b) == (_col // b) - 1))
    reset = np.ones((P, T))
    reset[:, ::P] = 0.0
    odd = [
        ("levels", np.concatenate(levels, 1)),
        ("four", np.concatenate([_col < _row, _row < _col, _row <= _col, _row <= _col], 1)),
        ("reset", reset),
        ("heads", np.stack([_i // 64 == 0, _i // 64 == 1], 1)),
    ]
    return common + odd, even


def _offsets(cols):
    at, out = 0, {}
    for name, a in cols:
        out[name] = (at, a.shape[1])
        at += a.shape[1]
    return out, at


MAIN_COLS, EVEN_COLS = _const_columns()
MAIN_AT, MAIN_W = _offsets(MAIN_COLS)
EVEN_AT, EVEN_W = _offsets(EVEN_COLS)

STACK_A = [("mix_norm", 16), ("mlp_norm", 16), ("final_norm", 8), ("ml_conv_w", 16), ("ml_conv_b", 4),
           ("ssm_conv_w", 32), ("ssm_conv_b", 8)]
STACK_B = [("rw_mu", 14), ("rw_w0", 4), ("rw_a0", 4), ("rw_k_k", 4), ("rw_k_a", 4), ("rw_r_k", 4)]
ROWS = [("att_sinks", 8), ("ml_i_bias", 4), ("ml_f_bias", 4), ("ssm_dt_bias", 8), ("ssm_a_log", 8), ("ssm_d", 8),
        ("ml_norm", 512), ("ssm_norm", 512), ("rw_ln_w", 512), ("rw_ln_b", 512)]


def _starts(spec):
    at, out = 0, {}
    for name, n in spec:
        out[name] = at
        at += n
    return out, at


A_AT, A_N = _starts(STACK_A)
B_AT, B_N = _starts(STACK_B)
R_AT, R_N = _starts(ROWS)

E_GATES, E_Q, E_K, E_VA, E_QK, E_V, E_O = 2304, 0, 512, 640, 768, 1280, 1792
GATE_SLOT = E_GATES + 8 - P
EVEN_SLOTS = ([(GATE_SLOT, ("f", "gates"))] + [(E_QK + P * j, ("qk", j)) for j in range(4)]
              + [(E_K, ("k",)), (E_VA, ("f", "v_att"))] + [(E_Q + P * j, ("q", j)) for j in range(4)]
              + [(E_V + P * j, ("f", "v", j)) for j in range(4)] + [(E_O + P * j, ("f", "o", j)) for j in range(4)])
O_Z, O_XBC, O_DT, O_RW = 0, 512, 1536, 1544
RW_ORDER = [12, 13] + list(range(4, 8)) + list(range(4)) + list(range(8, 12))
ODD_SLOTS = ([(O_DT, ("f", "dt"))] + [(O_XBC + P * j, ("xbc", j)) for j in range(8)]
             + [(O_Z + P * j, ("f", "z", j)) for j in range(4)] + [(O_RW + P * j, ("rw", j)) for j in RW_ORDER])


def even_front():
    for j in range(11):
        yield "slot", j
        if j == 1:
            yield "turn", ("gates",)
        if j == 6:
            yield "rope", 4
        if j == 7:
            yield "turn", ("v_att",)
        if j == 8:
            yield "dup", 0
            yield "dup", 1
        if j == 9:
            yield "rope", 0
            yield "rope", 1
    yield "rope", 2
    for u in range(8 + 3):
        if u < 8:
            yield "slot", 11 + u
        if u == 0:
            yield "rope", 3
        if 1 <= u < 9:
            yield "turn", EVEN_SLOTS[10 + u][1][1:]
        if u < 8:
            yield "score", u
        if 2 <= u < 10:
            yield "att_turn", u - 2
        if u >= 3:
            yield "att_out", u - 3
        if u < 8:
            yield "att_exp", u


def odd_front():
    after = {14: ("ssd_front", 0), 16: ("ssd_back", 0), 17: ("ssd_front", 1), 19: ("ssd_back", 1),
             20: ("ssd_front", 2), 22: ("ssd_back", 2), 23: ("ssd_front", 3), 25: ("ssd_back", 3)}
    for j in range(len(ODD_SLOTS)):
        yield "slot", j
        if j == 1:
            yield "turn", ("dt",)
        if 10 <= j < 14:
            yield "turn", ("z", j - 10)
        if j == 13:
            yield "a_cum",
        if j in after:
            yield after[j]


STAGE_AT = 13056
ARENA = STAGE_AT + 2 * P


class Plan:

    def __init__(self):
        self.turns = [0] * NBANK
        self.at = {}
        self.next = 0

    def put(self, *key, bank=None, times=1):
        if bank is None:
            bank = self.next
            self.next = (self.next + 1) % NBANK
        assert key not in self.at, key
        self.at[key] = (bank, self.turns[bank])
        self.turns[bank] += times


def make_plan():
    plan = Plan()
    put = plan.put
    put("stack_a")
    put("stack_b")
    for k in range(KT):
        put("x", k)
    for layer in range(2):
        put("norm", 2 * layer)
        if layer == 0:
            for item in even_front():
                kind = item[0]
                if kind == "slot":
                    put(*EVEN_SLOTS[item[1]][1])
                elif kind == "turn":
                    put(*item[1])
                elif kind in ("rope", "dup"):
                    put(*item)
                elif kind == "score":
                    put("score", item[1], 0)
                    put("score", item[1], 1)
                elif kind == "att_turn":
                    put("turn", item[1], 0)
                    put("turn", item[1], 1)
                elif kind == "att_out":
                    put("att", item[1])
            put("cum")
            for n in range(NT):
                put("g_row", n)
            for a in range(2):
                put("k_tok", a)
            for n in range(NT):
                put("m_row", n)
            for n in range(NT):
                for par in range(2):
                    put("qk_st", n, par)
                if n < NT - 1:
                    for a in range(2):
                        put("c_loc", n, a)
                for a in range(2):
                    put("num", n, a)
                if n:
                    for par in range(2):
                        put("inter", n, par)
            for f in range(4):
                put("y_ml", f)
        else:
            for item in odd_front():
                kind = item[0]
                if kind == "slot":
                    put(*ODD_SLOTS[item[1]][1])
                elif kind == "turn":
                    put(*item[1])
                elif kind == "a_cum":
                    put("a_cum")
                elif kind == "ssd_front":
                    n = item[1]
                    put("x_tok", n)
                    put("b_tok", n)
                    put("a_row", n, 0)
                    put("a_row", n, 1)
                    put("cb", n)
                else:
                    n = item[1]
                    put("y_diag", n)
                    if n:
                        put("y_off", n)
                    if n < NT - 1:
                        put("s_loc", n)
            for f in range(4):
                put("y_ssm", f)
            for f in range(4):
                put("decay", f)
                put("a", f)
                put("kk_sum", f)
            for n in range(NT):
                put("g_tok", n)
            for n in range(NT):
                put("rv_tok", n)
            put("bonus")
            for n in range(NT):
                for par in range(2):
                    put("sub", n, par)
            for n in range(NT):
                put("rk_tok", n)
                put("rb_tok", n)
                for f in range(4):
                    for par in range(2):
                        put("mats", n, f, par)
                for level in range(LEVELS):
                    put("pt", n, level, 0)
                    put("pt", n, level, 1)
                    for half in range(2):
                        if level < LEVELS - 1:
                            put("d", n, level, half)
                        put("dt_", n, level, half)
                put("rhs", n)
                put("u", n)
                put("y", n)
                if n < NT - 1:
                    put("s_rw", n)
            for f in range(4):
                put("y_rw", f)
        for j in range(KT):
            put("out", layer, j, bank=j)
        put("norm", 2 * layer + 1, bank=0)
        for j in range(8):
            put("mlp", layer, j, bank=j, times=8)
    put("norm", 4)
    for t in range(NT):
        for half in range(2):
            put("result", t, half)
    return plan


def trunk(nc, dram, out):
    PLAN = make_plan()
    with ExitStack() as ctx:
        def sb(name, width):
            return ctx.enter_context(nc.sbuf_tensor(name, [P, width], F32))

        def sem(name):
            return ctx.enter_context(nc.semaphore(name))

        def cut(tile, at, *shape):
            n = int(np.prod(shape))
            v = tile[:, at:at + n]
            if len(shape) == 2:
                v = v.rearrange("p (a b) -> p a b", b=shape[1])
            if len(shape) == 3:
                v = v.rearrange("p (a b c) -> p a b c", b=shape[1], c=shape[2])
            return v

        ps = ctx.enter_context(nc.psum_tensor("ps", [P, NBANK, BANK], F32))
        h_t = sb("h", KT * T)
        y_t = sb("y_mix", KT * T)
        raw_w = sb("raw_w", RING * KT * SW)[:, :].rearrange("p (r k c) -> p r k c", r=RING, c=SW)

        def sbr(stack, name, width):
            return stack.enter_context(nc.sbuf_tensor(name, [P, width], F32R))

        w_hi = sbr(ctx, "w_hi", CUT * KT * SW)[:, :].rearrange("p (r k c) -> p r k c", r=CUT, c=SW)
        w_lo = sbr(ctx, "w_lo", CUT * KT * SW)[:, :].rearrange("p (r k c) -> p r k c", r=CUT, c=SW)
        main_t = sb("main", MAIN_W)
        cols_t = sb("cols", A_N + B_N)
        rows_t = sb("rows", R_N)
        small = sb("small", 640)
        rwkv_raw = sb("rwkv_raw", 14 * (T + 1))
        with ExitStack() as inner:
            hn_hi = sbr(inner, "hn_hi", KT * T)[:, :].rearrange("p (k t) -> p k t", t=T)
            hn_lo = sbr(inner, "hn_lo", KT * T)[:, :].rearrange("p (k t) -> p k t", t=T)
        late = sb("late", 2 * KT * T)
        with ExitStack() as inner:
            hid_hi = sbr(inner, "hid_hi", KT * T)[:, :].rearrange("p (k t) -> p k t", t=T)
            hid_lo = sbr(inner, "hid_lo", KT * T)[:, :].rearrange("p (k t) -> p k t", t=T)
        arena = sb("arena", ARENA)
        rms_t = sb("rms", T)[:, :]
        relu_t = sb("relu", 2 * T)[:, :].rearrange("p (a t) -> p a t", a=2)
        lora = sb("lora", 512 * 2)

        h = cut(h_t, 0, KT, T)
        y_mix = cut(y_t, 0, KT, T)

        def const(name):
            at, w = MAIN_AT[name]
            return main_t[:, at:at + w]

        ident, ones, upper, blocks = const("ident"), const("ones"), const("upper"), const("blocks")
        eps = const("eps")

        def col_a(name, i):
            return cols_t[:, A_AT[name] + i:A_AT[name] + i + 1]

        def col_b(name, i):
            return cols_t[:, A_N + B_AT[name] + i:A_N + B_AT[name] + i + 1]

        def row(name, width):
            return rows_t[:, R_AT[name]:R_AT[name] + width]

        def over(ap, axis, n):
            v = ap.unsqueeze(axis)
            shape = list(v.shape)
            shape[axis] = n
            return v.to_broadcast(shape)

        bank_full = [sem(f"bank_full{b}") for b in range(NBANK)]
        bank_free = [sem(f"bank_free{b}") for b in range(NBANK)]
        w_full = [sem(f"w_full{r}") for r in range(RING)]
        w_high = sem("w_high")
        w_cut = sem("w_cut")
        x_in = sem("x_in")
        main_in = sem("main_in")
        even_in = sem("even_in")
        stack_in = sem("stack_in")
        rows_in = sem("rows_in")
        lora_in = sem("lora_in")
        out_done = sem("out_done")
        dve_step = sem("dve_step")
        act_step = sem("act_step")
        stack_zero = sem("stack_zero")
        squared = sem("squared")
        rms_root = sem("rms_root")
        normed = sem("normed")
        summed = sem("summed")
        scaled = sem("scaled")
        high = sem("high")
        hid_square, hid_high, hid_ready = sem("hid_square"), sem("hid_high"), sem("hid_ready")

        def bank(key):
            return ps[:, PLAN.at[key][0], :]

        def free(eng, *key):
            b, turn = PLAN.at[key]
            if turn:
                eng.wait_ge(bank_free[b], turn)
            return ps[:, b, :]

        def full(eng, *key):
            b, turn = PLAN.at[key]
            eng.wait_ge(bank_full[b], turn + 1)
            return ps[:, b, :]

        def drained(eng, *key):
            b, turn = PLAN.at[key]
            eng.wait_ge(bank_free[b], turn + 1)

        def full_sem(*key):
            return bank_full[PLAN.at[key][0]]

        def free_sem(*key):
            return bank_free[PLAN.at[key][0]]

        base = {}
        n_slots = 0
        for layer in range(2):
            base["in", layer] = n_slots
            n_slots += len(EVEN_SLOTS if layer == 0 else ODD_SLOTS)
            base["out", layer] = n_slots
            n_slots += KT
            base["mlp", layer] = n_slots
            n_slots += 4 * 16

        slot_use = []
        for layer in range(2):
            slot_use += [PLAN.at[key] for _, key in (EVEN_SLOTS if layer == 0 else ODD_SLOTS)]
            slot_use += [PLAN.at["out", layer, j] for j in range(KT)]
            for s in range(4 * 16):
                b, t0 = PLAN.at["mlp", layer, s % 8]
                slot_use.append((b, t0 + s // 8))

        w_in = [dram["e_w_in"][0], dram["o_w_in"][0]]
        w_out = [dram["e_w_out"][0], dram["o_w_out"][0]]

        pos = [0]

        def take(*shape):
            at = pos[0]
            pos[0] += int(np.prod(shape))
            assert pos[0] <= STAGE_AT, pos[0]
            return cut(arena, at, *shape)

        even_t = take(EVEN_W)

        def even_const(name):
            at, w = EVEN_AT[name]
            return even_t[:, at:at + w]

        x_tok_in = rwkv_raw[:, 0:NT * D].rearrange("p (n d) -> p n d", n=NT)
        qk_raw = rwkv_raw[:, 4096:4096 + 5 * T].rearrange("p (a t) -> p a t", a=5)
        q_rot = qk_raw
        k_rot = rwkv_raw[:, 6656:6656 + T]
        f_tile = [cut(rwkv_raw, 2048, 2, T), cut(y_t, 3072, 2, T)]
        k_dup = take(2, P + T)
        v_dup = take(NT + 1, 2, P)
        conv_at = pos[0]
        conv_in = take(4, T + 3)
        conv_out = take(4, T)
        v_ml = take(NT, 4, 129)
        o_gate = take(NT, 512)
        att_p = [cut(rwkv_raw, 0, 4, 256), cut(rwkv_raw, 1024, 4, 256),
                 relu_t.rearrange("p a t -> p (a t)").rearrange("p (j k) -> p j k", k=256)]
        att_pt = y_mix[:, 4:, :].rearrange("p (a b) t -> p a b t", a=2)
        k_w = cut(arena, conv_at, NT, 256)
        w_ml = cut(late, 0, 4, 4, P)
        k_keep = cut(rwkv_raw, 0, 2, 512)
        dg = cut(rwkv_raw, 1024, 2, 4 * P)
        mtmp = cut(rwkv_raw, 2048, 2, 4 * P)
        qkw = cut(rwkv_raw, 3072, 2, 4 * P)
        n_sb = cut(rwkv_raw, 4096, 2, 2, 129 * 2)
        c_state = cut(rwkv_raw, 4096 + 1032, NT, 2, 129)
        c_tmp = cut(rwkv_raw, 4096 + 1032 + 1032, 2, 129)
        sm_at = [0]

        def tiny(*shape):
            at = sm_at[0]
            sm_at[0] += int(np.prod(shape))
            assert sm_at[0] <= 640
            return cut(small, at, *shape)

        a_mx, a_nm, a_se, a_rs, a_es, a_l = (tiny(3, 4) for _ in range(6))
        gt = tiny(NT, 8)
        fg, af, lf, li, gg, gmax, cmx, mx, marr, mm, dfa, dfb, wi_arg, em_arg = (tiny(NT, 4) for _ in range(14))
        cumb = tiny(2, 16)
        wgt_arg = tiny(NT, 4)
        dn = tiny(2, 4)
        st6 = tiny(6)
        mv = tiny(16, 2)

        raw = cut(rwkv_raw, 0, 14, T + 1)
        pos[0] = 0
        z_tok = take(NT, 512)
        xbc_at = pos[0]
        xbc_in = take(8, T + 3)
        xbc = take(8, T)
        xs_tok = take(2, 512)
        b_tok = take(2, 256)
        s_state = take(2, 512)
        xdt, xds, s_w, s_t = (cut(arena, xbc_at + j * 1024, 2, 512) for j in range(4))
        s_dg = s_t
        s_m = cut(y_t, 0, 2, 8 * P)
        s_y = y_mix[:, 4:, :]
        pos[0] = 0
        kk_s, b_s, v_tok, g_tok = (cut(late, j * 2048, 4, T) for j in range(4))
        t1, t8 = take(T), take(T)
        inv_at = pos[0]
        inv_d = take(8, P)
        inv_t = take(8, P)
        inv_p = take(8, P)
        t2, t3, t4, t5, t6, t7 = (cut(arena, inv_at + j * T, T) for j in range(6))
        y_rw = take(NT, 512)
        mats_at = pos[0]
        mats = take(8, 4, P)
        mats_rk = cut(arena, mats_at, 4, T)
        sums_at = pos[0]
        s_sum = take(512)
        rhs_sb = take(512)
        neg_u = take(512)
        s_rw = take(2, 512)
        sub_tok, sub_prob = (cut(arena, sums_at + j * SUB * SUB, SUB, SUB) for j in range(2))
        sub_tmp = cut(arena, sums_at + 2 * SUB * SUB, 512)
        sub_inv = cut(arena, inv_at, SUB, SUB)
        inv_rows, inv_cols = (cut(rwkv_raw, 8 * (T + 1) + j * SUB * SUB, SUB, SUB) for j in range(2))
        k_tok, bb_tok = (cut(y_t, 2048 + j * 1024, 2, 512) for j in range(2))
        wa2 = lora[:, 0:512]
        g2 = lora[:, 512:1024]
        sm_at[0] = 0
        dtr, dta, dte, dtt, dA = (tiny(NT, 8) for _ in range(5))
        acum = tiny(2, 32)
        nacum, dsx, ea, ds_, dec = (tiny(32) for _ in range(5))
        expa = tiny(8)
        gss = tiny(8)
        bon = tiny(NT, 8)
        e_s = tiny(4, NT)
        e_a = tiny(4, NT)
        omka = tiny(4)
        lnm = tiny(NT, 8)
        lnv = tiny(NT, 8)

        names = ("att_max att_exp att_probs halo rope_done kd_v v_ones conv_ready silu_done soft_e soft_l lf_ready "
                 "g_diag g_ready m_diag m_ready wl_ready mexp k_scaled qkw_ready c_ready n_keep hm_done ln_var ln_root "
                 "o_sig y_ml_ready ssm_conv ssm_silu s_soft_e s_soft_l da_ready acum_args acum_exps s_diag s_masked "
                 "s_decay s_m_ready xdt_ready s_new xs_kept s_yprod z_silu s_sq s_root y_ssm_ready mixed tanh_done "
                 "gd_sig sgm a_sig cum_args cum_exps kk_sq kk_root rk_ready scales_arg scales tilde mats_ready "
                 "inv_step urhs_ready s_rw_ready ln2_sq ln2_var ln2_root y_rw_ready x_out kkraw inv_zero inv_filled").split()
        S = {n: sem(n) for n in names}

        block = ctx.enter_context(nc.Block())

        @block.sync
        def _(sp):
            sp.dma_start(x_tok_in, dram["x"][0].rearrange("(n p) d -> p n d", p=P)).then_inc(x_in, 16)

            def load(n, src):
                if n >= RING:
                    sp.wait_ge(w_cut, n - RING + 1)
                sp.dma_start(raw_w[:, n % RING], src).then_inc(w_full[n % RING], 16)

            for layer in range(2):
                for j, (c0, _) in enumerate(EVEN_SLOTS if layer == 0 else ODD_SLOTS):
                    load(base["in", layer] + j, w_in[layer][:, c0:c0 + SW].rearrange("(k p) c -> p k c", p=P))
                for j in range(KT):
                    load(base["out", layer] + j,
                         w_out[layer][:, j * SW:(j + 1) * SW].rearrange("(k p) c -> p k c", p=P))
                up = dram["w_up"][layer].rearrange("(k p) c -> p k c", p=P)
                down = dram["w_down"][layer].rearrange("(k p) c -> p k c", p=P)
                b0 = base["mlp", layer]
                with sp.Fori(0, 4) as i:
                    for s in range(16):
                        sp.wait_ge(w_cut, i * 16 + (b0 + s - RING + 1))
                        src = (up[:, :, bass.ds(i * (KT * SW) + s * SW, SW)] if s < 8 else
                               down[:, bass.ds(i * KT, KT), (s - 8) * SW:(s - 7) * SW])
                        sp.dma_start(raw_w[:, (b0 + s) % RING], src).then_inc(w_full[(b0 + s) % RING], 16)
            for t in range(NT):
                sp.wait_ge(S["x_out"], 2 * (t + 1))
                sp.dma_start(out[0, t * P:(t + 1) * P, :], arena[:, t * D:(t + 1) * D]).then_inc(out_done, 16)
            sp.wait_ge(out_done, 16 * NT)

        @block.gpsimd
        def _(pool):
            pool.dma_start(main_t[:, :], dram["main_const"]).then_inc(main_in, 16)
            n_stack = 0
            nc.gpsimd.memset(arena[:, STAGE_AT:STAGE_AT + 2 * P], 0.0).then_inc(stack_zero, 1)
            pool.wait_ge(stack_zero, 1)
            stage = {"a": (arena[:, STAGE_AT:STAGE_AT + P], STACK_A, A_AT), "b": (arena[:, STAGE_AT + P:STAGE_AT + 2 * P], STACK_B, B_AT)}
            for key in "ab":
                tile, spec, at = stage[key]
                for name, n in spec:
                    a = dram[name]
                    flat = a.rearrange(" ".join("abcd"[:len(a.shape)]) + " -> (" + " ".join("abcd"[:len(a.shape)]) + ")") \
                        if len(a.shape) > 1 else a
                    pool.dma_start(tile[at[name]:at[name] + n, :], flat.rearrange("(n p) -> n p", p=P)
                                   ).then_inc(stack_in, 16)
                    n_stack += 1
            pool.dma_start(even_t, dram["even_const"]).then_inc(even_in, 16)
            for name, n in ROWS:
                pool.dma_start(row(name, n), dram[name][0:1, :].to_broadcast([P, n])).then_inc(rows_in, 16)
            pool.dma_start(wa2[0:64, :], dram["rw_w2"][0]).then_inc(lora_in, 16)
            pool.dma_start(wa2[64:128, :], dram["rw_a2"][0]).then_inc(lora_in, 16)
            pool.dma_start(g2, dram["rw_g2"][0]).then_inc(lora_in, 16)

            def low_part(n):
                nc.gpsimd.tensor_tensor(w_lo[:, n % CUT], raw_w[:, n % RING], w_hi[:, n % CUT].bitcast(F32), ALU.subtract).then_inc(w_cut, 1)

            for layer in range(2):
                for n in range(base["in", layer], base["mlp", layer]):
                    pool.wait_ge(w_high, n + 1)
                    low_part(n)
                b0 = base["mlp", layer]
                with pool.Fori(0, 4) as i:
                    for s in range(16):
                        pool.wait_ge(w_high, i * 16 + (b0 + s + 1))
                        low_part(b0 + s)

        N_STACK = len(STACK_A) + len(STACK_B)
        stage_a, stage_b = arena[:, STAGE_AT:STAGE_AT + P], arena[:, STAGE_AT + P:STAGE_AT + 2 * P]

        @block.tensor
        def _(pe):
            mm = nc.tensor.matmul

            def close(ins, *key):
                ins.then_inc(full_sem(*key), 1)

            def turn(key, parts):
                o = free(pe, *key)
                for j, src in enumerate(parts):
                    ins = nc.tensor.transpose(o[:, j * P:(j + 1) * P], src, ident)
                close(ins, *key)

            def norm(i):
                o = free(pe, "norm", i)
                pe.wait_ge(summed, KT * (i + 1))
                close(mm(o, ones, rms_t, start=True, stop=True), "norm", i)

            def products(pairs):
                for k in range(KT):
                    o, (a_hi, a_lo), (b_hi, b_lo) = pairs(k)
                    mm(o, a_hi, b_hi, start=(k == 0), stop=False)
                    mm(o, a_hi, b_lo, start=False, stop=False)
                    ins = mm(o, a_lo, b_hi, start=False, stop=(k == KT - 1))
                return ins

            def feature_tile(o, slot, hi, lo, before=None):
                def pairs(k):
                    if before:
                        before(k)
                    return o, (w_hi[:, slot, k, :], w_lo[:, slot, k, :]), (hi[:, k, :], lo[:, k, :])
                return products(pairs)

            def operand_ready(phase):
                return lambda k: pe.wait_ge(normed, KT * phase + k + 1)

            def project_in(layer, j):
                n = base["in", layer] + j
                key = (EVEN_SLOTS if layer == 0 else ODD_SLOTS)[j][1]
                pe.wait_ge(w_cut, n + 1)
                close(feature_tile(free(pe, *key), n % CUT, hn_hi, hn_lo,
                                   before=operand_ready(3 * layer) if j == 0 else None), *key)

            def turn_projected(layer, key, buf):
                drained(pe, "f", *key)
                turn(key, [f_tile[layer][:, buf, t * P:(t + 1) * P] for t in range(NT)])

            def project_out(layer):
                for j in range(KT):
                    n = base["out", layer] + j
                    pe.wait_ge(w_cut, n + 1)
                    close(feature_tile(free(pe, "out", layer, j), n % CUT, hid_hi, hid_lo,
                                       before=operand_ready(3 * layer + 1) if j == 0 else None), "out", layer, j)

            def mlp(layer):
                b0 = base["mlp", layer]
                with pe.Fori(0, 4) as i:
                    for s in range(16):
                        n = b0 + s
                        b, t0 = PLAN.at["mlp", layer, s % 8]
                        pe.wait_ge(w_cut, i * 16 + (n + 1))
                        pe.wait_ge(bank_free[b], i * 2 + (t0 + s // 8))
                        if s < 8:
                            ins = feature_tile(ps[:, b, :], n % CUT, hn_hi, hn_lo,
                                               before=operand_ready(3 * layer + 2) if s == 0 else None)
                        else:
                            ins = feature_tile(ps[:, b, :], n % CUT, hid_hi, hid_lo, before=(
                                lambda k: pe.wait_ge(hid_ready, i * 8 + (32 * layer + k + 1))) if s == 8 else None)
                        ins.then_inc(bank_full[b], 1)

            def even():
                dup = even_const("dup").rearrange("p (g m) -> p g m", g=2)
                turned = 0
                for item in even_front():
                    kind, u = item[0], item[1]
                    n, g = (u // 2, u % 2) if kind in ("score", "att_out") else (None, None)
                    if kind == "slot":
                        project_in(0, u)
                    elif kind == "turn":
                        turn_projected(0, u, turned % 2)
                        turned += 1
                    elif kind == "rope":
                        drained(pe, *(("q", u) if u < 4 else ("k",)))
                        pe.wait_ge(even_in, 16)
                        close(mm(free(pe, "rope", u), even_const("rot"), qk_raw[:, u, :], start=True, stop=True),
                              "rope", u)
                    elif kind == "dup":
                        pe.wait_ge(S["rope_done"], 1)
                        close(mm(free(pe, "dup", u), dup[:, u, :], k_rot, start=True, stop=True), "dup", u)
                    elif kind == "score":
                        if u == 0:
                            drained(pe, "dup", 1)
                            drained(pe, "dup", 0)
                            pe.wait_ge(S["halo"], 3)
                            drained(pe, "v_att")
                        pe.wait_ge(S["rope_done"], 3 if u == 0 else 5)
                        for par in range(2):
                            o = free(pe, "score", u, par)
                            r = slice(64 * par, 64 * par + 64)
                            for a in range(2):
                                ins = mm(o[:, a * 256:(a + 1) * 256], q_rot[r, 2 * g + a, n * P:(n + 1) * P],
                                         k_dup[r, g, n * P:n * P + 256], start=True, stop=True)
                            close(ins, "score", u, par)
                    elif kind == "att_turn":
                        pe.wait_ge(S["att_probs"], u + 1)
                        for blk in range(2):
                            turn(("turn", u, blk), [att_p[u % 3][:, j, blk * P:(blk + 1) * P] for j in range(4)])
                    elif kind == "att_out":
                        o = free(pe, "att", u)
                        for blk in range(2):
                            drained(pe, "turn", u, blk)
                            ins = mm(o, v_dup[:, n + blk, g, :], att_pt[:, u % 2, blk, :], start=(blk == 0), stop=(blk == 1))
                        close(ins, "att", u)
                pe.wait_ge(S["lf_ready"], 1)
                o = free(pe, "cum")
                lf_ = lf.rearrange("p a b -> p (a b)")
                mm(o[:, 0:16], upper, lf_, start=True, stop=True)
                close(mm(o[:, 16:32], ones, lf_, start=True, stop=True), "cum")
                for n in range(NT):
                    pe.wait_ge(S["g_diag"], n + 1)
                    close(mm(free(pe, "g_row", n), ones, dg[:, n % 2, :], start=True, stop=True), "g_row", n)
                pe.wait_ge(S["silu_done"], 4)
                for a in range(2):
                    turn(("k_tok", a), [conv_out[:, 2 + a, n * P:(n + 1) * P] for n in range(NT)])
                for n in range(NT):
                    pe.wait_ge(S["m_diag"], n + 1)
                    close(mm(free(pe, "m_row", n), ones, dg[:, n % 2, :], start=True, stop=True), "m_row", n)
                for j in range(4):
                    drained(pe, "v", j)
                pe.wait_ge(S["v_ones"], 1)
                for n in range(NT):
                    tok = slice(n * P, (n + 1) * P)
                    for par in range(2):
                        o = free(pe, "qk_st", n, par)
                        r = slice(64 * par, 64 * par + 64)
                        for a in range(2):
                            ins = mm(o[:, a * P:(a + 1) * P], conv_out[r, 2 + a, tok], conv_out[r, a, tok],
                                     start=True, stop=True)
                        close(ins, "qk_st", n, par)
                    if n < NT - 1:
                        pe.wait_ge(S["k_scaled"], n + 1)
                        for a in range(2):
                            o = free(pe, "c_loc", n, a)
                            for par in range(2):
                                ins = mm(o[:, par * 129:(par + 1) * 129], k_w[:, n, a * P:(a + 1) * P],
                                         v_ml[:, n, 2 * a + par, :], start=True, stop=True)
                            close(ins, "c_loc", n, a)
                    pe.wait_ge(S["qkw_ready"], n + 1)
                    for a in range(2):
                        o = free(pe, "num", n, a)
                        for par in range(2):
                            hh = 2 * a + par
                            ins = mm(o[:, par * 129:(par + 1) * 129], qkw[:, n % 2, hh * P:(hh + 1) * P],
                                     v_ml[:, n, hh, :], start=True, stop=True)
                        close(ins, "num", n, a)
                    if n:
                        pe.wait_ge(S["c_ready"], n)
                        for par in range(2):
                            o = free(pe, "inter", n, par)
                            r = slice(64 * par, 64 * par + 64)
                            for a in range(2):
                                ins = mm(o[:, a * 129:(a + 1) * 129], conv_out[r, a, tok], c_state[r, n, a, :],
                                         start=True, stop=True)
                            close(ins, "inter", n, par)
                pe.wait_ge(S["y_ml_ready"], 1)
                for f in range(4):
                    turn(("y_ml", f), [o_gate[:, n, f * P:(f + 1) * P] for n in range(NT)])

            def odd():
                turned = 0
                for item in odd_front():
                    kind = item[0]
                    n = item[1] if kind in ("ssd_front", "ssd_back") else 0
                    tok = slice(n * P, (n + 1) * P)
                    if kind == "slot":
                        project_in(1, item[1])
                    elif kind == "turn":
                        turn_projected(1, item[1], turned % 2)
                        turned += 1
                    elif kind == "a_cum":
                        pe.wait_ge(S["da_ready"], 1)
                        o = free(pe, "a_cum")
                        da_ = dA.rearrange("p a b -> p (a b)")
                        mm(o[:, 0:32], upper, da_, start=True, stop=True)
                        close(mm(o[:, 32:64], ones, da_, start=True, stop=True), "a_cum")
                    elif kind == "ssd_front":
                        pe.wait_ge(S["ssm_silu"], 8)
                        turn(("x_tok", n), [xbc[:, i, tok] for i in range(4)])
                        turn(("b_tok", n), [xbc[:, 4 + g, tok] for g in range(2)])
                        for half in range(2):
                            pe.wait_ge(S["s_diag"], 2 * n + half + 1)
                            close(mm(free(pe, "a_row", n, half), ones, s_dg[:, half, :], start=True, stop=True),
                                  "a_row", n, half)
                        o = free(pe, "cb", n)
                        for g in range(2):
                            ins = mm(o[:, g * P:(g + 1) * P], xbc[:, 4 + g, tok], xbc[:, 6 + g, tok],
                                     start=True, stop=True)
                        close(ins, "cb", n)
                    else:
                        pe.wait_ge(S["s_m_ready"], n + 1)
                        pe.wait_ge(S["xdt_ready"], n + 1)
                        o = free(pe, "y_diag", n)
                        for hh in range(8):
                            c = slice(hh * 64, hh * 64 + 64)
                            ins = mm(o[:, c], s_m[:, n % 2, hh * P:(hh + 1) * P], xdt[:, n % 2, c], start=True, stop=True)
                        close(ins, "y_diag", n)
                        if n:
                            pe.wait_ge(S["s_new"], n)
                            o = free(pe, "y_off", n)
                            for g in range(2):
                                c = slice(g * 256, g * 256 + 256)
                                ins = mm(o[:, c], xbc[:, 6 + g, tok], s_state[:, n % 2, c], start=True, stop=True)
                            close(ins, "y_off", n)
                        if n < NT - 1:
                            drained(pe, "b_tok", n)
                            o = free(pe, "s_loc", n)
                            for g in range(2):
                                c = slice(g * 256, g * 256 + 256)
                                ins = mm(o[:, c], b_tok[:, n % 2, g * P:(g + 1) * P], xds[:, n % 2, c],
                                         start=True, stop=True)
                            close(ins, "s_loc", n)
                pe.wait_ge(S["y_ssm_ready"], 1)
                for f in range(4):
                    turn(("y_ssm", f), [s_y[:, n, f * P:(f + 1) * P] for n in range(NT)])
                pe.wait_ge(S["tanh_done"], 1)
                pe.wait_ge(lora_in, 48)
                for f in range(4):
                    close(mm(free(pe, "decay", f), wa2[0:64, f * P:(f + 1) * P], raw[0:64, 12, 1:], start=True, stop=True),
                          "decay", f)
                    close(mm(free(pe, "a", f), wa2[64:128, f * P:(f + 1) * P], raw[64:128, 12, 1:], start=True, stop=True),
                          "a", f)
                    pe.wait_ge(S["kk_sq"], f + 1)
                    close(mm(free(pe, "kk_sum", f), blocks, t8, start=True, stop=True), "kk_sum", f)
                pe.wait_ge(S["gd_sig"], 1)
                for n in range(NT):
                    close(mm(free(pe, "g_tok", n), raw[:, 13, 1 + n * P:1 + (n + 1) * P], g2, start=True, stop=True),
                          "g_tok", n)
                for n in range(NT):
                    turn(("rv_tok", n), [raw[:, 8 + f, 1 + n * P:1 + (n + 1) * P] for f in range(4)])
                pe.wait_ge(S["rk_ready"], 4)
                o = free(pe, "bonus")
                heads = const("heads")
                for n in range(NT):
                    for f in range(4):
                        ins = mm(o[:, n * 8 + 2 * f:n * 8 + 2 * f + 2], mats_rk[:, f, n * P:(n + 1) * P], heads,
                                 start=True, stop=True)
                close(ins, "bonus")
                pe.wait_ge(S["tilde"], 4)
                for n in range(NT):
                    tok = slice(n * P, (n + 1) * P)
                    for par in range(2):
                        r = slice(64 * par, 64 * par + 64)
                        o = free(pe, "sub", n, par)
                        for f in range(4):
                            ins = mm(o[:, f * P:(f + 1) * P], kk_s[r, f, tok], b_s[r, f, tok], start=True, stop=True)
                        close(ins, "sub", n, par)
                for n in range(NT):
                    tok = slice(n * P, (n + 1) * P)
                    rtok = slice(1 + n * P, 1 + (n + 1) * P)
                    turn(("rk_tok", n), [raw[:, 4 + f, rtok] for f in range(4)])
                    turn(("rb_tok", n), [b_s[:, f, tok] for f in range(4)])
                    for f in range(4):
                        for par in range(2):
                            r = slice(64 * par, 64 * par + 64)
                            o = free(pe, "mats", n, f, par)
                            mm(o[:, 0:P], kk_s[r, f, tok], b_s[r, f, tok], start=True, stop=True)
                            mm(o[:, P:2 * P], raw[r, 4 + f, rtok], kk_s[r, f, tok], start=True, stop=True)
                            mm(o[:, 2 * P:3 * P], raw[r, 4 + f, rtok], raw[r, f, rtok], start=True, stop=True)
                            close(mm(o[:, 3 * P:4 * P], b_s[r, f, tok], raw[r, f, rtok], start=True, stop=True),
                                  "mats", n, f, par)
                    for f in range(4):
                        for par in range(2):
                            drained(pe, "mats", n, f, par)
                    pe.wait_ge(S["inv_filled"], n + 1)
                    for level in range(LEVELS):
                        last = level == LEVELS - 1
                        for half in range(2):
                            if level:
                                drained(pe, "dt_", n, level - 1, half)
                            o = free(pe, "pt", n, level, half)
                            for j in range(4):
                                hh = 4 * half + j
                                ins = mm(o[:, j * P:(j + 1) * P], mats[:, hh, 0, :], inv_t[:, hh, :],
                                         start=True, stop=True)
                            close(ins, "pt", n, level, half)
                        for half in range(2):
                            drained(pe, "pt", n, level, half)
                            if not last:
                                o = free(pe, "d", n, level, half)
                                for j in range(4):
                                    hh = 4 * half + j
                                    ins = mm(o[:, j * P:(j + 1) * P], inv_p[:, hh, :],
                                             inv_d[:, hh, :], start=True, stop=True)
                                close(ins, "d", n, level, half)
                            o = free(pe, "dt_", n, level, half)
                            for j in range(4):
                                hh = 4 * half + j
                                ins = mm(o[:, j * P:(j + 1) * P], inv_d[:, hh, :],
                                         inv_p[:, hh, :], start=True, stop=True)
                            close(ins, "dt_", n, level, half)
                    for half in range(2):
                        drained(pe, "dt_", n, LEVELS - 1, half)
                    drained(pe, "rv_tok", n)
                    if n:
                        pe.wait_ge(S["s_rw_ready"], n)
                    o = free(pe, "rhs", n)
                    for f in range(4):
                        c = slice(f * P, (f + 1) * P)
                        if n:
                            mm(o[:, c], kk_s[:, f, tok], s_rw[:, n % 2, c], start=True, stop=True,
                               skip_group_check=True)
                        for par in range(2):
                            hh = 2 * f + par
                            c = slice(hh * 64, hh * 64 + 64)
                            ins = mm(o[:, c], mats[:, hh, 1, :], v_tok[:, n, c], start=(n == 0), stop=True,
                                     skip_group_check=True)
                    close(ins, "rhs", n)
                    drained(pe, "rhs", n)
                    o = free(pe, "u", n)
                    for hh in range(8):
                        c = slice(hh * 64, hh * 64 + 64)
                        ins = mm(o[:, c], inv_t[:, hh, :], rhs_sb[:, c], start=True, stop=True)
                    close(ins, "u", n)
                    drained(pe, "u", n)
                    o = free(pe, "y", n)
                    for f in range(4):
                        c = slice(f * P, (f + 1) * P)
                        if n:
                            mm(o[:, c], raw[:, f, rtok], s_rw[:, n % 2, c], start=True, stop=True,
                               skip_group_check=True)
                        for par in range(2):
                            hh = 2 * f + par
                            c = slice(hh * 64, hh * 64 + 64)
                            mm(o[:, c], mats[:, hh, 2, :], v_tok[:, n, c], start=(n == 0), stop=True,
                               skip_group_check=True)
                            ins = mm(o[:, c], mats[:, hh, 3, :], neg_u[:, c], start=False, stop=True,
                                     skip_group_check=True)
                    close(ins, "y", n)
                    if n < NT - 1:
                        drained(pe, "rk_tok", n)
                        drained(pe, "rb_tok", n)
                        o = free(pe, "s_rw", n)
                        for f in range(4):
                            c = slice(f * P, (f + 1) * P)
                            mm(o[:, c], k_tok[:, n % 2, c], v_tok[:, n, c], start=True, stop=False)
                            ins = mm(o[:, c], bb_tok[:, n % 2, c], neg_u[:, c], start=False, stop=True)
                        close(ins, "s_rw", n)
                pe.wait_ge(S["y_rw_ready"], NT)
                for f in range(4):
                    turn(("y_rw", f), [y_rw[:, n, f * P:(f + 1) * P] for n in range(NT)])

            pe.wait_ge(main_in, 16)
            pe.wait_ge(stack_in, 16 * N_STACK)
            for key, tile in (("stack_a", stage_a), ("stack_b", stage_b)):
                close(nc.tensor.transpose(free(pe, key)[:, 0:P], tile, ident), key)
            pe.wait_ge(x_in, 16)
            for k in range(KT):
                turn(("x", k), [x_tok_in[:, n, k * P:(k + 1) * P] for n in range(NT)])
            for layer in range(2):
                norm(2 * layer)
                (even if layer == 0 else odd)()
                project_out(layer)
                norm(2 * layer + 1)
                mlp(layer)
            norm(4)
            pe.wait_ge(normed, KT * 7)
            for t in range(NT):
                for half in range(2):
                    turn(("result", t, half), [y_mix[:, 4 * half + j, t * P:(t + 1) * P] for j in range(4)])

        @block.scalar
        def _(act):
            steps = [0]
            A = nc.scalar.activation

            def link(ins):
                steps[0] += 1
                ins.then_inc(act_step, 1)
                act.wait_ge(act_step, steps[0])

            def drain(dst, *key, src=None, scale=1.0):
                o = full(act, *key)
                A(dst, o if src is None else src, ACT.Copy, scale=scale).then_inc(free_sem(*key), 1)

            next_slot = [0]

            def high_part(n):
                A(w_hi[:, n % CUT], raw_w[:, n % RING], ACT.Copy).then_inc(w_high, 1)

            def cut_next():
                n = next_slot[0]
                if n == n_slots:
                    return
                next_slot[0] += 1
                act.wait_ge(w_full[n % RING], 16 * (n // RING + 1))
                if n >= CUT:
                    b, turn = slot_use[n - CUT]
                    act.wait_ge(bank_full[b], turn + 1)
                    act.wait_ge(w_cut, n - CUT + 1)
                high_part(n)

            def square(i, k):
                n = KT * i + k
                if k >= 2:
                    act.wait_ge(summed, n - 1)
                A(relu_t[:, k % 2, :], h[:, k, :], ACT.Square).then_inc(squared, 1)

            def norm(i):
                o = full(act, "norm", i)
                A(rms_t, o, ACT.Sqrt, scale=1.0 / D, bias=eps[:, 0:1]).then_inc(free_sem("norm", i), 1)

            def cut_normed(i):
                for k in range(KT):
                    act.wait_ge(scaled, KT * (i // 2) + k + 1)
                    A(hn_hi[:, k, :], relu_t[:, k % 2, :], ACT.Copy).then_inc(high, 1)

            def cut_mixed(turned):
                for f in range(4):
                    drained(act, turned, f)
                for k in range(KT):
                    A(hid_hi[:, k, :], y_mix[:, k, :], ACT.Copy).then_inc(high, 1)

            def project_out(layer):
                for k in range(KT):
                    cut_next()
                    drained(act, "out", layer, k)
                    square(2 * layer + 1, k)
                    A(hn_hi[:, k, :], h[:, k, :], ACT.Copy, scale=col_a("mlp_norm", 8 * layer + k)).then_inc(high, 1)

            def mlp(layer):
                def hidden(i, j):
                    b, t0 = PLAN.at["mlp", layer, j]
                    act.wait_ge(bank_free[b], i * 2 + (t0 + 1))
                    A(relu_t[:, j % 2, :], relu_t[:, j % 2, :], ACT.Square).then_inc(hid_square, 1)
                    act.wait_ge(hid_square, i * 8 + (32 * layer + j + 1))
                    A(hid_hi[:, j, :], relu_t[:, j % 2, :], ACT.Copy).then_inc(hid_high, 1)

                b0 = base["mlp", layer]
                assert next_slot[0] == b0 + CUT
                with act.Fori(0, 3) as i:
                    for s in range(16):
                        n = b0 + s + CUT
                        b, t0 = PLAN.at["mlp", layer, s % 8]
                        act.wait_ge(w_full[n % RING], i * (16 * 16 // RING) + 16 * (n // RING + 1))
                        act.wait_ge(bank_full[b], i * 2 + (t0 + s // 8 + 1))
                        act.wait_ge(w_cut, i * 16 + (n - CUT + 1))
                        high_part(n)
                        if s < 8:
                            hidden(i, s)
                next_slot[0] += 48
                for s in range(16):
                    cut_next()
                    if s < 8:
                        hidden(3, s)
                    else:
                        b, t0 = PLAN.at["mlp", layer, s - 8]
                        act.wait_ge(bank_free[b], t0 + 8)
                        square(2 * layer + 2, s - 8)

            act.wait_ge(main_in, 16)
            for key, at, n in (("stack_a", 0, A_N), ("stack_b", A_N, B_N)):
                o = full(act, key)
                A(cols_t[:, at:at + n], o[:, 0:n], ACT.Copy).then_inc(free_sem(key), 1)
            for k in range(KT):
                drain(h[:, k, :], "x", k)

            cut_next()
            cut_next()
            for k in range(KT):
                drained(act, "x", k)
                square(0, k)
            norm(0)
            cut_normed(0)

            def column_block(tile, j):
                return tile[:, :, j * P:(j + 1) * P]

            turned = 0
            f_count = 0

            def drain_feature(layer, key, buf):
                drain(f_tile[layer][:, buf, :], *key)

            for item in even_front():
                kind, u = item
                if kind == "slot":
                    key = EVEN_SLOTS[u][1]
                    if key[0] == "f":
                        drain_feature(0, key, f_count % 2)
                        f_count += 1
                    elif key[0] == "qk":
                        drain(conv_in[:, key[1], 3:], *key)
                    else:
                        drain(qk_raw[:, key[1] if key[0] == "q" else 4, :], *key)
                    cut_next()
                    if u == 7:
                        for i in range(4):
                            act.wait_ge(S["conv_ready"], i + 1)
                            A(conv_out[:, i, :], conv_out[:, i, :], ACT.Silu).then_inc(S["silu_done"], 1)
                elif kind == "turn" and u[0] == "v_att":
                    o = full(act, "v_att").rearrange("p (n g d) -> p n g d", n=NT, g=2)
                    for j in range(2):
                        for g in range(2):
                            ins = A(v_dup[:, 1:NT + 1, g, 64 * j:64 * j + 64], o[:, :, g, :], ACT.Copy)
                    ins.then_inc(free_sem("v_att"), 1)
                elif kind == "turn" and u[0] == "v":
                    drain(v_ml[:, :, u[1], 0:P], *u, src=bank(u).rearrange("p (n d) -> p n d", n=NT))
                elif kind == "turn" and u[0] == "o":
                    drain(column_block(o_gate, u[1]), *u, src=bank(u).rearrange("p (n d) -> p n d", n=NT))
                elif kind == "dup":
                    act.wait_ge(S["halo"], 3)
                    drain(k_dup[:, u, P:], "dup", u)
                elif kind == "att_exp":
                    b = u % 3
                    act.wait_ge(S["att_max"], u + 1)
                    for j in range(4):
                        A(att_p[b][:, j, :], att_p[b][:, j, :], ACT.Exp, bias=a_nm[:, b, j:j + 1],
                          accum_out=a_rs[:, b, j:j + 1])
                    A(a_es[:, b, :], a_se[:, b, :], ACT.Exp).then_inc(S["att_exp"], 1)
                elif kind == "att_turn":
                    for blk in range(2):
                        drain(att_pt[:, u % 2, blk, :], "turn", u, blk)
                elif kind == "att_out":
                    n, g = u // 2, u % 2
                    o = full(act, "att", u)
                    for par in range(2):
                        r = slice(64 * par, 64 * par + 64)
                        ins = A(y_mix[r, 2 * g:2 * g + 2, n * P:(n + 1) * P],
                                o[r, par * 256:par * 256 + 256].rearrange("p (a t) -> p a t", a=2), ACT.Copy)
                    ins.then_inc(free_sem("att", u), 1)
            act.wait_ge(S["soft_e"], 1)
            link(A(af, af, ACT.Exp, scale=-1.0))
            A(af, af, ACT.Ln, bias=1.0).then_inc(S["soft_l"], 1)
            for j in range(4):
                drained(act, "o", j)
            for a in range(2):
                drain(k_keep[:, a, :], "k_tok", a)
            act.wait_ge(S["m_ready"], 1)
            for ap in (dfa, dfb, wi_arg, em_arg, wgt_arg):
                ins = A(ap, ap, ACT.Exp)
            ins.then_inc(S["mexp"], 1)
            for n in range(NT):
                act.wait_ge(S["wl_ready"], n + 1)
                for j in range(4):
                    ins = A(w_ml[:, n, j, :], mtmp[:, n % 2, j * P:(j + 1) * P], ACT.Exp, bias=gg[:, n, j:j + 1])
                ins.then_inc(S["n_keep"], 1)
            A(o_gate, o_gate, ACT.Sigmoid).then_inc(S["o_sig"], 1)
            for n in range(NT):
                for a in range(2):
                    if n >= 2:
                        act.wait_ge(S["hm_done"], n - 1)
                    drain(n_sb[:, n % 2, a, :], "num", n, a, src=bank(("num", n, a))[:, 0:258])
            act.wait_ge(S["ln_var"], 1)
            A(mv[:, :, 1], mv[:, :, 1], ACT.Sqrt, bias=eps[:, 1:2]).then_inc(S["ln_root"], 1)
            for f in range(4):
                drain(y_mix[:, 4 + f, :], "y_ml", f)

            cut_mixed("y_ml")

            project_out(0)
            norm(1)
            mlp(0)
            norm(2)
            cut_normed(2)

            f_count = 0
            for item in odd_front():
                kind = item[0]
                if kind == "slot":
                    key = ODD_SLOTS[item[1]][1]
                    if key[0] == "f":
                        drain_feature(1, key, f_count % 2)
                        f_count += 1
                    elif key[0] == "xbc":
                        drain(xbc_in[:, key[1], 3:], *key)
                    else:
                        drain(raw[:, key[1], 1:], *key)
                    cut_next()
                    if item[1] == 10:
                        for i in range(8):
                            act.wait_ge(S["ssm_conv"], i + 1)
                            A(xbc[:, i, :], xbc[:, i, :], ACT.Silu).then_inc(S["ssm_silu"], 1)
                elif kind == "turn" and item[1][0] == "z":
                    key = item[1]
                    o = full(act, *key).rearrange("p (n d) -> p n d", n=NT)
                    A(column_block(z_tok, key[1]), o, ACT.Silu).then_inc(free_sem(*key), 1)
                    if key[1] == 2:
                        act.wait_ge(rows_in, 16 * len(ROWS))
                        A(expa, row("ssm_a_log", 8), ACT.Exp)
                        act.wait_ge(S["s_soft_e"], 1)
                        link(A(dta, dta, ACT.Exp, scale=-1.0))
                        A(dta, dta, ACT.Ln, bias=1.0).then_inc(S["s_soft_l"], 1)
                elif kind == "ssd_front":
                    n = item[1]
                    if n == 0:
                        act.wait_ge(S["acum_args"], 1)
                        A(ea, acum[:, 0, :], ACT.Exp)
                        A(dec, acum[:, 1, :], ACT.Exp)
                        A(ds_, dsx, ACT.Exp).then_inc(S["acum_exps"], 1)
                    if n >= 2:
                        act.wait_ge(S["s_yprod"], n - 1)
                        full(act, "s_loc", n - 2)
                    drain(xs_tok[:, n % 2, :], "x_tok", n)
                    drain(b_tok[:, n % 2, :], "b_tok", n, src=bank(("b_tok", n))[:, 0:256])
                    for half in range(2):
                        act.wait_ge(S["s_masked"], 2 * n + half + 1)
                        for j in range(4):
                            c = 8 * n + 4 * half + j
                            ins = A(s_w[:, half, j * P:(j + 1) * P], s_t[:, half, j * P:(j + 1) * P], ACT.Exp,
                                    bias=nacum[:, c:c + 1])
                        ins.then_inc(S["s_decay"], 1)
            for n in range(NT):
                act.wait_ge(S["z_silu"], n + 1)
                for g in range(2):
                    ins = A(xbc[:, n, g * 256:(g + 1) * 256], s_y[:, n, g * 256:(g + 1) * 256], ACT.Square,
                            accum_out=gss[:, 2 * n + g:2 * n + g + 1])
                    if n == NT - 1 and g == 1:
                        link(ins)
            A(gss, gss, ACT.Sqrt, scale=1.0 / 256, bias=eps[:, 0:1]).then_inc(S["s_root"], 1)
            for f in range(4):
                drain(y_mix[:, f, :], "y_ssm", f)
            def ln_root(n):
                act.wait_ge(S["ln2_var"], n + 1)
                A(lnv[:, n, :], lnv[:, n, :], ACT.Sqrt, scale=1.0 / 64, bias=eps[:, 2:3]).then_inc(S["ln2_root"], 1)

            act.wait_ge(S["mixed"], 1)
            A(raw[0:64, 12, 1:], raw[0:64, 12, 1:], ACT.Tanh).then_inc(S["tanh_done"], 1)
            A(raw[:, 13, 1:], raw[:, 13, 1:], ACT.Sigmoid).then_inc(S["gd_sig"], 1)
            for f in range(4):
                if f:
                    act.wait_ge(S["tilde"], f)
                o = full(act, "decay", f)
                A(t1, o, ACT.Sigmoid, bias=col_b("rw_w0", f)).then_inc(free_sem("decay", f), 1)
                o = full(act, "a", f)
                A(t2, o, ACT.Sigmoid, bias=col_b("rw_a0", f)).then_inc(free_sem("a", f), 1)
                act.wait_ge(S["kkraw"], f + 1)
                A(t8, t7, ACT.Square).then_inc(S["kk_sq"], 1)
                o = full(act, "kk_sum", f)
                A(t6, o, ACT.Sqrt).then_inc(free_sem("kk_sum", f), 1)
                act.wait_ge(S["cum_args"], f + 1)
                A(t5, t3, ACT.Exp, scale=-DECAY_K)
                A(t4, t4, ACT.Exp, scale=-DECAY_K)
                A(t3, t3, ACT.Exp, scale=DECAY_K).then_inc(S["cum_exps"], 1)
            A(e_s, e_a, ACT.Exp, scale=-DECAY_K).then_inc(S["scales"], 1)
            for n in range(NT):
                drain(g_tok[:, n, :], "g_tok", n)
            for n in range(NT):
                drain(v_tok[:, n, :], "rv_tok", n)
            for n in range(NT):
                o = full(act, "sub", n, 0).rearrange("p (f s) -> p f s", f=4)
                for q in range(P // SUB):
                    rows = slice(q * SUB, (q + 1) * SUB)
                    ins = A(sub_tok[rows, :, n * 8:n * 8 + 8:2].rearrange("p s f -> p f s"), o[rows, :, rows], ACT.Copy,
                            scale=-1.0)
                ins.then_inc(free_sem("sub", n, 0), 1)
            for n in range(NT):
                if n >= 2:
                    full(act, "s_rw", n - 2)
                drain(k_tok[:, n % 2, :], "rk_tok", n)
                drain(bb_tok[:, n % 2, :], "rb_tok", n)
                act.wait_ge(S["inv_zero"], n + 1)
                for src, dst in ((inv_rows, inv_d), (inv_cols, inv_t)):
                    for q in range(P // SUB):
                        rows = slice(q * SUB, (q + 1) * SUB)
                        ins = A(dst[rows, :, rows], src[rows, :, n * 8:n * 8 + 8].rearrange("p c j -> p j c"), ACT.Copy)
                ins.then_inc(S["inv_filled"], 1)
                drain(rhs_sb, "rhs", n)
                if n:
                    full(act, "s_rw", n - 1)
                drain(neg_u, "u", n, scale=-1.0)
                drain(y_rw[:, n, :], "y", n)
                if n:
                    ln_root(n - 1)
            ln_root(NT - 1)
            for f in range(4):
                drain(y_mix[:, 4 + f, :], "y_rw", f)
            cut_mixed("y_rw")
            project_out(1)
            norm(3)
            mlp(1)
            norm(4)
            for t in range(NT):
                for half in range(2):
                    o = full(act, "result", t, half)
                    A(arena[:, t * D + half * 512:t * D + half * 512 + 512], o, ACT.Copy).then_inc(S["x_out"], 1)

        @block.vector
        def _(dve):
            steps = [0]
            V = nc.vector

            def link(ins):
                steps[0] += 1
                ins.then_inc(dve_step, 1)
                dve.wait_ge(dve_step, steps[0])

            def sum_squares(i, k):
                n = KT * i + k
                dve.wait_ge(squared, n + 1)
                if k:
                    dve.wait_ge(summed, n)
                    V.tensor_tensor(rms_t, rms_t, relu_t[:, k % 2, :], ALU.add).then_inc(summed, 1)
                else:
                    V.tensor_copy(rms_t, relu_t[:, k % 2, :]).then_inc(summed, 1)

            def norm(i):
                gains = {0: ("mix_norm", 0), 1: ("mlp_norm", 0), 2: ("mix_norm", 8), 3: ("mlp_norm", 8),
                         4: ("final_norm", 0)}[i]
                drained(dve, "norm", i)
                link(V.reciprocal(rms_t, rms_t))
                if i in (1, 3):
                    return
                for k in range(KT):
                    if i < 4 and k >= 2:
                        low(i, k - 2)
                    dst = relu_t[:, k % 2, :] if i < 4 else y_mix[:, k, :]
                    V.scalar_tensor_tensor(out=dst, in0=h[:, k, :], scalar=col_a(gains[0], gains[1] + k),
                                           in1=rms_t, op0=ALU.mult, op1=ALU.mult
                                           ).then_inc(scaled if i < 4 else normed, 1)
                if i < 4:
                    low(i, KT - 2)
                    low(i, KT - 1)

            def low(i, k):
                phase = [0, 2, 3, 5][i]
                dve.wait_ge(high, KT * phase + k + 1)
                V.tensor_tensor(hn_lo[:, k, :], relu_t[:, k % 2, :], hn_hi[:, k, :].bitcast(F32), ALU.subtract
                                ).then_inc(normed, 1)
                dve.wait_ge(normed, KT * phase + k + 1)

            def low_mixed(layer):
                for k in range(KT):
                    dve.wait_ge(high, KT * (3 * layer + 1) + k + 1)
                    V.tensor_tensor(hid_lo[:, k, :], y_mix[:, k, :], hid_hi[:, k, :].bitcast(F32), ALU.subtract
                                    ).then_inc(normed, 1)

            def project_out(layer):
                def low_gained(k):
                    dve.wait_ge(high, KT * (3 * layer + 2) + k + 1)
                    V.scalar_tensor_tensor(out=hn_lo[:, k, :], in0=h[:, k, :], scalar=col_a("mlp_norm", 8 * layer + k),
                                           in1=hn_hi[:, k, :].bitcast(F32), op0=ALU.mult, op1=ALU.subtract
                                           ).then_inc(normed, 1)

                low_mixed(layer)
                for k in range(KT):
                    o = full(dve, "out", layer, k)
                    V.tensor_tensor(h[:, k, :], h[:, k, :], o, ALU.add).then_inc(free_sem("out", layer, k), 1)
                    if k:
                        sum_squares(2 * layer + 1, k - 1)
                        low_gained(k - 1)
                sum_squares(2 * layer + 1, KT - 1)
                low_gained(KT - 1)

            def mlp(layer):
                def hidden(i):
                    for j in range(8):
                        b, t0 = PLAN.at["mlp", layer, j]
                        dve.wait_ge(bank_full[b], i * 2 + (t0 + 1))
                        V.scalar_tensor_tensor(out=relu_t[:, j % 2, :], in0=ps[:, b, :], scalar=0.0, in1=rms_t,
                                               op0=ALU.max, op1=ALU.mult).then_inc(bank_free[b], 1)
                        dve.wait_ge(hid_high, i * 8 + (32 * layer + j + 1))
                        V.tensor_tensor(hid_lo[:, j, :], relu_t[:, j % 2, :], hid_hi[:, j, :].bitcast(F32), ALU.subtract
                                        ).then_inc(hid_ready, 1)
                        dve.wait_ge(hid_ready, i * 8 + (32 * layer + j + 1))

                def add(i, j):
                    b, t0 = PLAN.at["mlp", layer, j]
                    dve.wait_ge(bank_full[b], i * 2 + (t0 + 2))
                    V.tensor_tensor(h[:, j, :], h[:, j, :], ps[:, b, :], ALU.add).then_inc(bank_free[b], 1)

                dve.wait_ge(summed, KT * (2 * layer + 2))
                with dve.Fori(0, 3) as i:
                    hidden(i)
                    for j in range(8):
                        add(i, j)
                hidden(3)
                for j in range(8):
                    add(3, j)
                    if j:
                        sum_squares(2 * layer + 2, j - 1)
                sum_squares(2 * layer + 2, KT - 1)

            def conv(dst, src, w, b, i, tiles, signal):
                link(V.tensor_scalar(dst, src[:, 0:T], col_a(w, i), col_a(b, i), ALU.mult, ALU.add))
                for tap in range(1, 4):
                    ins = V.scalar_tensor_tensor(out=dst, in0=src[:, tap:tap + T], scalar=col_a(w, tap * tiles + i),
                                                 in1=dst, op0=ALU.mult, op1=ALU.add)
                    if tap < 3:
                        link(ins)
                    else:
                        ins.then_inc(signal, 1)

            drained(dve, "stack_a")
            drained(dve, "stack_b")
            drained(dve, "x", KT - 1)
            for k in range(KT):
                sum_squares(0, k)
            norm(0)
            V.memset(k_dup[:, :, 0:P], 0.0).then_inc(S["halo"], 1)
            V.memset(v_dup[:, 0, :, :], 0.0).then_inc(S["halo"], 1)
            V.memset(conv_in[:, :, 0:3], 0.0).then_inc(S["halo"], 1)
            V.memset(v_ml[:, :, :, 128:129], 1.0).then_inc(S["v_ones"], 1)
            dve.wait_ge(rows_in, 16 * len(ROWS))
            g_ps = full(dve, "gates").rearrange("p (n c) -> p n c", n=NT)[:, :, P - 8:]
            link(V.tensor_tensor(li, g_ps[:, :, 0:4], over(row("ml_i_bias", 4), 1, NT), ALU.add))
            V.tensor_tensor(fg, g_ps[:, :, 4:8], over(row("ml_f_bias", 4), 1, NT), ALU.add).then_inc(free_sem("gates"), 1)
            drained(dve, "gates")
            V.scalar_tensor_tensor(out=af, in0=fg, scalar=-1.0, in1=fg, op0=ALU.mult, op1=ALU.max
                                   ).then_inc(S["soft_e"], 1)
            dve.wait_ge(S["halo"], 3)
            for i in range(4):
                drained(dve, "qk", i)
                conv(conv_out[:, i, :], conv_in[:, i, :], "ml_conv_w", "ml_conv_b", i, 4, S["conv_ready"])
            dve.wait_ge(even_in, 16)
            cos, sin = even_const("cos"), even_const("sin")
            for i in (4, 0, 1, 2, 3):
                dst = q_rot[:, i, :] if i < 4 else k_rot
                drained(dve, *(("q", i) if i < 4 else ("k",)))
                o = full(dve, "rope", i)
                V.tensor_tensor(relu_t[:, i % 2, :], o, sin, ALU.mult).then_inc(free_sem("rope", i), 1)
                link(V.tensor_tensor(dst, qk_raw[:, i, :], cos, ALU.mult))
                drained(dve, "rope", i)
                V.tensor_tensor(dst, dst, relu_t[:, i % 2, :], ALU.add).then_inc(S["rope_done"], 1)
            sinks = row("att_sinks", 8)
            band, first = even_const("band"), even_const("first")

            def att_scores(u):
                n, g = u // 2, u % 2
                b = u % 3
                if u == 2:
                    dve.wait_ge(S["rope_done"], 5)
                if u >= 3:
                    full(dve, "turn", u - 3, 0)
                    full(dve, "turn", u - 3, 1)
                for par in range(2):
                    o = full(dve, "score", u, par).rearrange("p (a k) -> p a k", a=2)
                    V.scalar_tensor_tensor(out=att_p[b][:, 2 * par:2 * par + 2, :], in0=o, scalar=0.125,
                                           in1=over(band if n else first, 1, 2), op0=ALU.mult, op1=ALU.add
                                           ).then_inc(free_sem("score", u, par), 1)
                drained(dve, "score", u, 0)
                drained(dve, "score", u, 1)
                sk = sinks[:, 4 * g:4 * g + 4].rearrange("p (a par) -> p par a", par=2)
                v2 = lambda ap: ap.rearrange("p (par a) -> p par a", par=2)
                link(V.tensor_reduce(a_mx[:, b, :], att_p[b], AX.X, ALU.max))
                link(V.tensor_tensor(v2(a_mx[:, b, :]), v2(a_mx[:, b, :]), sk, ALU.max))
                link(V.tensor_scalar(a_nm[:, b, :], a_mx[:, b, :], -1.0, None, ALU.mult))
                V.tensor_tensor(v2(a_se[:, b, :]), v2(a_nm[:, b, :]), sk, ALU.add).then_inc(S["att_max"], 1)

            def att_norm(u):
                b = u % 3
                dve.wait_ge(S["att_exp"], u + 1)
                link(V.tensor_tensor(a_l[:, b, :], a_rs[:, b, :], a_es[:, b, :], ALU.add))
                link(V.reciprocal(a_l[:, b, :], a_l[:, b, :]))
                V.tensor_tensor(att_p[b], att_p[b], over(a_l[:, b, :], 2, 256), ALU.mult
                                ).then_inc(S["att_probs"], 1)

            for u in range(9):
                if u < 8:
                    att_scores(u)
                if u:
                    att_norm(u - 1)
            dve.wait_ge(S["soft_l"], 1)
            V.scalar_tensor_tensor(out=lf, in0=fg, scalar=0.0, in1=af, op0=ALU.min, op1=ALU.subtract
                                   ).then_inc(S["lf_ready"], 1)
            o = full(dve, "cum")
            V.tensor_copy(cumb, o[:, 0:32].rearrange("p (a b) -> p a b", a=2)).then_inc(free_sem("cum"), 1)
            drained(dve, "cum")
            b_ = cumb[:, 0, :].rearrange("p (n c) -> p n c", n=NT)
            bl = cumb[:, 1, :].rearrange("p (n c) -> p n c", n=NT)
            link(V.tensor_tensor(gg, li, b_, ALU.subtract))

            def diag(dst, col, signal):
                V.tensor_tensor(dst.rearrange("p (a t) -> p a t", a=4), over(ident, 1, 4), over(col, 2, P), ALU.mult
                                ).then_inc(signal, 1)

            full(dve, "att", 7)
            for n in range(2):
                diag(dg[:, n % 2, :], gg[:, n, :], S["g_diag"])
            for n in range(NT):
                o = full(dve, "g_row", n).rearrange("p (a t) -> p a t", a=4)
                link(V.tensor_reduce(gmax[:, n, :], o, AX.X, ALU.max))
                V.tensor_tensor(mtmp[:, n % 2, :].rearrange("p (a t) -> p a t", a=4), o, over(const("add_ts"), 1, 4),
                                ALU.add).then_inc(free_sem("g_row", n), 1)
                drained(dve, "g_row", n)
                link(V.tensor_reduce(cmx[:, n, :], mtmp[:, n % 2, :].rearrange("p (a t) -> p a t", a=4), AX.X, ALU.max))
                if n + 2 < NT:
                    diag(dg[:, n % 2, :], gg[:, n + 2, :], S["g_diag"])
            link(V.memset(marr[:, 0, :], 0.0))
            for n in range(NT):
                link(V.tensor_tensor(mx[:, n, :], marr[:, n, :], gmax[:, n, :], ALU.max))
                if n < NT - 1:
                    link(V.tensor_tensor(marr[:, n + 1, :], bl[:, n, :], mx[:, n, :], ALU.add))
            mm_ = mm
            link(V.tensor_tensor(mm_, marr, cmx, ALU.max))
            V.tensor_tensor(dfa, marr, mx, ALU.subtract)
            V.tensor_tensor(dfb, gmax, mx, ALU.subtract)
            V.tensor_tensor(wi_arg, marr, mm_, ALU.subtract)
            V.tensor_tensor(wgt_arg, gg, gmax, ALU.subtract)
            link(V.tensor_tensor(em_arg, b_, mm_, ALU.add))
            V.tensor_scalar(em_arg, em_arg, -1.0, None, ALU.mult).then_inc(S["m_ready"], 1)
            for n in range(2):
                diag(dg[:, n % 2, :], mm_[:, n, :], S["m_diag"])
            for n in range(NT):
                o = full(dve, "m_row", n).rearrange("p (a t) -> p a t", a=4)
                if n >= 2:
                    dve.wait_ge(S["n_keep"], n - 1)
                V.tensor_tensor(mtmp[:, n % 2, :].rearrange("p (a t) -> p a t", a=4), over(const("add_st"), 1, 4), o,
                                ALU.subtract).then_inc(free_sem("m_row", n), 1)
                drained(dve, "m_row", n)
                dve.sem_inc(S["wl_ready"], 1)
                if n + 2 < NT:
                    diag(dg[:, n % 2, :], mm_[:, n + 2, :], S["m_diag"])
            dve.wait_ge(S["mexp"], 1)
            for a in range(2):
                drained(dve, "k_tok", a)
            kk4 = k_keep.rearrange("p a (n f) -> p n a f", n=NT)
            for n in range(NT):
                for a in range(2):
                    ins = V.scalar_tensor_tensor(
                        out=k_w[:, n, a * P:(a + 1) * P].rearrange("p (b d) -> p b d", b=2),
                        in0=kk4[:, n, a, :].rearrange("p (b d) -> p b d", b=2), scalar=0.125,
                        in1=over(wgt_arg[:, n, 2 * a:2 * a + 2], 2, 64), op0=ALU.mult, op1=ALU.mult)
                    if a == 0:
                        link(ins)
                    else:
                        ins.then_inc(S["k_scaled"], 1)
            for n in range(NT):
                dve.wait_ge(S["n_keep"], n + 1)
                for par in range(2):
                    o = full(dve, "qk_st", n, par)[:, 0:256].rearrange("p (a t) -> p a t", a=2)
                    wv = w_ml[:, n].rearrange("p (a b) t -> p b a t", b=2)[:, par]
                    qv = qkw[:, n % 2, :].rearrange("p (a b t) -> p b a t", a=2, b=2)[:, par]
                    if n >= 2 and par == 0:
                        full(dve, "num", n - 2, 1)
                    V.scalar_tensor_tensor(out=qv, in0=o, scalar=0.125, in1=wv, op0=ALU.mult, op1=ALU.mult
                                           ).then_inc(free_sem("qk_st", n, par), 1)
                drained(dve, "qk_st", n, 0)
                drained(dve, "qk_st", n, 1)
                dve.sem_inc(S["qkw_ready"], 1)
                if n < NT - 1:
                    for a in range(2):
                        o = full(dve, "c_loc", n, a)[:, 0:258].rearrange("p (b v) -> p b v", b=2)
                        for par in range(2):
                            r = slice(64 * par, 64 * par + 64)
                            hh = 2 * a + par
                            dst = c_state[r, n + 1, a, :]
                            if n:
                                link(V.tensor_scalar(c_tmp[r, a, :], c_state[r, n, a, :], dfa[r, n, hh:hh + 1], None,
                                                     ALU.mult))
                                ins = V.scalar_tensor_tensor(out=dst, in0=o[r, par, :], scalar=dfb[r, n, hh:hh + 1],
                                                             in1=c_tmp[r, a, :], op0=ALU.mult, op1=ALU.add)
                            else:
                                ins = V.tensor_scalar(dst, o[r, par, :], dfb[r, n, hh:hh + 1], None, ALU.mult)
                            if par:
                                ins.then_inc(free_sem("c_loc", n, a), 1)
                            else:
                                link(ins)
                    drained(dve, "c_loc", n, 0)
                    drained(dve, "c_loc", n, 1)
                    dve.sem_inc(S["c_ready"], 1)
                drained(dve, "num", n, 0)
                drained(dve, "num", n, 1)
                nn = n_sb[:, n % 2].rearrange("p a (b v) -> p a b v", b=2)
                if n:
                    for par in range(2):
                        o = full(dve, "inter", n, par)[:, 0:258].rearrange("p (a v) -> p a v", a=2)
                        for a in range(2):
                            hh = 2 * a + par
                            ins = V.scalar_tensor_tensor(out=nn[:, a, par, :], in0=o[:, a, :],
                                                         scalar=wi_arg[:, n, hh:hh + 1], in1=nn[:, a, par, :],
                                                         op0=ALU.mult, op1=ALU.add)
                            if a:
                                ins.then_inc(free_sem("inter", n, par), 1)
                    drained(dve, "inter", n, 0)
                    drained(dve, "inter", n, 1)
                den = nn[:, :, :, 128:129].rearrange("p a b v -> p a (b v)")
                d2 = dn[:, n % 2, :].rearrange("p (a b) -> p a b", a=2)
                em = em_arg[:, n, :].rearrange("p (a b) -> p a b", a=2)
                link(V.tensor_scalar(d2, den, -1.0, None, ALU.mult))
                link(V.tensor_tensor(d2, d2, den, ALU.max))
                link(V.tensor_tensor(d2, d2, em, ALU.max))
                link(V.reciprocal(dn[:, n % 2, :], dn[:, n % 2, :]))
                for hh in range(4):
                    link(V.tensor_scalar(w_ml[:, n, hh, :], nn[:, hh // 2, hh % 2, 0:P], dn[:, n % 2, hh:hh + 1], None,
                                         ALU.mult))
                    link(V.bn_stats(st6, w_ml[:, n, hh, :]))
                    ins = V.bn_aggr(mv[:, 4 * n + hh, :], st6)
                    if hh < 3:
                        link(ins)
                    else:
                        ins.then_inc(S["hm_done"], 1)
                        dve.wait_ge(S["hm_done"], n + 1)
            dve.sem_inc(S["ln_var"], 1)
            dve.wait_ge(S["o_sig"], 1)
            link(V.tensor_tensor(o_gate, o_gate, over(row("ml_norm", 512), 1, NT), ALU.mult))
            dve.wait_ge(S["ln_root"], 1)
            link(V.reciprocal(mv[:, :, 1], mv[:, :, 1]))
            for n in range(NT):
                for hh in range(4):
                    j = 4 * n + hh
                    link(V.tensor_scalar(w_ml[:, n, hh, :], w_ml[:, n, hh, :], mv[:, j, 0:1], mv[:, j, 1:2],
                                         ALU.subtract, ALU.mult))
            V.tensor_tensor(o_gate, o_gate, w_ml.rearrange("p n h t -> p n (h t)"), ALU.mult
                            ).then_inc(S["y_ml_ready"], 1)
            project_out(0)
            norm(1)
            mlp(0)
            norm(2)

            V.memset(xbc_in[:, :, 0:3], 0.0).then_inc(S["halo"], 1)
            V.memset(raw[:, :, 0:1], 0.0).then_inc(S["halo"], 1)
            d_ps = full(dve, "dt").rearrange("p (n c) -> p n c", n=NT)[:, :, 0:8]
            V.tensor_tensor(dtr, d_ps, over(row("ssm_dt_bias", 8), 1, NT), ALU.add).then_inc(free_sem("dt"), 1)
            drained(dve, "dt")
            V.scalar_tensor_tensor(out=dta, in0=dtr, scalar=-1.0, in1=dtr, op0=ALU.mult, op1=ALU.max
                                   ).then_inc(S["s_soft_e"], 1)
            dve.wait_ge(S["halo"], 5)
            for i in range(8):
                drained(dve, "xbc", i)
                conv(xbc[:, i, :], xbc_in[:, i, :], "ssm_conv_w", "ssm_conv_b", i, 8, S["ssm_conv"])
            dve.wait_ge(S["s_soft_l"], 1)
            link(V.scalar_tensor_tensor(out=dtt, in0=dtr, scalar=0.0, in1=dta, op0=ALU.max, op1=ALU.add))
            V.scalar_tensor_tensor(out=dA, in0=dtt, scalar=-1.0, in1=over(expa, 1, NT), op0=ALU.mult, op1=ALU.mult
                                   ).then_inc(S["da_ready"], 1)
            o = full(dve, "a_cum")
            V.tensor_copy(acum, o[:, 0:64].rearrange("p (a b) -> p a b", a=2)).then_inc(free_sem("a_cum"), 1)
            drained(dve, "a_cum")
            link(V.tensor_tensor(dsx, acum[:, 1, :], acum[:, 0, :], ALU.subtract))
            V.tensor_scalar(nacum, acum[:, 0, :], -1.0, None, ALU.mult).then_inc(S["acum_args"], 1)
            dve.wait_ge(S["acum_exps"], 1)
            a4 = acum[:, 0, :].rearrange("p (n b c) -> p n b c", n=NT, b=2)
            h8 = lambda ap: ap.rearrange("p (c d) -> p c d", d=64)

            def ssd_front(n):
                b = n % 2
                for half in range(2):
                    diag(s_dg[:, half, :], a4[:, n, half, :], S["s_diag"])
                for half in range(2):
                    o = full(dve, "a_row", n, half).rearrange("p (a t) -> p a t", a=4)
                    V.tensor_tensor(s_t[:, half, :].rearrange("p (a t) -> p a t", a=4), o, over(const("add_st"), 1, 4),
                                    ALU.add).then_inc(free_sem("a_row", n, half), 1)
                    drained(dve, "a_row", n, half)
                    dve.sem_inc(S["s_masked"], 1)
                drained(dve, "x_tok", n)
                dt_n = dtt[:, n, :]
                if n >= 2:
                    full(dve, "y_diag", n - 2)
                    full(dve, "s_loc", n - 2)
                link(V.tensor_tensor(h8(xdt[:, b, :]), h8(xs_tok[:, b, :]), over(dt_n, 2, 64), ALU.mult))
                V.tensor_tensor(h8(xds[:, b, :]), h8(xdt[:, b, :]), over(ds_[:, 8 * n:8 * n + 8], 2, 64), ALU.mult
                                ).then_inc(S["xdt_ready"], 1)
                o = full(dve, "cb", n)[:, 0:256].rearrange("p (g t) -> p g t", g=2)
                for half in range(2):
                    dve.wait_ge(S["s_decay"], 2 * n + half + 1)
                    ins = V.tensor_tensor(s_m[:, b, half * 512:(half + 1) * 512].rearrange("p (a t) -> p a t", a=4),
                                          s_w[:, half, :].rearrange("p (a t) -> p a t", a=4), over(o[:, half, :], 1, 4),
                                          ALU.mult)
                    if half == 0:
                        link(ins)
                    else:
                        ins.then_inc(free_sem("cb", n), 1)
                drained(dve, "cb", n)
                dve.sem_inc(S["s_m_ready"], 1)

            def shift(i, last=False):
                drained(dve, "rw", i)
                link(V.tensor_tensor(relu_t[:, 1, :], raw[:, i, 0:T], raw[:, i, 1:], ALU.subtract))
                ins = V.scalar_tensor_tensor(out=raw[:, i, 1:], in0=relu_t[:, 1, :], scalar=col_b("rw_mu", i),
                                             in1=raw[:, i, 1:], op0=ALU.mult, op1=ALU.add)
                if last:
                    ins.then_inc(S["mixed"], 1)
                else:
                    link(ins)

            def ssd_back(n):
                b = n % 2
                y = s_y[:, n, :]
                link(V.tensor_tensor(h8(y), h8(xs_tok[:, b, :]), over(row("ssm_d", 8), 2, 64), ALU.mult))
                o = full(dve, "y_diag", n)
                V.tensor_tensor(y, y, o, ALU.add).then_inc(free_sem("y_diag", n), 1)
                drained(dve, "y_diag", n)
                if n:
                    o = full(dve, "y_off", n)
                    V.tensor_tensor(h8(relu_t[:, 0, :]), h8(o), over(ea[:, 8 * n:8 * n + 8], 2, 64), ALU.mult
                                    ).then_inc(free_sem("y_off", n), 1)
                    drained(dve, "y_off", n)
                    link(V.tensor_tensor(y, y, relu_t[:, 0, :], ALU.add))
                if n == 0:
                    for j in range(4):
                        drained(dve, "z", j)
                V.tensor_tensor(y, y, z_tok[:, n, :], ALU.mult).then_inc(S["z_silu"], 1)
                dve.wait_ge(S["z_silu"], n + 1)
                dve.sem_inc(S["s_yprod"], 1)
                if n < NT - 1:
                    o = full(dve, "s_loc", n)
                    nxt = s_state[:, (n + 1) % 2, :]
                    if n:
                        link(V.tensor_tensor(h8(nxt), h8(s_state[:, b, :]), over(dec[:, 8 * n:8 * n + 8], 2, 64), ALU.mult))
                        V.tensor_tensor(nxt, nxt, o, ALU.add).then_inc(free_sem("s_loc", n), 1)
                    else:
                        V.tensor_copy(nxt, o).then_inc(free_sem("s_loc", n), 1)
                    drained(dve, "s_loc", n)
                    dve.sem_inc(S["s_new"], 1)
            for item in odd_front():
                if item[0] == "ssd_front":
                    ssd_front(item[1])
                elif item[0] == "ssd_back":
                    ssd_back(item[1])
                elif item[0] == "slot" and item[1] >= 14:
                    shift(ODD_SLOTS[item[1] - 1][1][1])
            shift(ODD_SLOTS[-1][1][1], last=True)
            dve.wait_ge(S["s_root"], 1)
            link(V.reciprocal(gss, gss))
            for n in range(NT):
                for g in range(2):
                    c = slice(g * 256, g * 256 + 256)
                    ins = V.scalar_tensor_tensor(out=s_y[:, n, c], in0=s_y[:, n, c], scalar=gss[:, 2 * n + g:2 * n + g + 1],
                                                 in1=row("ssm_norm", 512)[:, c], op0=ALU.mult, op1=ALU.mult)
                    if (n, g) == (NT - 1, 1):
                        ins.then_inc(S["y_ssm_ready"], 1)
                    else:
                        link(ins)
            for f in range(4):
                drained(dve, "y_ssm", f)
            link(V.tensor_scalar(omka, cols_t[:, A_N + B_AT["rw_k_a"]:A_N + B_AT["rw_k_a"] + 4], -1.0, 1.0,
                                 ALU.mult, ALU.add))
            for f in range(4):
                r_, k_ = raw[:, f, 1:], raw[:, 4 + f, 1:]
                if f:
                    dve.wait_ge(S["kk_sq"], f)
                V.tensor_scalar(t7, k_, col_b("rw_k_k", f), None, ALU.mult).then_inc(S["kkraw"], 1)
                drained(dve, "decay", f)
                link(V.tensor_tensor_scan(t3, const("reset"), t1, 0.0, ALU.mult, ALU.add))
                t3c = t3.rearrange("p (n t) -> p n t", n=NT)
                mid = t3[:, P // 2 - 1::P]
                end = t3[:, P - 1::P]
                link(V.tensor_tensor(e_a[:, f, :], end, mid, ALU.subtract))
                link(V.tensor_tensor(e_a[:, f, 0:NT - 1], e_a[:, f, 0:NT - 1], mid[:, 1:NT], ALU.add))
                link(V.tensor_copy(lnm[:, f, 0:NT], mid))
                link(V.tensor_tensor(t3c, t3c, over(lnm[:, f, 0:NT], 2, P), ALU.subtract))
                V.tensor_tensor(t4, t3, t1, ALU.subtract).then_inc(S["cum_args"], 1)
                drained(dve, "kk_sum", f)
                link(V.tensor_scalar(t6, t6, 1e-12, None, ALU.max))
                link(V.reciprocal(t6, t6))
                link(V.tensor_tensor(t7, t7, t6, ALU.mult))
                drained(dve, "a", f)
                link(V.tensor_scalar(t6, t2, col_b("rw_k_a", f), omka[:, f:f + 1], ALU.mult, ALU.add))
                link(V.tensor_tensor(k_, k_, t6, ALU.mult))
                V.scalar_tensor_tensor(out=mats_rk[:, f, :], in0=r_, scalar=col_b("rw_r_k", f), in1=k_, op0=ALU.mult,
                                       op1=ALU.mult).then_inc(S["rk_ready"], 1)
                link(V.tensor_tensor(t2, t2, t7, ALU.mult))
                dve.wait_ge(S["cum_exps"], f + 1)
                dve.wait_ge(S["rk_ready"], f + 1)
                link(V.tensor_tensor(b_s[:, f, :], t2, t3, ALU.mult))
                link(V.tensor_tensor(k_, k_, t3, ALU.mult))
                link(V.tensor_tensor(kk_s[:, f, :], t7, t4, ALU.mult))
                V.tensor_tensor(r_, r_, t5, ALU.mult).then_inc(S["tilde"], 1)
            dve.wait_ge(S["tilde"], 4)
            o = full(dve, "bonus")
            V.tensor_copy(bon, o[:, 0:32].rearrange("p (n c) -> p n c", n=NT)).then_inc(free_sem("bonus"), 1)
            dve.wait_ge(S["scales"], 1)
            for n in range(NT):
                o = full(dve, "sub", n, 1).rearrange("p (f s) -> p f s", f=4)
                for q in range(P // SUB):
                    rows = slice(q * SUB, (q + 1) * SUB)
                    ins = V.tensor_scalar(sub_tok[rows, :, n * 8 + 1:n * 8 + 8:2].rearrange("p s f -> p f s"),
                                          o[rows, :, rows], -1.0, None, ALU.mult)
                ins.then_inc(free_sem("sub", n, 1), 1)
            V.memset(sub_inv, 0.0)
            for n in range(NT):
                for par in range(2):
                    drained(dve, "sub", n, par)
            link(V.transpose(sub_prob, sub_tok))
            diagonal = sub_inv.rearrange("p t c -> p (t c)")[:, ::SUB + 1]
            link(V.tensor_copy(diagonal, ones[:, 0:SUB]))
            for s_ in range(SUB - 1):
                rest, width = SUB - 1 - s_, s_ + 1
                tmp = sub_tmp[:, 0:rest * width].rearrange("p (t c) -> p t c", c=width)
                link(V.tensor_tensor(tmp, over(sub_prob[:, s_, s_ + 1:SUB], 2, width),
                                     over(sub_inv[:, s_, 0:width], 1, rest), ALU.mult))
                below = sub_inv[:, s_ + 1:SUB, 0:width]
                link(V.tensor_tensor(below, below, tmp, ALU.add))
            for n in range(NT):
                full(dve, "rv_tok", n)
            V.transpose(inv_rows, sub_inv.rearrange("p t c -> p c t"))
            link(V.transpose(inv_cols, sub_inv))

            def zero_inverses(n):
                if n:
                    full(dve, "u", n - 1)
                V.memset(inv_d, 0.0)
                V.memset(inv_t, 0.0).then_inc(S["inv_zero"], 1)

            def ln_stats(n):
                drained(dve, "y", n)
                y8 = h8(y_rw[:, n, :])
                link(V.tensor_reduce(lnm[:, n, :], y8, AX.X, ALU.add))
                link(V.tensor_scalar(lnm[:, n, :], lnm[:, n, :], 1.0 / 64, None, ALU.mult))
                link(V.tensor_tensor(y8, y8, over(lnm[:, n, :], 2, 64), ALU.subtract))
                link(V.tensor_tensor(t1, y_rw[:, n, :], y_rw[:, n, :], ALU.mult))
                V.tensor_reduce(lnv[:, n, :], h8(t1), AX.X, ALU.add).then_inc(S["ln2_var"], 1)

            def ln_out(n):
                dve.wait_ge(S["ln2_root"], n + 1)
                link(V.reciprocal(lnv[:, n, :], lnv[:, n, :]))
                drained(dve, "g_tok", n)
                drained(dve, "rv_tok", n)
                y = y_rw[:, n, :]
                link(V.tensor_tensor(h8(y), h8(y), over(lnv[:, n, :], 2, 64), ALU.mult))
                link(V.tensor_tensor(y, y, row("rw_ln_w", 512), ALU.mult))
                link(V.tensor_tensor(y, y, row("rw_ln_b", 512), ALU.add))
                link(V.tensor_tensor(h8(t1), h8(v_tok[:, n, :]), over(bon[:, n, :], 2, 64), ALU.mult))
                link(V.tensor_tensor(y, y, t1, ALU.add))
                V.tensor_tensor(y, y, g_tok[:, n, :], ALU.mult).then_inc(S["y_rw_ready"], 1)

            zero_inverses(0)
            lv = const("levels")
            for n in range(NT):
                for f in range(4):
                    for par in range(2):
                        o = full(dve, "mats", n, f, par)
                        V.scalar_tensor_tensor(out=mats[:, 2 * f + par].rearrange("p a b -> p (a b)"), in0=o, scalar=HUGE,
                                               in1=const("four"), op0=ALU.min, op1=ALU.mult
                                               ).then_inc(free_sem("mats", n, f, par), 1)
                for level in range(LEVELS):
                    mask = over(lv[:, level * P:(level + 1) * P], 1, 4)
                    for half in range(2):
                        hs = slice(4 * half, 4 * half + 4)
                        o = full(dve, "pt", n, level, half).rearrange("p (a t) -> p a t", a=4)
                        V.tensor_tensor(inv_p[:, hs, :], o, mask, ALU.mult).then_inc(free_sem("pt", n, level, half), 1)
                    for half in range(2):
                        hs = slice(4 * half, 4 * half + 4)
                        if level < LEVELS - 1:
                            o = full(dve, "d", n, level, half).rearrange("p (a t) -> p a t", a=4)
                            full(dve, "dt_", n, level, half)
                            if level:
                                drained(dve, "d", n, level - 1, half)
                            V.tensor_tensor(inv_d[:, hs, :], inv_d[:, hs, :], o, ALU.subtract
                                            ).then_inc(free_sem("d", n, level, half), 1)
                        o = full(dve, "dt_", n, level, half).rearrange("p (a t) -> p a t", a=4)
                        if level:
                            drained(dve, "dt_", n, level - 1, half)
                        V.tensor_tensor(inv_t[:, hs, :], inv_t[:, hs, :], o, ALU.subtract
                                        ).then_inc(free_sem("dt_", n, level, half), 1)
                if n:
                    ln_stats(n - 1)
                if n < NT - 1:
                    zero_inverses(n + 1)
                    o = full(dve, "s_rw", n)
                    if n:
                        link(V.tensor_tensor(s_sum, s_rw[:, n % 2, :], o, ALU.add))
                    else:
                        link(V.tensor_copy(s_sum, o))
                    for f in range(4):
                        c = slice(f * P, (f + 1) * P)
                        ins = V.scalar_tensor_tensor(out=s_rw[:, (n + 1) % 2, c], in0=s_sum[:, c],
                                                     scalar=e_s[:, f, n:n + 1], in1=blocks, op0=ALU.mult, op1=ALU.mult)
                        if f < 3:
                            link(ins)
                        else:
                            ins.then_inc(free_sem("s_rw", n), 1)
                    drained(dve, "s_rw", n)
                    dve.sem_inc(S["s_rw_ready"], 1)
                if n:
                    ln_out(n - 1)
            ln_stats(NT - 1)
            ln_out(NT - 1)
            project_out(1)
            norm(3)
            mlp(1)
            norm(4)


PARAMS = ["x", "w_up", "w_down", "e_w_in", "e_w_out", "o_w_in", "o_w_out", "rw_w2", "rw_a2", "rw_g2"]


def kernel(**inputs):
    import concourse.bacc as bacc
    from concourse.bass_utils import run_bass_kernel_spmd

    nc = bacc.Bacc("TRN2", target_bir_lowering=False, num_devices=1)
    arrays, dram = {}, {}
    names = PARAMS + [n for n, _ in STACK_A + STACK_B + ROWS]
    data = {n: np.ascontiguousarray(inputs[n]) for n in names}
    data["main_const"] = np.concatenate([np.asarray(a, np.float32) for _, a in MAIN_COLS], 1)
    data["even_const"] = np.concatenate([np.asarray(a, np.float32) for _, a in EVEN_COLS], 1)
    for name, a in data.items():
        arrays[f"in_{name}"] = a
        dram[name] = nc.dram_tensor(f"in_{name}", a.shape, mybir.dt.from_np(a.dtype), kind="ExternalInput").ap()
    out = nc.dram_tensor("out_0", (1, T, D), F32, kind="ExternalOutput").ap()
    trunk(nc, dram, out)
    r = run_bass_kernel_spmd(nc, [arrays], core_ids=[0])
    return r.results[0]["out_0"]
```

```python
from contextlib import ExitStack

import numpy as np
import concourse.bass as bass
from concourse import mybir

F32 = mybir.dt.float32
F32R = mybir.dt.float32r
ALU = mybir.AluOpType
ACT = mybir.ActivationFunctionType
AX = mybir.AxisListType

P = 128
T = 512
NT = T // P
D = 1024
KT = D // P
FF = 4096
FT = FF // P
SW = P
RING = 4
CUT = 2
NBANK = 8
BANK = 512
NEG = -1.0e30
HUGE = 1.0e38
DECAY_K = float(np.exp(np.float32(-0.5)))

SUB = 32
HALF = P // 2

_i = np.arange(P)
_row, _col = _i[:, None], _i[None, :]


def _const_columns():
    half = 8
    inv = np.float32(500000.0) ** (-np.arange(half, dtype=np.float32) * np.float32(2.0) / np.float32(16))
    ang = (np.arange(T, dtype=np.float32)[:, None] * inv[None, :]).astype(np.float32)
    cos, sin = np.ones((P, T), np.float32), np.zeros((P, T), np.float32)
    rot = np.zeros((P, P), np.float32)
    for base in (0, 64):
        for j in range(half):
            cos[base + j] = cos[base + half + j] = np.cos(ang[:, j])
            sin[base + j] = sin[base + half + j] = np.sin(ang[:, j])
            rot[base + half + j, base + j] = -1.0
            rot[base + j, base + half + j] = 1.0
    dup = np.zeros((P, 2, P), np.float32)
    for g in range(2):
        for m in range(P):
            dup[64 * g + m % 64, g, m] = 1.0
    k = np.arange(2 * P)[None, :]
    band = np.where((k > _row) & (k <= _row + P), 0.0, NEG)
    first = np.where((k > _row) & (k <= _row + P) & (k >= P), 0.0, NEG)
    even = [("cos", cos), ("sin", sin), ("rot", rot), ("dup", dup.reshape(P, -1)), ("band", band), ("first", first)]
    common = [
        ("ident", np.eye(P)), ("ones", np.ones((P, P))),
        ("upper", _row <= _col),
        ("blocks", (_row // 64) == (_col // 64)),
        ("add_st", np.where(_row <= _col, 0.0, NEG)),
        ("add_ts", np.where(_col <= _row, 0.0, NEG)),
        ("eps", np.repeat(np.array([[1e-5, 1e-6, 64e-5, 0.0]]), P, 0)),
    ]
    pairs = (((_col // SUB) % 2 == 1) & ((_row // SUB) == (_col // SUB) - 1))[:, (_i // SUB) % 2 == 1]
    reset = np.ones((P, T))
    reset[:, ::P] = 0.0
    odd = [
        ("pairs", pairs),
        ("four", np.concatenate([_col < _row, _row < _col, _row <= _col, _row <= _col], 1)),
        ("reset", reset),
        ("heads", np.stack([_i // 64 == 0, _i // 64 == 1], 1)),
        ("to_head", np.concatenate([np.arange(8)[None, :] == 2 * f + _row // 64 for f in range(4)], 1)),
        ("from_head", np.concatenate([_row == 2 * f + _col // 64 for f in range(4)], 1)),
    ]
    return common + odd, even


def _offsets(cols):
    at, out = 0, {}
    for name, a in cols:
        out[name] = (at, a.shape[1])
        at += a.shape[1]
    return out, at


MAIN_COLS, EVEN_COLS = _const_columns()
MAIN_AT, MAIN_W = _offsets(MAIN_COLS)
EVEN_AT, EVEN_W = _offsets(EVEN_COLS)

STACK_A = [("mix_norm", 16), ("mlp_norm", 16), ("final_norm", 8), ("ml_conv_w", 16), ("ml_conv_b", 4),
           ("ssm_conv_w", 32), ("ssm_conv_b", 8)]
STACK_B = [("rw_mu", 14), ("rw_w0", 4), ("rw_a0", 4), ("rw_k_k", 4), ("rw_k_a", 4), ("rw_r_k", 4)]
ROWS = [("att_sinks", 8), ("ml_i_bias", 4), ("ml_f_bias", 4), ("ssm_dt_bias", 8), ("ssm_a_log", 8), ("ssm_d", 8),
        ("ml_norm", 512), ("ssm_norm", 512), ("rw_ln_w", 512), ("rw_ln_b", 512)]


def _starts(spec):
    at, out = 0, {}
    for name, n in spec:
        out[name] = at
        at += n
    return out, at


A_AT, A_N = _starts(STACK_A)
B_AT, B_N = _starts(STACK_B)
R_AT, R_N = _starts(ROWS)

E_GATES, E_Q, E_K, E_VA, E_QK, E_V, E_O = 2304, 0, 512, 640, 768, 1280, 1792
GATE_SLOT = E_GATES + 8 - P
EVEN_SLOTS = ([(GATE_SLOT, ("f", "gates"))] + [(E_QK + P * j, ("qk", j)) for j in range(4)]
              + [(E_K, ("k",)), (E_VA, ("f", "v_att"))] + [(E_Q + P * j, ("q", j)) for j in range(4)]
              + [(E_V + P * j, ("f", "v", j)) for j in range(4)] + [(E_O + P * j, ("f", "o", j)) for j in range(4)])
O_Z, O_XBC, O_DT, O_RW = 0, 512, 1536, 1544
RW_ORDER = [12, 13] + list(range(4, 8)) + list(range(4)) + list(range(8, 12))
ODD_SLOTS = ([(O_DT, ("f", "dt"))] + [(O_XBC + P * j, ("xbc", j)) for j in range(8)]
             + [(O_Z + P * j, ("f", "z", j)) for j in range(4)] + [(O_RW + P * j, ("rw", j)) for j in RW_ORDER])


def even_front():
    for j in range(11):
        yield "slot", j
        if j == 1:
            yield "turn", ("gates",)
        if j == 4:
            yield "soft", 0
        if j == 6:
            yield "cum", 0
            yield "rope", 4
        if j == 7:
            yield "turn", ("v_att",)
        if j == 8:
            yield "dup", 0
            yield "dup", 1
        if j == 9:
            yield "rope", 0
            yield "rope", 1
    yield "rope", 2
    for u in range(8 + 3):
        if u < 8:
            yield "slot", 11 + u
        if u == 0:
            yield "rope", 3
        if 1 <= u < 9:
            yield "turn", EVEN_SLOTS[10 + u][1][1:]
        if u < 8:
            yield "score", u
        if 2 <= u < 10:
            yield "att_turn", u - 2
        if u >= 3:
            yield "att_out", u - 3
        if u < 8:
            yield "att_exp", u
        if u < 4:
            yield "g_row", u
        if u == 5:
            yield "m_exp", 0
        if u in (5, 6, 8, 9):
            yield "m_row", (5, 6, 8, 9).index(u)
        if u == 8:
            yield "w_exp", 0
            yield "w_exp", 1
        if u in (9, 10):
            yield "w_exp", u - 7


def odd_front():
    after = {14: ("ssd_front", 0), 16: ("ssd_back", 0), 17: ("ssd_front", 1), 19: ("ssd_back", 1),
             20: ("ssd_front", 2), 22: ("ssd_back", 2), 23: ("ssd_front", 3), 25: ("ssd_back", 3)}
    for j in range(len(ODD_SLOTS)):
        yield "slot", j
        if j == 1:
            yield "turn", ("dt",)
        if 10 <= j < 14:
            yield "turn", ("z", j - 10)
        if j == 13:
            yield "a_cum",
        if j in after:
            yield after[j]


def rwkv_chunks():
    def heads(n, first, last):
        for hh in range(first, last):
            yield "mats", n, hh // 2, hh % 2

    yield "rk_tok", 0
    yield "rb_tok", 0
    yield from heads(0, 0, 8)
    for n in range(NT):
        for half in range(2):
            yield "pt", n, 0, half
        for half in range(2):
            yield "d", n, half
            yield "dt_", n, 0, half
        for half in range(2):
            yield "pt", n, 1, half
        for half in range(2):
            yield "dt_", n, 1, half
        more = n + 1 < NT
        yield "rhs", n
        if more:
            yield "rk_tok", n + 1
            yield "rb_tok", n + 1
        yield "u", n
        if more:
            yield from heads(n + 1, 0, 1)
        yield "y", n
        if more:
            yield from heads(n + 1, 1, 2)
            yield "s_rw", n
            yield from heads(n + 1, 2, 8)


SCALED_TILES = [key[1:] for _, key in ODD_SLOTS if key[0] == "f"]
STAGE_AT = 13056
ARENA = STAGE_AT + 2 * P


class Plan:

    def __init__(self):
        self.turns = [0] * NBANK
        self.at = {}
        self.next = 0

    def put(self, *key, bank=None, times=1):
        if bank is None:
            bank = self.next
            self.next = (self.next + 1) % NBANK
        assert key not in self.at, key
        self.at[key] = (bank, self.turns[bank])
        self.turns[bank] += times


def make_plan():
    plan = Plan()
    put = plan.put
    for k in range(KT):
        put("x", k)
    for layer in range(2):
        put("norm", 2 * layer)
        if layer == 0:
            put("stack_a")
            put("stack_b")
        if layer == 0:
            for item in even_front():
                kind = item[0]
                if kind == "slot":
                    put(*EVEN_SLOTS[item[1]][1])
                elif kind == "turn":
                    put(*item[1])
                elif kind in ("rope", "dup"):
                    put(*item)
                elif kind == "score":
                    put("score", item[1], 0)
                    put("score", item[1], 1)
                elif kind == "att_turn":
                    put("turn", item[1], 0)
                    put("turn", item[1], 1)
                elif kind == "att_out":
                    put("att", item[1])
                elif kind in ("cum", "g_row", "m_row"):
                    put(*item)
            for a in range(2):
                put("k_tok", a)
            for n in range(NT):
                for par in range(2):
                    put("qk_st", n, par)
                if n < NT - 1:
                    for a in range(2):
                        put("c_loc", n, a)
                for a in range(2):
                    put("num", n, a)
                if n:
                    for par in range(2):
                        put("inter", n, par)
            for f in range(4):
                put("y_ml", f)
        else:
            for item in odd_front():
                kind = item[0]
                if kind == "slot":
                    put(*ODD_SLOTS[item[1]][1])
                elif kind == "turn":
                    put(*item[1])
                elif kind == "a_cum":
                    put("a_cum")
                elif kind == "ssd_front":
                    n = item[1]
                    put("x_tok", n)
                    put("b_tok", n)
                    put("a_row", n, 0)
                    put("a_row", n, 1)
                    put("cb", n)
                else:
                    n = item[1]
                    put("y_diag", n)
                    if n:
                        put("y_off", n)
                    if n < NT - 1:
                        put("s_loc", n)
            put("kk_sum")
            for f in range(4):
                put("decay", f)
                put("a", f)
            for f in range(4):
                put("y_ssm", f)
            for f in range(4):
                put("kk_inv", f)
            for n in range(NT):
                put("g_tok", n)
            inv_bank = plan.at["kk_inv", 0][0]
            for f in range(4):
                for par in range(2):
                    put("sub", f, par, bank=(inv_bank + par + (2 if f == 3 else 0)) % NBANK)
                if f == 0:
                    for n in range(NT):
                        put("rv_tok", n, bank=plan.at["g_tok", n][0])
            put("bonus")
            for item in rwkv_chunks():
                put(*item)
            for f in range(4):
                put("y_rw", f)
        for j in range(KT):
            put("out", layer, j, bank=j)
        put("norm", 2 * layer + 1, bank=0)
        for j in range(8):
            put("mlp", layer, j, bank=j, times=8)
    put("norm", 4)
    for t in range(NT):
        for half in range(2):
            put("result", t, half)
    return plan


def trunk(nc, dram, out):
    PLAN = make_plan()
    with ExitStack() as ctx:
        def sb(name, width):
            return ctx.enter_context(nc.sbuf_tensor(name, [P, width], F32))

        def sem(name):
            return ctx.enter_context(nc.semaphore(name))

        def cut(tile, at, *shape):
            n = int(np.prod(shape))
            v = tile[:, at:at + n]
            if len(shape) == 2:
                v = v.rearrange("p (a b) -> p a b", b=shape[1])
            if len(shape) == 3:
                v = v.rearrange("p (a b c) -> p a b c", b=shape[1], c=shape[2])
            return v

        ps = ctx.enter_context(nc.psum_tensor("ps", [P, NBANK, BANK], F32))
        h_t = sb("h", KT * T)
        y_t = sb("y_mix", KT * T)
        raw_w = sb("raw_w", RING * KT * SW)[:, :].rearrange("p (r k c) -> p r k c", r=RING, c=SW)

        def sbr(stack, name, width):
            return stack.enter_context(nc.sbuf_tensor(name, [P, width], F32R))

        w_hi = sbr(ctx, "w_hi", CUT * KT * SW)[:, :].rearrange("p (r k c) -> p r k c", r=CUT, c=SW)
        w_lo = sbr(ctx, "w_lo", CUT * KT * SW)[:, :].rearrange("p (r k c) -> p r k c", r=CUT, c=SW)
        main_t = sb("main", MAIN_W)
        cols_t = sb("cols", A_N + B_N)
        rows_t = sb("rows", R_N)
        small = sb("small", 640)
        rwkv_raw = sb("rwkv_raw", 14 * (T + 1))
        with ExitStack() as inner:
            hn_hi = sbr(inner, "hn_hi", KT * T)[:, :].rearrange("p (k t) -> p k t", t=T)
            hn_lo = sbr(inner, "hn_lo", KT * T)[:, :].rearrange("p (k t) -> p k t", t=T)
        late = sb("late", 2 * KT * T)
        with ExitStack() as inner:
            hid_hi = sbr(inner, "hid_hi", KT * T)[:, :].rearrange("p (k t) -> p k t", t=T)
            hid_lo = sbr(inner, "hid_lo", KT * T)[:, :].rearrange("p (k t) -> p k t", t=T)
        arena = sb("arena", ARENA)
        rms_t = sb("rms", T)[:, :]
        relu_t = sb("relu", 2 * T)[:, :].rearrange("p (a t) -> p a t", a=2)
        lora = sb("lora", 512 * 2)

        h = cut(h_t, 0, KT, T)
        y_mix = cut(y_t, 0, KT, T)

        def const(name):
            at, w = MAIN_AT[name]
            return main_t[:, at:at + w]

        ident, ones, upper, blocks = const("ident"), const("ones"), const("upper"), const("blocks")
        eps = const("eps")

        def col_a(name, i):
            return cols_t[:, A_AT[name] + i:A_AT[name] + i + 1]

        def col_b(name, i):
            return cols_t[:, A_N + B_AT[name] + i:A_N + B_AT[name] + i + 1]

        def row(name, width):
            return rows_t[:, R_AT[name]:R_AT[name] + width]

        def over(ap, axis, n):
            v = ap.unsqueeze(axis)
            shape = list(v.shape)
            shape[axis] = n
            return v.to_broadcast(shape)

        bank_full = [sem(f"bank_full{b}") for b in range(NBANK)]
        bank_free = [sem(f"bank_free{b}") for b in range(NBANK)]
        w_full = [sem(f"w_full{r}") for r in range(RING)]
        w_high = sem("w_high")
        w_cut = sem("w_cut")
        x_in = sem("x_in")
        ident_in = sem("ident_in")
        main_in = sem("main_in")
        even_in = sem("even_in")
        stack_in = sem("stack_in")
        rows_in = sem("rows_in")
        lora_in = sem("lora_in")
        out_done = sem("out_done")
        dve_step = sem("dve_step")
        act_step = sem("act_step")
        stack_zero = sem("stack_zero")
        squared = sem("squared")
        rms_root = sem("rms_root")
        normed = sem("normed")
        summed = sem("summed")
        scaled = sem("scaled")
        high = sem("high")
        hid_square, hid_high, hid_ready = sem("hid_square"), sem("hid_high"), sem("hid_ready")

        def bank(key):
            return ps[:, PLAN.at[key][0], :]

        def free(eng, *key):
            b, turn = PLAN.at[key]
            if turn:
                eng.wait_ge(bank_free[b], turn)
            return ps[:, b, :]

        def full(eng, *key):
            b, turn = PLAN.at[key]
            eng.wait_ge(bank_full[b], turn + 1)
            return ps[:, b, :]

        def drained(eng, *key):
            b, turn = PLAN.at[key]
            eng.wait_ge(bank_free[b], turn + 1)

        def full_sem(*key):
            return bank_full[PLAN.at[key][0]]

        def free_sem(*key):
            return bank_free[PLAN.at[key][0]]

        base = {}
        n_slots = 0
        for layer in range(2):
            base["in", layer] = n_slots
            n_slots += len(EVEN_SLOTS if layer == 0 else ODD_SLOTS)
            base["out", layer] = n_slots
            n_slots += KT
            base["mlp", layer] = n_slots
            n_slots += 4 * 16

        slot_use = []
        for layer in range(2):
            slot_use += [PLAN.at[key] for _, key in (EVEN_SLOTS if layer == 0 else ODD_SLOTS)]
            slot_use += [PLAN.at["out", layer, j] for j in range(KT)]
            for s in range(4 * 16):
                b, t0 = PLAN.at["mlp", layer, s % 8]
                slot_use.append((b, t0 + s // 8))

        w_in = [dram["e_w_in"][0], dram["o_w_in"][0]]
        w_out = [dram["e_w_out"][0], dram["o_w_out"][0]]

        pos = [0]

        def take(*shape):
            at = pos[0]
            pos[0] += int(np.prod(shape))
            assert pos[0] <= STAGE_AT, pos[0]
            return cut(arena, at, *shape)

        even_t = take(EVEN_W)

        def even_const(name):
            at, w = EVEN_AT[name]
            return even_t[:, at:at + w]

        x_tok_in = rwkv_raw[:, 0:NT * D].rearrange("p (n d) -> p n d", n=NT)
        qk_raw = rwkv_raw[:, 4096:4096 + 5 * T].rearrange("p (a t) -> p a t", a=5)
        q_rot = qk_raw
        k_rot = rwkv_raw[:, 6656:6656 + T]
        f_tile = [cut(rwkv_raw, 2048, 2, T), cut(y_t, 3072, 2, T)]
        k_dup = take(2, P + T)
        v_dup = take(NT + 1, 2, P)
        conv_at = pos[0]
        conv_in = take(4, T + 3)
        conv_out = take(4, T)
        v_ml = take(NT, 4, 129)
        o_gate = take(NT, 512)
        att_p = [cut(rwkv_raw, 0, 4, 256), cut(rwkv_raw, 1024, 4, 256),
                 relu_t.rearrange("p a t -> p (a t)").rearrange("p (j k) -> p j k", k=256)]
        att_pt = y_mix[:, 4:, :].rearrange("p (a b) t -> p a b t", a=2)
        k_w = cut(arena, conv_at, NT, 256)
        w_ml = cut(late, 0, 4, 4, P)
        k_keep = cut(rwkv_raw, 0, 2, 512)
        dg = cut(arena, conv_at + 1024, 2, 4 * P)
        mtmp = cut(rwkv_raw, 3072, 2, 4 * P)
        qkw = cut(rwkv_raw, 2048, 2, 4 * P)
        n_sb = cut(rwkv_raw, 4096, 2, 2, 129 * 2)
        c_state = cut(rwkv_raw, 4096 + 1032, NT, 2, 129)
        c_tmp = cut(rwkv_raw, 4096 + 1032 + 1032, 2, 129)
        sm_at = [0]

        def tiny(*shape):
            at = sm_at[0]
            sm_at[0] += int(np.prod(shape))
            assert sm_at[0] <= 640
            return cut(small, at, *shape)

        a_mx, a_nm, a_se, a_rs, a_es, a_l = (tiny(3, 4) for _ in range(6))
        gt = tiny(NT, 8)
        fg, af, lf, li, gg, gmax, cmx, mx, marr, mm, dfa, dfb, wi_arg, em_arg = (tiny(NT, 4) for _ in range(14))
        cumb = tiny(2, 16)
        wgt_arg = tiny(NT, 4)
        dn = tiny(2, 4)
        st6 = tiny(4, 6)
        mv = tiny(16, 2)

        raw = cut(rwkv_raw, 0, 14, T + 1)
        pos[0] = 0
        z_tok = take(NT, 512)
        xbc_at = pos[0]
        xbc_in = take(8, T + 3)
        xbc = take(8, T)
        xs_tok = take(2, 512)
        b_tok = take(2, 256)
        s_state = take(2, 512)
        xdt, xds, s_w, s_t = (cut(arena, xbc_at + j * 1024, 2, 512) for j in range(4))
        s_dg = s_t
        s_m = cut(y_t, 0, 2, 8 * P)
        s_y = y_mix[:, 4:, :]
        pos[0] = 0
        kk_s, b_s, v_tok, g_tok = (cut(late, j * 2048, 4, T) for j in range(4))
        t1, inv_q = take(T), take(8, HALF)
        inv_at = pos[0]
        inv_d = take(8, P)
        inv_t = take(8, P)
        inv_p = take(8, P)
        cum_now, cum_before, cum_exp = (cut(arena, inv_at + j * 2 * T, 2, T) for j in range(3))
        y_rw = take(NT, 512)
        mats_at = pos[0]
        mats = take(8, 4, P)
        mats_rk = cut(arena, mats_at, 4, T)
        decay_s = cut(arena, mats_at + 4 * T, 4, T)
        k_gain = y_rw
        sums_at = pos[0]
        s_sum = take(512)
        rhs_sb = take(512)
        neg_u = take(512)
        s_rw = take(2, 512)
        a_s = cut(arena, sums_at, 4, T)
        sub_tok = cut(y_t, 2048, SUB, SUB)
        sub_prob = cut(arena, sums_at, SUB, SUB)
        sub_tmp = cut(arena, sums_at + 2 * SUB * SUB, 512)
        sub_inv = cut(arena, inv_at, SUB, SUB)
        inv_rows, inv_cols = (cut(rwkv_raw, 8 * (T + 1) + j * SUB * SUB, SUB, SUB) for j in range(2))
        k_tok, bb_tok = (cut(y_t, 2048 + j * 1024, 2, 512) for j in range(2))
        wa2 = lora[:, 0:512]
        g2 = lora[:, 512:1024]
        sm_at[0] = 0
        dtr, dta, dte, dtt, dA = (tiny(NT, 8) for _ in range(5))
        acum = tiny(2, 32)
        nacum, dsx, ea, ds_, dec = (tiny(32) for _ in range(5))
        expa = tiny(8)
        gss = tiny(8)
        bon = tiny(NT, 8)
        e_s = tiny(4, NT)
        e_a = tiny(4, NT)
        omka = tiny(4)
        token_root = tiny(NT)
        lnm = tiny(NT, 8)
        lnv = tiny(NT, 8)

        names = ("att_max att_exp att_probs halo rope_done kd_v v_ones conv_ready silu_done soft_e soft_l lf_ready "
                 "g_diag g_ready m_diag m_ready wl_ready mexp k_scaled qkw_ready c_ready n_keep hm_done ln_root "
                 "o_sig y_ml_ready ssm_conv ssm_silu s_soft_e s_soft_l da_ready acum_args acum_exps s_diag s_masked "
                 "s_decay s_m_ready xdt_ready s_new xs_kept s_yprod z_silu s_sq s_root y_ssm_ready mixed tanh_done "
                 "gd_sig sgm a_sig cum_args cum_exps kk_sq kk_root rk_ready scales_arg scales tilde mats_ready "
                 "inv_step urhs_ready s_rw_ready ln2_sq ln2_var ln2_root y_rw_ready x_out kkraw inv_zero inv_filled omka_ready f_scaled x_out_right root_inverted sub_turned k_gained kk_inverted tilde_kr").split()
        S = {n: sem(n) for n in names}

        block = ctx.enter_context(nc.Block())

        @block.sync
        def _(sp):
            sp.dma_start(x_tok_in, dram["x"][0].rearrange("(n p) d -> p n d", p=P)).then_inc(x_in, 16)
            sp.dma_start(main_t[:, 0:2 * P], dram["main_const"][:, 0:2 * P]).then_inc(ident_in, 16)

            def load(n, src):
                if n >= RING:
                    sp.wait_ge(w_cut, n - RING + 1)
                sp.dma_start(raw_w[:, n % RING], src).then_inc(w_full[n % RING], 16)

            for layer in range(2):
                for j, (c0, _) in enumerate(EVEN_SLOTS if layer == 0 else ODD_SLOTS):
                    load(base["in", layer] + j, w_in[layer][:, c0:c0 + SW].rearrange("(k p) c -> p k c", p=P))
                for j in range(KT):
                    load(base["out", layer] + j,
                         w_out[layer][:, j * SW:(j + 1) * SW].rearrange("(k p) c -> p k c", p=P))
                up = dram["w_up"][layer].rearrange("(k p) c -> p k c", p=P)
                down = dram["w_down"][layer].rearrange("(k p) c -> p k c", p=P)
                b0 = base["mlp", layer]
                with sp.Fori(0, 4) as i:
                    for s in range(16):
                        sp.wait_ge(w_cut, i * 16 + (b0 + s - RING + 1))
                        src = (up[:, :, bass.ds(i * (KT * SW) + s * SW, SW)] if s < 8 else
                               down[:, bass.ds(i * KT, KT), (s - 8) * SW:(s - 7) * SW])
                        sp.dma_start(raw_w[:, (b0 + s) % RING], src).then_inc(w_full[(b0 + s) % RING], 16)
            for t in range(NT):
                sp.wait_ge(S["x_out"], t + 1)
                sp.wait_ge(S["x_out_right"], t + 1)
                sp.dma_start(out[0, t * P:(t + 1) * P, :], arena[:, t * D:(t + 1) * D]).then_inc(out_done, 16)
            sp.wait_ge(out_done, 16 * NT)

        @block.gpsimd
        def _(pool):
            n_stack = 0
            nc.gpsimd.memset(arena[:, STAGE_AT:STAGE_AT + 2 * P], 0.0).then_inc(stack_zero, 1)
            pool.wait_ge(stack_zero, 1)
            stage = {"a": (arena[:, STAGE_AT:STAGE_AT + P], STACK_A, A_AT), "b": (arena[:, STAGE_AT + P:STAGE_AT + 2 * P], STACK_B, B_AT)}
            for key in "ab":
                tile, spec, at = stage[key]
                for name, n in spec:
                    a = dram[name]
                    flat = a.rearrange(" ".join("abcd"[:len(a.shape)]) + " -> (" + " ".join("abcd"[:len(a.shape)]) + ")") \
                        if len(a.shape) > 1 else a
                    pool.dma_start(tile[at[name]:at[name] + n, :], flat.rearrange("(n p) -> n p", p=P)
                                   ).then_inc(stack_in, 16)
                    n_stack += 1
            pool.dma_start(main_t[:, 2 * P:], dram["main_const"][:, 2 * P:]).then_inc(main_in, 16)
            pool.dma_start(even_t, dram["even_const"]).then_inc(even_in, 16)
            for name, n in ROWS:
                pool.dma_start(row(name, n), dram[name][0:1, :].to_broadcast([P, n])).then_inc(rows_in, 16)
            pool.dma_start(wa2[0:64, :], dram["rw_w2"][0]).then_inc(lora_in, 16)
            pool.dma_start(wa2[64:128, :], dram["rw_a2"][0]).then_inc(lora_in, 16)
            pool.dma_start(g2, dram["rw_g2"][0]).then_inc(lora_in, 16)

            def low_part(n):
                nc.gpsimd.tensor_tensor(w_lo[:, n % CUT], raw_w[:, n % RING], w_hi[:, n % CUT].bitcast(F32), ALU.subtract).then_inc(w_cut, 1)

            for layer in range(2):
                for n in range(base["in", layer], base["mlp", layer]):
                    pool.wait_ge(w_high, n + 1)
                    low_part(n)
                    if n == base["out", 1] + CUT - 1:
                        for f in range(4):
                            pool.wait_ge(S["rk_ready"], f + 1)
                            pool.wait_ge(S["cum_exps"], f + 1)
                            nc.gpsimd.tensor_tensor(kk_s[:, f, :], kk_s[:, f, :], cum_before[:, f % 2, :], ALU.mult)
                            nc.gpsimd.tensor_tensor(raw[:, f, 1:], raw[:, f, 1:], cum_exp[:, f % 2, :], ALU.mult
                                                    ).then_inc(S["tilde_kr"], 1)
                b0 = base["mlp", layer]
                with pool.Fori(0, 4) as i:
                    for s in range(16):
                        pool.wait_ge(w_high, i * 16 + (b0 + s + 1))
                        low_part(b0 + s)

        N_STACK = len(STACK_A) + len(STACK_B)
        stage_a, stage_b = arena[:, STAGE_AT:STAGE_AT + P], arena[:, STAGE_AT + P:STAGE_AT + 2 * P]

        @block.tensor
        def _(pe):
            mm = nc.tensor.matmul

            def close(ins, *key):
                ins.then_inc(full_sem(*key), 1)

            def turn(key, parts):
                o = free(pe, *key)
                for j, src in enumerate(parts):
                    ins = nc.tensor.transpose(o[:, j * P:(j + 1) * P], src, ident)
                close(ins, *key)

            def norm(i):
                o = free(pe, "norm", i)
                pe.wait_ge(summed, KT * (i + 1))
                close(mm(o, ones, rms_t, start=True, stop=True), "norm", i)

            def products(pairs):
                for k in range(KT):
                    o, (a_hi, a_lo), (b_hi, b_lo) = pairs(k)
                    mm(o, a_hi, b_hi, start=(k == 0), stop=False)
                    mm(o, a_hi, b_lo, start=False, stop=False)
                    ins = mm(o, a_lo, b_hi, start=False, stop=(k == KT - 1))
                return ins

            def feature_tile(o, slot, hi, lo, before=None):
                def pairs(k):
                    if before:
                        before(k)
                    return o, (w_hi[:, slot, k, :], w_lo[:, slot, k, :]), (hi[:, k, :], lo[:, k, :])
                return products(pairs)

            def operand_ready(phase):
                return lambda k: pe.wait_ge(normed, KT * phase + k + 1)

            def project_in(layer, j):
                n = base["in", layer] + j
                key = (EVEN_SLOTS if layer == 0 else ODD_SLOTS)[j][1]
                pe.wait_ge(w_cut, n + 1)
                close(feature_tile(free(pe, *key), n % CUT, hn_hi, hn_lo,
                                   before=operand_ready(3 * layer) if j == 0 else None), *key)

            def turn_projected(layer, key, buf):
                if layer == 0:
                    drained(pe, "f", *key)
                else:
                    pe.wait_ge(S["f_scaled"], SCALED_TILES.index(key) + 1)
                turn(key, [f_tile[layer][:, buf, t * P:(t + 1) * P] for t in range(NT)])

            def project_out(layer):
                for j in range(KT):
                    n = base["out", layer] + j
                    pe.wait_ge(w_cut, n + 1)
                    close(feature_tile(free(pe, "out", layer, j), n % CUT, hid_hi, hid_lo,
                                       before=operand_ready(3 * layer + 1) if j == 0 else None), "out", layer, j)

            def mlp(layer):
                b0 = base["mlp", layer]
                with pe.Fori(0, 4) as i:
                    for s in range(16):
                        n = b0 + s
                        b, t0 = PLAN.at["mlp", layer, s % 8]
                        pe.wait_ge(w_cut, i * 16 + (n + 1))
                        pe.wait_ge(bank_free[b], i * 2 + (t0 + s // 8))
                        if s < 8:
                            ins = feature_tile(ps[:, b, :], n % CUT, hn_hi, hn_lo,
                                               before=operand_ready(3 * layer + 2) if s == 0 else None)
                        else:
                            ins = feature_tile(ps[:, b, :], n % CUT, hid_hi, hid_lo, before=(
                                lambda k: pe.wait_ge(hid_ready, i * 8 + (32 * layer + k + 1))) if s == 8 else None)
                        ins.then_inc(bank_full[b], 1)

            def even():
                dup = even_const("dup").rearrange("p (g m) -> p g m", g=2)
                turned = 0
                for item in even_front():
                    kind, u = item[0], item[1]
                    n, g = (u // 2, u % 2) if kind in ("score", "att_out") else (None, None)
                    if kind == "slot":
                        project_in(0, u)
                    elif kind == "turn":
                        turn_projected(0, u, turned % 2)
                        turned += 1
                    elif kind == "rope":
                        drained(pe, *(("q", u) if u < 4 else ("k",)))
                        pe.wait_ge(even_in, 16)
                        close(mm(free(pe, "rope", u), even_const("rot"), qk_raw[:, u, :], start=True, stop=True),
                              "rope", u)
                    elif kind == "dup":
                        pe.wait_ge(S["rope_done"], 1)
                        close(mm(free(pe, "dup", u), dup[:, u, :], k_rot, start=True, stop=True), "dup", u)
                    elif kind == "score":
                        if u == 0:
                            drained(pe, "dup", 1)
                            drained(pe, "dup", 0)
                            pe.wait_ge(S["halo"], 3)
                            drained(pe, "v_att")
                        pe.wait_ge(S["rope_done"], 3 if u == 0 else 5)
                        for par in range(2):
                            o = free(pe, "score", u, par)
                            r = slice(64 * par, 64 * par + 64)
                            for a in range(2):
                                ins = mm(o[:, a * 256:(a + 1) * 256], q_rot[r, 2 * g + a, n * P:(n + 1) * P],
                                         k_dup[r, g, n * P:n * P + 256], start=True, stop=True)
                            close(ins, "score", u, par)
                    elif kind == "att_turn":
                        pe.wait_ge(S["att_probs"], u + 1)
                        for blk in range(2):
                            turn(("turn", u, blk), [att_p[u % 3][:, j, blk * P:(blk + 1) * P] for j in range(4)])
                    elif kind == "att_out":
                        o = free(pe, "att", u)
                        for blk in range(2):
                            drained(pe, "turn", u, blk)
                            ins = mm(o, v_dup[:, n + blk, g, :], att_pt[:, u % 2, blk, :], start=(blk == 0), stop=(blk == 1))
                        close(ins, "att", u)
                    elif kind == "cum":
                        pe.wait_ge(S["lf_ready"], 1)
                        o = free(pe, "cum", 0)
                        lf_ = lf.rearrange("p a b -> p (a b)")
                        mm(o[:, 0:16], upper, lf_, start=True, stop=True)
                        close(mm(o[:, 16:32], ones, lf_, start=True, stop=True), "cum", 0)
                    elif kind in ("g_row", "m_row"):
                        pe.wait_ge(S["g_diag" if kind == "g_row" else "m_diag"], u + 1)
                        close(mm(free(pe, kind, u), ones, dg[:, u % 2, :], start=True, stop=True), kind, u)
                pe.wait_ge(S["silu_done"], 4)
                for a in range(2):
                    turn(("k_tok", a), [conv_out[:, 2 + a, n * P:(n + 1) * P] for n in range(NT)])
                for j in range(4):
                    drained(pe, "v", j)
                pe.wait_ge(S["v_ones"], 1)
                for n in range(NT):
                    tok = slice(n * P, (n + 1) * P)
                    for par in range(2):
                        o = free(pe, "qk_st", n, par)
                        r = slice(64 * par, 64 * par + 64)
                        for a in range(2):
                            ins = mm(o[:, a * P:(a + 1) * P], conv_out[r, 2 + a, tok], conv_out[r, a, tok],
                                     start=True, stop=True)
                        close(ins, "qk_st", n, par)
                    if n < NT - 1:
                        pe.wait_ge(S["k_scaled"], n + 1)
                        for a in range(2):
                            o = free(pe, "c_loc", n, a)
                            for par in range(2):
                                ins = mm(o[:, par * 129:(par + 1) * 129], k_w[:, n, a * P:(a + 1) * P],
                                         v_ml[:, n, 2 * a + par, :], start=True, stop=True)
                            close(ins, "c_loc", n, a)
                    pe.wait_ge(S["qkw_ready"], n + 1)
                    for a in range(2):
                        o = free(pe, "num", n, a)
                        for par in range(2):
                            hh = 2 * a + par
                            ins = mm(o[:, par * 129:(par + 1) * 129], qkw[:, n % 2, hh * P:(hh + 1) * P],
                                     v_ml[:, n, hh, :], start=True, stop=True)
                        close(ins, "num", n, a)
                    if n:
                        pe.wait_ge(S["c_ready"], n)
                        for par in range(2):
                            o = free(pe, "inter", n, par)
                            r = slice(64 * par, 64 * par + 64)
                            for a in range(2):
                                ins = mm(o[:, a * 129:(a + 1) * 129], conv_out[r, a, tok], c_state[r, n, a, :],
                                         start=True, stop=True)
                            close(ins, "inter", n, par)
                pe.wait_ge(S["y_ml_ready"], NT)
                for f in range(4):
                    turn(("y_ml", f), [o_gate[:, n, f * P:(f + 1) * P] for n in range(NT)])

            def odd():
                turned = 0
                for item in odd_front():
                    kind = item[0]
                    n = item[1] if kind in ("ssd_front", "ssd_back") else 0
                    tok = slice(n * P, (n + 1) * P)
                    if kind == "slot":
                        project_in(1, item[1])
                    elif kind == "turn":
                        turn_projected(1, item[1], turned % 2)
                        turned += 1
                    elif kind == "a_cum":
                        pe.wait_ge(S["da_ready"], 1)
                        o = free(pe, "a_cum")
                        da_ = dA.rearrange("p a b -> p (a b)")
                        mm(o[:, 0:32], upper, da_, start=True, stop=True)
                        close(mm(o[:, 32:64], ones, da_, start=True, stop=True), "a_cum")
                    elif kind == "ssd_front":
                        pe.wait_ge(S["ssm_silu"], 8)
                        turn(("x_tok", n), [xbc[:, i, tok] for i in range(4)])
                        turn(("b_tok", n), [xbc[:, 4 + g, tok] for g in range(2)])
                        for half in range(2):
                            pe.wait_ge(S["s_diag"], 2 * n + half + 1)
                            close(mm(free(pe, "a_row", n, half), ones, s_dg[:, half, :], start=True, stop=True),
                                  "a_row", n, half)
                        o = free(pe, "cb", n)
                        for g in range(2):
                            ins = mm(o[:, g * P:(g + 1) * P], xbc[:, 4 + g, tok], xbc[:, 6 + g, tok],
                                     start=True, stop=True)
                        close(ins, "cb", n)
                    else:
                        pe.wait_ge(S["s_m_ready"], n + 1)
                        pe.wait_ge(S["xdt_ready"], n + 1)
                        o = free(pe, "y_diag", n)
                        for hh in range(8):
                            c = slice(hh * 64, hh * 64 + 64)
                            ins = mm(o[:, c], s_m[:, n % 2, hh * P:(hh + 1) * P], xdt[:, n % 2, c], start=True, stop=True)
                        close(ins, "y_diag", n)
                        if n:
                            pe.wait_ge(S["s_new"], n)
                            o = free(pe, "y_off", n)
                            for g in range(2):
                                c = slice(g * 256, g * 256 + 256)
                                ins = mm(o[:, c], xbc[:, 6 + g, tok], s_state[:, n % 2, c], start=True, stop=True)
                            close(ins, "y_off", n)
                        if n < NT - 1:
                            drained(pe, "b_tok", n)
                            o = free(pe, "s_loc", n)
                            for g in range(2):
                                c = slice(g * 256, g * 256 + 256)
                                ins = mm(o[:, c], b_tok[:, n % 2, g * P:(g + 1) * P], xds[:, n % 2, c],
                                         start=True, stop=True)
                            close(ins, "s_loc", n)
                o = free(pe, "kk_sum")
                for f in range(4):
                    pe.wait_ge(S["kk_sq"], f + 1)
                    ins = mm(o[0:8, :], const("to_head")[:, 8 * f:8 * f + 8], b_s[:, f, :], start=(f == 0), stop=(f == 3))
                close(ins, "kk_sum")
                pe.wait_ge(S["tanh_done"], 1)
                pe.wait_ge(lora_in, 48)
                for f in range(4):
                    close(mm(free(pe, "decay", f), wa2[0:64, f * P:(f + 1) * P], raw[0:64, 12, 1:], start=True, stop=True),
                          "decay", f)
                    close(mm(free(pe, "a", f), wa2[64:128, f * P:(f + 1) * P], raw[64:128, 12, 1:], start=True, stop=True),
                          "a", f)
                pe.wait_ge(S["y_ssm_ready"], 1)
                for f in range(4):
                    turn(("y_ssm", f), [s_y[:, n, f * P:(f + 1) * P] for n in range(NT)])
                pe.wait_ge(S["kk_inverted"], 1)
                for f in range(4):
                    close(mm(free(pe, "kk_inv", f), const("from_head")[0:8, f * P:(f + 1) * P], rms_t[0:8, :],
                             start=True, stop=True), "kk_inv", f)
                pe.wait_ge(S["gd_sig"], 1)
                for n in range(NT):
                    close(mm(free(pe, "g_tok", n), raw[:, 13, 1 + n * P:1 + (n + 1) * P], g2, start=True, stop=True),
                          "g_tok", n)
                for f in range(4):
                    pe.wait_ge(S["tilde"], f + 1)
                    pe.wait_ge(S["tilde_kr"], f + 1)
                    for par in range(2):
                        r = slice(64 * par, 64 * par + 64)
                        o = free(pe, "sub", f, par)
                        for n in range(NT):
                            tok = slice(n * P, (n + 1) * P)
                            ins = mm(o[:, tok], kk_s[r, f, tok], b_s[r, f, tok], start=True, stop=True)
                        close(ins, "sub", f, par)
                    if f == 0:
                        for n in range(NT):
                            turn(("rv_tok", n), [raw[:, 8 + f, 1 + n * P:1 + (n + 1) * P] for f in range(4)])
                pe.wait_ge(S["rk_ready"], 4)
                o = free(pe, "bonus")
                heads = const("heads")
                for n in range(NT):
                    for f in range(4):
                        ins = mm(o[:, n * 8 + 2 * f:n * 8 + 2 * f + 2], mats_rk[:, f, n * P:(n + 1) * P], heads,
                                 start=True, stop=True)
                close(ins, "bonus")
                for item in rwkv_chunks():
                    kind, n = item[0], item[1]
                    tok = slice(n * P, (n + 1) * P)
                    rtok = slice(1 + n * P, 1 + (n + 1) * P)
                    if kind == "rk_tok":
                        turn(item, [raw[:, 4 + f, rtok] for f in range(4)])
                    elif kind == "rb_tok":
                        turn(item, [b_s[:, f, tok] for f in range(4)])
                    elif kind == "mats":
                        f, par = item[2], item[3]
                        r = slice(64 * par, 64 * par + 64)
                        o = free(pe, *item)
                        mm(o[:, 0:P], kk_s[r, f, tok], b_s[r, f, tok], start=True, stop=True)
                        mm(o[:, P:2 * P], raw[r, 4 + f, rtok], kk_s[r, f, tok], start=True, stop=True)
                        mm(o[:, 2 * P:3 * P], raw[r, 4 + f, rtok], raw[r, f, rtok], start=True, stop=True)
                        close(mm(o[:, 3 * P:4 * P], b_s[r, f, tok], raw[r, f, rtok], start=True, stop=True), *item)
                    elif kind == "pt":
                        level, half = item[2], item[3]
                        if level == 0 and half == 0:
                            for hh in range(8):
                                drained(pe, "mats", n, hh // 2, hh % 2)
                            pe.wait_ge(S["inv_filled"], n + 1)
                        if level:
                            drained(pe, "dt_", n, 0, half)
                        o = free(pe, *item)
                        for j in range(4):
                            hh = 4 * half + j
                            if level == 0:
                                ins = mm(o[:, j * P:(j + 1) * P], mats[:, hh, 0, :], inv_t[:, hh, :], start=True, stop=True)
                            else:
                                ins = mm(o[0:HALF, j * P:(j + 1) * P], mats[HALF:, hh, 0, 0:HALF],
                                         inv_t[HALF:, hh, :], start=True, stop=True)
                        close(ins, *item)
                    elif kind == "d":
                        half = item[2]
                        drained(pe, "pt", n, 0, half)
                        o = free(pe, *item)
                        for j in range(4):
                            hh = 4 * half + j
                            ins = mm(o[:, j * P:(j + 1) * P], inv_p[:, hh, :], inv_d[:, hh, :], start=True, stop=True)
                        close(ins, *item)
                    elif kind == "dt_":
                        level, half = item[2], item[3]
                        drained(pe, "pt", n, level, half)
                        if level:
                            drained(pe, "d", n, half)
                        o = free(pe, *item)
                        for j in range(4):
                            hh = 4 * half + j
                            if level == 0:
                                ins = mm(o[:, j * P:(j + 1) * P], inv_d[:, hh, :], inv_p[:, hh, :], start=True, stop=True)
                            else:
                                ins = mm(o[0:HALF, j * HALF:(j + 1) * HALF], inv_d[0:HALF, hh, 0:HALF],
                                         inv_q[0:HALF, hh, :], start=True, stop=True)
                        close(ins, *item)
                    elif kind == "rhs":
                        drained(pe, "rv_tok", n)
                        if n:
                            pe.wait_ge(S["s_rw_ready"], n)
                        o = free(pe, "rhs", n)
                        for f in range(4):
                            c = slice(f * P, (f + 1) * P)
                            if n:
                                mm(o[:, c], kk_s[:, f, tok], s_rw[:, n % 2, c], start=True, stop=True,
                                   skip_group_check=True)
                            for par in range(2):
                                hh = 2 * f + par
                                c = slice(hh * 64, hh * 64 + 64)
                                ins = mm(o[:, c], mats[:, hh, 1, :], v_tok[:, n, c], start=(n == 0), stop=True,
                                         skip_group_check=True)
                        close(ins, "rhs", n)
                    elif kind == "u":
                        for half in range(2):
                            drained(pe, "dt_", n, 1, half)
                        drained(pe, "rhs", n)
                        o = free(pe, "u", n)
                        for hh in range(8):
                            c = slice(hh * 64, hh * 64 + 64)
                            ins = mm(o[:, c], inv_t[:, hh, :], rhs_sb[:, c], start=True, stop=True)
                        close(ins, "u", n)
                    elif kind == "y":
                        drained(pe, "u", n)
                        o = free(pe, "y", n)
                        for f in range(4):
                            c = slice(f * P, (f + 1) * P)
                            if n:
                                mm(o[:, c], raw[:, f, rtok], s_rw[:, n % 2, c], start=True, stop=True,
                                   skip_group_check=True)
                            for par in range(2):
                                hh = 2 * f + par
                                c = slice(hh * 64, hh * 64 + 64)
                                mm(o[:, c], mats[:, hh, 2, :], v_tok[:, n, c], start=(n == 0), stop=True,
                                   skip_group_check=True)
                                ins = mm(o[:, c], mats[:, hh, 3, :], neg_u[:, c], start=False, stop=True,
                                         skip_group_check=True)
                        close(ins, "y", n)
                    else:
                        drained(pe, "rk_tok", n)
                        drained(pe, "rb_tok", n)
                        o = free(pe, "s_rw", n)
                        for f in range(4):
                            c = slice(f * P, (f + 1) * P)
                            mm(o[:, c], k_tok[:, n % 2, c], v_tok[:, n, c], start=True, stop=False)
                            ins = mm(o[:, c], bb_tok[:, n % 2, c], neg_u[:, c], start=False, stop=True)
                        close(ins, "s_rw", n)
                pe.wait_ge(S["y_rw_ready"], NT)
                for f in range(4):
                    turn(("y_rw", f), [y_rw[:, n, f * P:(f + 1) * P] for n in range(NT)])

            pe.wait_ge(ident_in, 16)
            pe.wait_ge(x_in, 16)
            for k in range(KT):
                turn(("x", k), [x_tok_in[:, n, k * P:(k + 1) * P] for n in range(NT)])
            for layer in range(2):
                norm(2 * layer)
                if layer == 0:
                    pe.wait_ge(stack_in, 16 * N_STACK)
                    for key, tile in (("stack_a", stage_a), ("stack_b", stage_b)):
                        close(nc.tensor.transpose(free(pe, key)[:, 0:P], tile, ident), key)
                    pe.wait_ge(main_in, 16)
                (even if layer == 0 else odd)()
                project_out(layer)
                norm(2 * layer + 1)
                mlp(layer)
            pe.wait_ge(summed, KT * 5)
            o = free(pe, "norm", 4)
            for t in range(NT):
                ins = mm(o[:, t:t + 1], rms_t[:, t * P:(t + 1) * P], ones[:, 0:1], start=True, stop=True)
            close(ins, "norm", 4)
            pe.wait_ge(normed, KT * 7)
            for t in range(NT):
                for half in range(2):
                    turn(("result", t, half), [y_mix[:, 4 * half + j, t * P:(t + 1) * P] for j in range(4)])

        @block.scalar
        def _(act):
            steps = [0]
            A = nc.scalar.activation

            def link(ins):
                steps[0] += 1
                ins.then_inc(act_step, 1)
                act.wait_ge(act_step, steps[0])

            def drain(dst, *key, src=None, scale=1.0):
                o = full(act, *key)
                A(dst, o if src is None else src, ACT.Copy, scale=scale).then_inc(free_sem(*key), 1)

            next_slot = [0]

            def high_part(n):
                A(w_hi[:, n % CUT], raw_w[:, n % RING], ACT.Copy).then_inc(w_high, 1)

            def cut_next():
                n = next_slot[0]
                if n == n_slots:
                    return
                next_slot[0] += 1
                act.wait_ge(w_full[n % RING], 16 * (n // RING + 1))
                if n >= CUT:
                    b, turn = slot_use[n - CUT]
                    act.wait_ge(bank_full[b], turn + 1)
                    act.wait_ge(w_cut, n - CUT + 1)
                high_part(n)

            def square(i, k):
                n = KT * i + k
                if k >= 2:
                    act.wait_ge(summed, n - 1)
                A(relu_t[:, k % 2, :], h[:, k, :], ACT.Square).then_inc(squared, 1)

            def norm(i):
                o = full(act, "norm", i)
                A(rms_t, o, ACT.Sqrt, scale=1.0 / D, bias=eps[:, 0:1]).then_inc(free_sem("norm", i), 1)

            def cut_normed():
                for k in range(KT):
                    act.wait_ge(scaled, k + 1)
                    A(hn_hi[:, k, :], relu_t[:, k % 2, :], ACT.Copy).then_inc(high, 1)

            def cut_mixed(turned):
                for f in range(4):
                    drained(act, turned, f)
                for k in range(KT):
                    A(hid_hi[:, k, :], y_mix[:, k, :], ACT.Copy).then_inc(high, 1)

            def high_gained(gain, j):
                k = j % KT
                A(hn_hi[:, k, :], h[:, k, :], ACT.Copy, scale=col_a(gain, j)).then_inc(high, 1)

            def project_out(layer):
                for k in range(KT):
                    cut_next()
                    drained(act, "out", layer, k)
                    square(2 * layer + 1, k)
                    high_gained("mlp_norm", 8 * layer + k)

            def mlp(layer):
                def hidden(i, j):
                    b, t0 = PLAN.at["mlp", layer, j]
                    act.wait_ge(bank_free[b], i * 2 + (t0 + 1))
                    A(relu_t[:, j % 2, :], relu_t[:, j % 2, :], ACT.Square).then_inc(hid_square, 1)
                    act.wait_ge(hid_square, i * 8 + (32 * layer + j + 1))
                    A(hid_hi[:, j, :], relu_t[:, j % 2, :], ACT.Copy).then_inc(hid_high, 1)

                b0 = base["mlp", layer]
                assert next_slot[0] == b0 + CUT
                with act.Fori(0, 3) as i:
                    for s in range(16):
                        n = b0 + s + CUT
                        b, t0 = PLAN.at["mlp", layer, s % 8]
                        act.wait_ge(w_full[n % RING], i * (16 * 16 // RING) + 16 * (n // RING + 1))
                        act.wait_ge(bank_full[b], i * 2 + (t0 + s // 8 + 1))
                        act.wait_ge(w_cut, i * 16 + (n - CUT + 1))
                        high_part(n)
                        if s < 8:
                            hidden(i, s)
                next_slot[0] += 48
                for s in range(16):
                    cut_next()
                    if s < 8:
                        hidden(3, s)
                    else:
                        b, t0 = PLAN.at["mlp", layer, s - 8]
                        act.wait_ge(bank_free[b], t0 + 8)
                        square(2 * layer + 2, s - 8)
                        if layer == 0:
                            high_gained("mix_norm", 8 + s - 8)

            for k in range(KT):
                drain(h[:, k, :], "x", k)

            cut_next()
            cut_next()
            for k in range(KT):
                drained(act, "x", k)
                square(0, k)
            act.wait_ge(main_in, 16)
            norm(0)
            for key, at, n in (("stack_a", 0, A_N), ("stack_b", A_N, B_N)):
                o = full(act, key)
                A(cols_t[:, at:at + n], o[:, 0:n], ACT.Copy).then_inc(free_sem(key), 1)
            cut_normed()

            def column_block(tile, j):
                return tile[:, :, j * P:(j + 1) * P]

            turned = 0
            f_count = 0

            def drain_feature(layer, key, buf):
                drain(f_tile[layer][:, buf, :], *key)

            for item in even_front():
                kind, u = item
                if kind == "slot":
                    key = EVEN_SLOTS[u][1]
                    if key[0] == "f":
                        drain_feature(0, key, f_count % 2)
                        f_count += 1
                    elif key[0] == "qk":
                        drain(conv_in[:, key[1], 3:], *key)
                    else:
                        drain(qk_raw[:, key[1] if key[0] == "q" else 4, :], *key)
                    cut_next()
                    if u == 7:
                        for i in range(4):
                            act.wait_ge(S["conv_ready"], i + 1)
                            A(conv_out[:, i, :], conv_out[:, i, :], ACT.Silu).then_inc(S["silu_done"], 1)
                elif kind == "turn" and u[0] == "v_att":
                    o = full(act, "v_att").rearrange("p (n g d) -> p n g d", n=NT, g=2)
                    for j in range(2):
                        for g in range(2):
                            ins = A(v_dup[:, 1:NT + 1, g, 64 * j:64 * j + 64], o[:, :, g, :], ACT.Copy)
                    ins.then_inc(free_sem("v_att"), 1)
                elif kind == "turn" and u[0] == "v":
                    drain(v_ml[:, :, u[1], 0:P], *u, src=bank(u).rearrange("p (n d) -> p n d", n=NT))
                elif kind == "turn" and u[0] == "o":
                    drain(column_block(o_gate, u[1]), *u, src=bank(u).rearrange("p (n d) -> p n d", n=NT))
                elif kind == "dup":
                    act.wait_ge(S["halo"], 3)
                    drain(k_dup[:, u, P:], "dup", u)
                elif kind == "att_exp":
                    b = u % 3
                    act.wait_ge(S["att_max"], u + 1)
                    for j in range(4):
                        A(att_p[b][:, j, :], att_p[b][:, j, :], ACT.Exp, bias=a_nm[:, b, j:j + 1],
                          accum_out=a_rs[:, b, j:j + 1])
                    A(a_es[:, b, :], a_se[:, b, :], ACT.Exp).then_inc(S["att_exp"], 1)
                elif kind == "att_turn":
                    for blk in range(2):
                        drain(att_pt[:, u % 2, blk, :], "turn", u, blk)
                elif kind == "att_out":
                    n, g = u // 2, u % 2
                    o = full(act, "att", u)
                    for par in range(2):
                        r = slice(64 * par, 64 * par + 64)
                        ins = A(y_mix[r, 2 * g:2 * g + 2, n * P:(n + 1) * P],
                                o[r, par * 256:par * 256 + 256].rearrange("p (a t) -> p a t", a=2), ACT.Copy)
                    ins.then_inc(free_sem("att", u), 1)
                elif kind == "soft":
                    act.wait_ge(S["soft_e"], 1)
                    link(A(af, af, ACT.Exp, scale=-1.0))
                    A(af, af, ACT.Ln, bias=1.0).then_inc(S["soft_l"], 1)
                elif kind == "m_exp":
                    act.wait_ge(S["m_ready"], 1)
                    for ap in (dfa, dfb, wi_arg, em_arg, wgt_arg):
                        ins = A(ap, ap, ACT.Exp)
                    ins.then_inc(S["mexp"], 1)
                elif kind == "w_exp":
                    act.wait_ge(S["wl_ready"], u + 1)
                    for j in range(4):
                        ins = A(w_ml[:, u, j, :], mtmp[:, u % 2, j * P:(j + 1) * P], ACT.Exp, bias=gg[:, u, j:j + 1])
                    ins.then_inc(S["n_keep"], 1)
            for a in range(2):
                drain(k_keep[:, a, :], "k_tok", a)
            for j in range(4):
                drained(act, "o", j)
            A(o_gate, o_gate, ACT.Sigmoid).then_inc(S["o_sig"], 1)

            def ml_root(n):
                act.wait_ge(S["hm_done"], n + 1)
                A(mv[:, 4 * n:4 * n + 4, 1], mv[:, 4 * n:4 * n + 4, 1], ACT.Sqrt, bias=eps[:, 1:2]).then_inc(S["ln_root"], 1)

            for n in range(NT):
                for a in range(2):
                    if n >= 2:
                        act.wait_ge(S["hm_done"], n - 1)
                    drain(n_sb[:, n % 2, a, :], "num", n, a, src=bank(("num", n, a))[:, 0:258])
                if n:
                    ml_root(n - 1)
            ml_root(NT - 1)
            for f in range(4):
                drain(y_mix[:, 4 + f, :], "y_ml", f)

            cut_mixed("y_ml")

            project_out(0)
            norm(1)
            mlp(0)
            norm(2)

            def ssm_squares(n):
                act.wait_ge(S["z_silu"], n + 1)
                for g in range(2):
                    link(A(z_tok[:, n, g * 256:(g + 1) * 256], s_y[:, n, g * 256:(g + 1) * 256], ACT.Square,
                           accum_out=gss[:, 2 * n + g:2 * n + g + 1]))

            f_count = 0
            for item in odd_front():
                kind = item[0]
                if kind == "slot":
                    key = ODD_SLOTS[item[1]][1]
                    if key[0] == "f":
                        drain_feature(1, key, f_count % 2)
                        f_count += 1
                    elif key[0] == "xbc":
                        drain(xbc_in[:, key[1], 3:], *key)
                    else:
                        drain(raw[:, key[1], 1:], *key)
                    cut_next()
                    if item[1] == 17:
                        act.wait_ge(S["mixed"], 2)
                        A(raw[0:64, 12, 1:], raw[0:64, 12, 1:], ACT.Tanh).then_inc(S["tanh_done"], 1)
                        A(raw[:, 13, 1:], raw[:, 13, 1:], ACT.Sigmoid).then_inc(S["gd_sig"], 1)
                    if item[1] == 10:
                        for i in range(8):
                            act.wait_ge(S["ssm_conv"], i + 1)
                            A(xbc[:, i, :], xbc[:, i, :], ACT.Silu).then_inc(S["ssm_silu"], 1)
                elif kind == "turn" and item[1][0] == "z":
                    key = item[1]
                    o = full(act, *key).rearrange("p (n d) -> p n d", n=NT)
                    A(column_block(z_tok, key[1]), o, ACT.Silu).then_inc(free_sem(*key), 1)
                    if key[1] == 2:
                        act.wait_ge(rows_in, 16 * len(ROWS))
                        A(expa, row("ssm_a_log", 8), ACT.Exp)
                        act.wait_ge(S["s_soft_e"], 1)
                        link(A(dta, dta, ACT.Exp, scale=-1.0))
                        A(dta, dta, ACT.Ln, bias=1.0).then_inc(S["s_soft_l"], 1)
                elif kind == "a_cum":
                    act.wait_ge(S["acum_args"], 1)
                    A(ea, acum[:, 0, :], ACT.Exp)
                    A(dec, acum[:, 1, :], ACT.Exp)
                    A(ds_, dsx, ACT.Exp).then_inc(S["acum_exps"], 1)
                elif kind == "ssd_front":
                    n = item[1]
                    if n >= 2:
                        act.wait_ge(S["s_yprod"], n - 1)
                        full(act, "s_loc", n - 2)
                    drain(xs_tok[:, n % 2, :], "x_tok", n)
                    drain(b_tok[:, n % 2, :], "b_tok", n, src=bank(("b_tok", n))[:, 0:256])
                    for half in range(2):
                        act.wait_ge(S["s_masked"], 2 * n + half + 1)
                        for j in range(4):
                            c = 8 * n + 4 * half + j
                            ins = A(s_w[:, half, j * P:(j + 1) * P], s_t[:, half, j * P:(j + 1) * P], ACT.Exp,
                                    bias=nacum[:, c:c + 1])
                        ins.then_inc(S["s_decay"], 1)
                    if n:
                        ssm_squares(n - 1)
            act.wait_ge(S["mixed"], 6)
            for f in range(4):
                A(kk_s[:, f, :], raw[:, 4 + f, 1:], ACT.Copy, scale=col_b("rw_k_k", f)).then_inc(S["kkraw"], 1)
                act.wait_ge(S["kkraw"], f + 1)
                A(b_s[:, f, :], kk_s[:, f, :], ACT.Square).then_inc(S["kk_sq"], 1)
            ssm_squares(NT - 1)
            A(gss, gss, ACT.Sqrt, scale=1.0 / 256, bias=eps[:, 0:1]).then_inc(S["s_root"], 1)
            act.wait_ge(S["mixed"], 14)
            o = full(act, "kk_sum")
            A(rms_t[0:8, :], o[0:8, :], ACT.Sqrt).then_inc(free_sem("kk_sum"), 1)
            def ln_root(n):
                act.wait_ge(S["ln2_var"], n + 1)
                A(lnv[:, n, :], lnv[:, n, :], ACT.Sqrt, scale=1.0 / 64, bias=eps[:, 2:3]).then_inc(S["ln2_root"], 1)

            def sub_blocks(f, par):
                o = full(act, "sub", f, par).rearrange("p (n s) -> p n s", n=NT)
                for q in range(P // SUB):
                    rows = slice(q * SUB, (q + 1) * SUB)
                    ins = A(sub_tok[rows, :, 2 * f + par::8].rearrange("p s n -> p n s"), o[rows, :, rows], ACT.Copy,
                            scale=-1.0)
                ins.then_inc(free_sem("sub", f, par), 1)

            act.wait_ge(S["omka_ready"], 1)
            for f in range(4):
                o = full(act, "decay", f)
                A(decay_s[:, f, :], o, ACT.Sigmoid, bias=col_b("rw_w0", f)).then_inc(free_sem("decay", f), 1)
                o = full(act, "a", f)
                A(a_s[:, f, :], o, ACT.Sigmoid, bias=col_b("rw_a0", f)).then_inc(free_sem("a", f), 1)
                drained(act, "a", f)
                A(k_gain[:, f, :], a_s[:, f, :], ACT.Identity, scale=col_b("rw_k_a", f), bias=omka[:, f:f + 1]
                  ).then_inc(S["k_gained"], 1)
            for f in range(4):
                b = f % 2
                if f >= 2:
                    act.wait_ge(S["tilde_kr"], f - 1)
                act.wait_ge(S["cum_args"], f + 1)
                A(cum_exp[:, b, :], cum_now[:, b, :], ACT.Exp, scale=-DECAY_K)
                A(cum_before[:, b, :], cum_before[:, b, :], ACT.Exp, scale=-DECAY_K)
                A(cum_now[:, b, :], cum_now[:, b, :], ACT.Exp, scale=DECAY_K).then_inc(S["cum_exps"], 1)
                if f == 0:
                    for i in range(4):
                        drain(y_mix[:, i, :], "y_ssm", i)
                if f == 1:
                    for n in range(NT):
                        drain(g_tok[:, n, :], "g_tok", n)
                if f == 2:
                    sub_blocks(0, 0)
                    sub_blocks(0, 1)
                    for n in range(NT):
                        drain(v_tok[:, n, :], "rv_tok", n)
            A(e_s, e_a, ACT.Exp, scale=-DECAY_K).then_inc(S["scales"], 1)
            for f in range(1, 4):
                sub_blocks(f, 0)
                if f < 3:
                    sub_blocks(f, 1)
            def turned(n):
                if n >= 2:
                    full(act, "s_rw", n - 2)
                drain(k_tok[:, n % 2, :], "rk_tok", n)
                drain(bb_tok[:, n % 2, :], "rb_tok", n)

            def fill_inverses(n):
                act.wait_ge(S["inv_zero"], n + 1)
                for src, dst in ((inv_rows, inv_d), (inv_cols, inv_t)):
                    for q in range(P // SUB):
                        rows = slice(q * SUB, (q + 1) * SUB)
                        ins = A(dst[rows, :, rows], src[rows, :, n * 8:n * 8 + 8].rearrange("p c j -> p j c"), ACT.Copy)
                ins.then_inc(S["inv_filled"], 1)

            act.wait_ge(S["sub_turned"], 1)
            turned(0)
            for n in range(NT):
                fill_inverses(n)
                for half in range(2):
                    hs = slice(4 * half, 4 * half + 4)
                    o = full(act, "pt", n, 1, half)[0:HALF, :].rearrange("p (a t) -> p a t", a=4)
                    A(inv_q[0:HALF, hs, :], o[:, :, HALF:], ACT.Copy).then_inc(free_sem("pt", n, 1, half), 1)
                for half in range(2):
                    hs = slice(4 * half, 4 * half + 4)
                    o = full(act, "dt_", n, 1, half)[0:HALF, 0:4 * HALF].rearrange("p (a t) -> p a t", a=4)
                    A(inv_t[0:HALF, hs, HALF:], o, ACT.Copy, scale=-1.0).then_inc(free_sem("dt_", n, 1, half), 1)
                drain(rhs_sb, "rhs", n)
                if n:
                    ln_root(n - 1)
                if n + 1 < NT:
                    turned(n + 1)
                if n:
                    full(act, "s_rw", n - 1)
                drain(neg_u, "u", n, scale=-1.0)
                drain(y_rw[:, n, :], "y", n)
            ln_root(NT - 1)
            for f in range(4):
                drain(y_mix[:, 4 + f, :], "y_rw", f)
            cut_mixed("y_rw")
            project_out(1)
            norm(3)
            mlp(1)
            o = full(act, "norm", 4)
            A(token_root, o[:, 0:NT], ACT.Sqrt, scale=1.0 / D, bias=eps[:, 0:1]).then_inc(free_sem("norm", 4), 1)
            act.wait_ge(S["root_inverted"], 1)
            for t in range(NT):
                o = full(act, "result", t, 0)
                A(arena[:, t * D:t * D + 512], o, ACT.Copy, scale=token_root[:, t:t + 1]).then_inc(S["x_out"], 1)

        @block.vector
        def _(dve):
            steps = [0]
            V = nc.vector

            def link(ins):
                steps[0] += 1
                ins.then_inc(dve_step, 1)
                dve.wait_ge(dve_step, steps[0])

            def sum_squares(i, k):
                n = KT * i + k
                dve.wait_ge(squared, n + 1)
                if k:
                    dve.wait_ge(summed, n)
                    V.tensor_tensor(rms_t, rms_t, relu_t[:, k % 2, :], ALU.add).then_inc(summed, 1)
                else:
                    V.tensor_copy(rms_t, relu_t[:, k % 2, :]).then_inc(summed, 1)

            def norm(i):
                drained(dve, "norm", i)
                link(V.reciprocal(rms_t, rms_t))
                if i == 0:
                    drained(dve, "stack_a")
                    drained(dve, "stack_b")
                    dve.wait_ge(main_in, 16)
                if i:
                    return
                for k in range(KT):
                    if k >= 2:
                        low(i, k - 2)
                    V.scalar_tensor_tensor(out=relu_t[:, k % 2, :], in0=h[:, k, :], scalar=col_a("mix_norm", k),
                                           in1=rms_t, op0=ALU.mult, op1=ALU.mult
                                           ).then_inc(scaled, 1)
                low(i, KT - 2)
                low(i, KT - 1)

            def low(i, k):
                phase = [0, 2, 3, 5][i]
                dve.wait_ge(high, KT * phase + k + 1)
                V.tensor_tensor(hn_lo[:, k, :], relu_t[:, k % 2, :], hn_hi[:, k, :].bitcast(F32), ALU.subtract
                                ).then_inc(normed, 1)
                dve.wait_ge(normed, KT * phase + k + 1)

            def low_mixed(layer):
                for k in range(KT):
                    dve.wait_ge(high, KT * (3 * layer + 1) + k + 1)
                    V.tensor_tensor(hid_lo[:, k, :], y_mix[:, k, :], hid_hi[:, k, :].bitcast(F32), ALU.subtract
                                    ).then_inc(normed, 1)

            def low_gained(phase, gain, j):
                k = j % KT
                dve.wait_ge(high, KT * phase + k + 1)
                V.scalar_tensor_tensor(out=hn_lo[:, k, :], in0=h[:, k, :], scalar=col_a(gain, j),
                                       in1=hn_hi[:, k, :].bitcast(F32), op0=ALU.mult, op1=ALU.subtract
                                       ).then_inc(normed, 1)

            def project_out(layer):
                low_mixed(layer)
                for k in range(KT):
                    o = full(dve, "out", layer, k)
                    V.tensor_tensor(h[:, k, :], h[:, k, :], o, ALU.add).then_inc(free_sem("out", layer, k), 1)
                    if k:
                        sum_squares(2 * layer + 1, k - 1)
                        low_gained(3 * layer + 2, "mlp_norm", 8 * layer + k - 1)
                sum_squares(2 * layer + 1, KT - 1)
                low_gained(3 * layer + 2, "mlp_norm", 8 * layer + KT - 1)

            def mlp(layer):
                def hidden(i):
                    for j in range(8):
                        b, t0 = PLAN.at["mlp", layer, j]
                        dve.wait_ge(bank_full[b], i * 2 + (t0 + 1))
                        V.scalar_tensor_tensor(out=relu_t[:, j % 2, :], in0=ps[:, b, :], scalar=0.0, in1=rms_t,
                                               op0=ALU.max, op1=ALU.mult).then_inc(bank_free[b], 1)
                        dve.wait_ge(hid_high, i * 8 + (32 * layer + j + 1))
                        V.tensor_tensor(hid_lo[:, j, :], relu_t[:, j % 2, :], hid_hi[:, j, :].bitcast(F32), ALU.subtract
                                        ).then_inc(hid_ready, 1)
                        dve.wait_ge(hid_ready, i * 8 + (32 * layer + j + 1))

                def add(i, j):
                    b, t0 = PLAN.at["mlp", layer, j]
                    dve.wait_ge(bank_full[b], i * 2 + (t0 + 2))
                    V.tensor_tensor(h[:, j, :], h[:, j, :], ps[:, b, :], ALU.add).then_inc(bank_free[b], 1)

                dve.wait_ge(summed, KT * (2 * layer + 2))
                def final(j):
                    sum_squares(2 * layer + 2, j)
                    if layer == 0:
                        low_gained(3, "mix_norm", 8 + j)
                    else:
                        V.tensor_scalar(y_mix[:, j, :], h[:, j, :], col_a("final_norm", j), None, ALU.mult
                                        ).then_inc(normed, 1)

                with dve.Fori(0, 3) as i:
                    hidden(i)
                    for j in range(8):
                        add(i, j)
                hidden(3)
                for j in range(8):
                    add(3, j)
                    if j:
                        final(j - 1)
                final(KT - 1)

            def conv(dst, src, w, b, i, tiles, signal):
                link(V.tensor_scalar(dst, src[:, 0:T], col_a(w, i), col_a(b, i), ALU.mult, ALU.add))
                for tap in range(1, 4):
                    ins = V.scalar_tensor_tensor(out=dst, in0=src[:, tap:tap + T], scalar=col_a(w, tap * tiles + i),
                                                 in1=dst, op0=ALU.mult, op1=ALU.add)
                    if tap < 3:
                        link(ins)
                    else:
                        ins.then_inc(signal, 1)

            drained(dve, "x", KT - 1)
            for k in range(KT):
                sum_squares(0, k)
            norm(0)
            V.memset(k_dup[:, :, 0:P], 0.0).then_inc(S["halo"], 1)
            V.memset(v_dup[:, 0, :, :], 0.0).then_inc(S["halo"], 1)
            V.memset(conv_in[:, :, 0:3], 0.0).then_inc(S["halo"], 1)
            V.memset(v_ml[:, :, :, 128:129], 1.0).then_inc(S["v_ones"], 1)
            dve.wait_ge(rows_in, 16 * len(ROWS))
            g_ps = full(dve, "gates").rearrange("p (n c) -> p n c", n=NT)[:, :, P - 8:]
            link(V.tensor_tensor(li, g_ps[:, :, 0:4], over(row("ml_i_bias", 4), 1, NT), ALU.add))
            V.tensor_tensor(fg, g_ps[:, :, 4:8], over(row("ml_f_bias", 4), 1, NT), ALU.add).then_inc(free_sem("gates"), 1)
            drained(dve, "gates")
            V.scalar_tensor_tensor(out=af, in0=fg, scalar=-1.0, in1=fg, op0=ALU.mult, op1=ALU.max
                                   ).then_inc(S["soft_e"], 1)
            dve.wait_ge(S["halo"], 3)
            for i in range(4):
                drained(dve, "qk", i)
                conv(conv_out[:, i, :], conv_in[:, i, :], "ml_conv_w", "ml_conv_b", i, 4, S["conv_ready"])
            dve.wait_ge(S["soft_l"], 1)
            V.scalar_tensor_tensor(out=lf, in0=fg, scalar=0.0, in1=af, op0=ALU.min, op1=ALU.subtract
                                   ).then_inc(S["lf_ready"], 1)
            o = full(dve, "cum", 0)
            V.tensor_copy(cumb, o[:, 0:32].rearrange("p (a b) -> p a b", a=2)).then_inc(free_sem("cum", 0), 1)
            drained(dve, "cum", 0)
            b_ = cumb[:, 0, :].rearrange("p (n c) -> p n c", n=NT)
            bl = cumb[:, 1, :].rearrange("p (n c) -> p n c", n=NT)
            link(V.tensor_tensor(gg, li, b_, ALU.subtract))

            def diag(dst, col, signal):
                V.tensor_tensor(dst.rearrange("p (a t) -> p a t", a=4), over(ident, 1, 4), over(col, 2, P), ALU.mult
                                ).then_inc(signal, 1)

            dve.wait_ge(S["conv_ready"], 4)
            for n in range(2):
                diag(dg[:, n % 2, :], gg[:, n, :], S["g_diag"])

            def gate_maxima(n):
                o = full(dve, "g_row", n).rearrange("p (a t) -> p a t", a=4)
                link(V.tensor_reduce(gmax[:, n, :], o, AX.X, ALU.max))
                V.tensor_tensor(mtmp[:, n % 2, :].rearrange("p (a t) -> p a t", a=4), o, over(const("add_ts"), 1, 4),
                                ALU.add).then_inc(free_sem("g_row", n), 1)
                drained(dve, "g_row", n)
                link(V.tensor_reduce(cmx[:, n, :], mtmp[:, n % 2, :].rearrange("p (a t) -> p a t", a=4), AX.X, ALU.max))
                if n + 2 < NT:
                    diag(dg[:, n % 2, :], gg[:, n + 2, :], S["g_diag"])

            mm_ = mm

            def maxima_tables():
                link(V.memset(marr[:, 0, :], 0.0))
                for n in range(NT):
                    link(V.tensor_tensor(mx[:, n, :], marr[:, n, :], gmax[:, n, :], ALU.max))
                    if n < NT - 1:
                        link(V.tensor_tensor(marr[:, n + 1, :], bl[:, n, :], mx[:, n, :], ALU.add))
                link(V.tensor_tensor(mm_, marr, cmx, ALU.max))
                V.tensor_tensor(dfa, marr, mx, ALU.subtract)
                V.tensor_tensor(dfb, gmax, mx, ALU.subtract)
                V.tensor_tensor(wi_arg, marr, mm_, ALU.subtract)
                V.tensor_tensor(wgt_arg, gg, gmax, ALU.subtract)
                link(V.tensor_tensor(em_arg, b_, mm_, ALU.add))
                V.tensor_scalar(em_arg, em_arg, -1.0, None, ALU.mult).then_inc(S["m_ready"], 1)
                for n in range(2):
                    diag(dg[:, n % 2, :], mm_[:, n, :], S["m_diag"])

            def weight_exponents(n):
                o = full(dve, "m_row", n).rearrange("p (a t) -> p a t", a=4)
                if n >= 2:
                    dve.wait_ge(S["n_keep"], n - 1)
                V.tensor_tensor(mtmp[:, n % 2, :].rearrange("p (a t) -> p a t", a=4), over(const("add_st"), 1, 4), o,
                                ALU.subtract).then_inc(free_sem("m_row", n), 1)
                drained(dve, "m_row", n)
                dve.sem_inc(S["wl_ready"], 1)
                if n + 2 < NT:
                    diag(dg[:, n % 2, :], mm_[:, n + 2, :], S["m_diag"])

            dve.wait_ge(even_in, 16)
            cos, sin = even_const("cos"), even_const("sin")
            for i in (4, 0, 1, 2, 3):
                dst = q_rot[:, i, :] if i < 4 else k_rot
                drained(dve, *(("q", i) if i < 4 else ("k",)))
                o = full(dve, "rope", i)
                V.tensor_tensor(relu_t[:, i % 2, :], o, sin, ALU.mult).then_inc(free_sem("rope", i), 1)
                link(V.tensor_tensor(dst, qk_raw[:, i, :], cos, ALU.mult))
                drained(dve, "rope", i)
                V.tensor_tensor(dst, dst, relu_t[:, i % 2, :], ALU.add).then_inc(S["rope_done"], 1)
            sinks = row("att_sinks", 8)
            band, first = even_const("band"), even_const("first")

            def att_scores(u):
                n, g = u // 2, u % 2
                b = u % 3
                if u == 2:
                    dve.wait_ge(S["rope_done"], 5)
                if u >= 3:
                    full(dve, "turn", u - 3, 0)
                    full(dve, "turn", u - 3, 1)
                for par in range(2):
                    o = full(dve, "score", u, par).rearrange("p (a k) -> p a k", a=2)
                    V.scalar_tensor_tensor(out=att_p[b][:, 2 * par:2 * par + 2, :], in0=o, scalar=0.125,
                                           in1=over(band if n else first, 1, 2), op0=ALU.mult, op1=ALU.add
                                           ).then_inc(free_sem("score", u, par), 1)
                drained(dve, "score", u, 0)
                drained(dve, "score", u, 1)
                sk = sinks[:, 4 * g:4 * g + 4].rearrange("p (a par) -> p par a", par=2)
                v2 = lambda ap: ap.rearrange("p (par a) -> p par a", par=2)
                link(V.tensor_reduce(a_mx[:, b, :], att_p[b], AX.X, ALU.max))
                link(V.tensor_tensor(v2(a_mx[:, b, :]), v2(a_mx[:, b, :]), sk, ALU.max))
                link(V.tensor_scalar(a_nm[:, b, :], a_mx[:, b, :], -1.0, None, ALU.mult))
                V.tensor_tensor(v2(a_se[:, b, :]), v2(a_nm[:, b, :]), sk, ALU.add).then_inc(S["att_max"], 1)

            def att_norm(u):
                b = u % 3
                dve.wait_ge(S["att_exp"], u + 1)
                link(V.tensor_tensor(a_l[:, b, :], a_rs[:, b, :], a_es[:, b, :], ALU.add))
                link(V.reciprocal(a_l[:, b, :], a_l[:, b, :]))
                V.tensor_tensor(att_p[b], att_p[b], over(a_l[:, b, :], 2, 256), ALU.mult
                                ).then_inc(S["att_probs"], 1)

            for u in range(9):
                if u < 8:
                    att_scores(u)
                if u:
                    att_norm(u - 1)
                if u < 4:
                    gate_maxima(u)
                if u == 4:
                    maxima_tables()
                if u in (5, 6):
                    weight_exponents(u - 5)
            weight_exponents(2)
            weight_exponents(3)
            full(dve, "att", 7)
            dve.wait_ge(S["mexp"], 1)
            for a in range(2):
                drained(dve, "k_tok", a)
            kk4 = k_keep.rearrange("p a (n f) -> p n a f", n=NT)
            for n in range(NT):
                for a in range(2):
                    ins = V.scalar_tensor_tensor(
                        out=k_w[:, n, a * P:(a + 1) * P].rearrange("p (b d) -> p b d", b=2),
                        in0=kk4[:, n, a, :].rearrange("p (b d) -> p b d", b=2), scalar=0.125,
                        in1=over(wgt_arg[:, n, 2 * a:2 * a + 2], 2, 64), op0=ALU.mult, op1=ALU.mult)
                    if a == 0:
                        link(ins)
                    else:
                        ins.then_inc(S["k_scaled"], 1)
            def ml_out(n):
                dve.wait_ge(S["ln_root"], n + 1)
                root = mv[:, 4 * n:4 * n + 4, 1]
                link(V.reciprocal(root, root))
                for hh in range(4):
                    j = 4 * n + hh
                    ins = V.tensor_scalar(w_ml[:, n, hh, :], w_ml[:, n, hh, :], mv[:, j, 0:1], mv[:, j, 1:2],
                                          ALU.subtract, ALU.mult)
                link(ins)
                V.tensor_tensor(o_gate[:, n, :], o_gate[:, n, :], w_ml[:, n].rearrange("p h t -> p (h t)"), ALU.mult
                                ).then_inc(S["y_ml_ready"], 1)

            def ml_weights(n):
                dve.wait_ge(S["n_keep"], n + 1)
                for par in range(2):
                    o = full(dve, "qk_st", n, par)[:, 0:256].rearrange("p (a t) -> p a t", a=2)
                    wv = w_ml[:, n].rearrange("p (a b) t -> p b a t", b=2)[:, par]
                    qv = qkw[:, n % 2, :].rearrange("p (a b t) -> p b a t", a=2, b=2)[:, par]
                    if n >= 2 and par == 0:
                        full(dve, "num", n - 2, 1)
                    V.scalar_tensor_tensor(out=qv, in0=o, scalar=0.125, in1=wv, op0=ALU.mult, op1=ALU.mult
                                           ).then_inc(free_sem("qk_st", n, par), 1)
                drained(dve, "qk_st", n, 0)
                drained(dve, "qk_st", n, 1)
                dve.sem_inc(S["qkw_ready"], 1)
                if n < NT - 1:
                    heads = [(a, par, slice(64 * par, 64 * par + 64)) for a in range(2) for par in range(2)]
                    if n:
                        for a, par, r in heads:
                            ins = V.tensor_scalar(c_tmp[r, a, :], c_state[r, n, a, :],
                                                  dfa[r, n, 2 * a + par:2 * a + par + 1], None, ALU.mult)
                        link(ins)
                    for a, par, r in heads:
                        o = full(dve, "c_loc", n, a)[r, 129 * par:129 * (par + 1)]
                        dst, gain = c_state[r, n + 1, a, :], dfb[r, n, 2 * a + par:2 * a + par + 1]
                        if n:
                            ins = V.scalar_tensor_tensor(out=dst, in0=o, scalar=gain, in1=c_tmp[r, a, :],
                                                         op0=ALU.mult, op1=ALU.add)
                        else:
                            ins = V.tensor_scalar(dst, o, gain, None, ALU.mult)
                        if par:
                            ins.then_inc(free_sem("c_loc", n, a), 1)
                    drained(dve, "c_loc", n, 0)
                    drained(dve, "c_loc", n, 1)
                    dve.sem_inc(S["c_ready"], 1)

            def ml_combine(n):
                drained(dve, "num", n, 0)
                drained(dve, "num", n, 1)
                nn = n_sb[:, n % 2].rearrange("p a (b v) -> p a b v", b=2)
                if n:
                    for par in range(2):
                        o = full(dve, "inter", n, par)[:, 0:258].rearrange("p (a v) -> p a v", a=2)
                        for a in range(2):
                            hh = 2 * a + par
                            ins = V.scalar_tensor_tensor(out=nn[:, a, par, :], in0=o[:, a, :],
                                                         scalar=wi_arg[:, n, hh:hh + 1], in1=nn[:, a, par, :],
                                                         op0=ALU.mult, op1=ALU.add)
                            if a:
                                ins.then_inc(free_sem("inter", n, par), 1)
                    drained(dve, "inter", n, 0)
                    drained(dve, "inter", n, 1)
                den = nn[:, :, :, 128:129].rearrange("p a b v -> p a (b v)")
                d2 = dn[:, n % 2, :].rearrange("p (a b) -> p a b", a=2)
                em = em_arg[:, n, :].rearrange("p (a b) -> p a b", a=2)
                link(V.tensor_scalar(d2, den, -1.0, None, ALU.mult))
                link(V.tensor_tensor(d2, d2, den, ALU.max))
                link(V.tensor_tensor(d2, d2, em, ALU.max))
                link(V.reciprocal(dn[:, n % 2, :], dn[:, n % 2, :]))
                for hh in range(4):
                    ins = V.tensor_scalar(w_ml[:, n, hh, :], nn[:, hh // 2, hh % 2, 0:P], dn[:, n % 2, hh:hh + 1], None,
                                          ALU.mult)
                link(ins)
                for hh in range(4):
                    ins = V.bn_stats(st6[:, hh, :], w_ml[:, n, hh, :])
                link(ins)
                for hh in range(4):
                    ins = V.bn_aggr(mv[:, 4 * n + hh, :], st6[:, hh, :])
                ins.then_inc(S["hm_done"], 1)
                dve.wait_ge(S["hm_done"], n + 1)

            ml_weights(0)
            for n in range(NT):
                if n + 1 < NT:
                    ml_weights(n + 1)
                if n == 1:
                    dve.wait_ge(S["o_sig"], 1)
                    link(V.tensor_tensor(o_gate, o_gate, over(row("ml_norm", 512), 1, NT), ALU.mult))
                ml_combine(n)
                if n:
                    ml_out(n - 1)
            ml_out(NT - 1)
            project_out(0)
            norm(1)
            mlp(0)
            norm(2)

            V.memset(xbc_in[:, :, 0:3], 0.0).then_inc(S["halo"], 1)
            V.memset(raw[:, :, 0:1], 0.0).then_inc(S["halo"], 1)
            def scale_projected(ap, *key):
                drained(dve, *key)
                return V.tensor_tensor(ap, ap, rms_t, ALU.mult)

            def scale_feature_tile(key):
                j = SCALED_TILES.index(key)
                scale_projected(f_tile[1][:, j % 2, :], "f", *key).then_inc(S["f_scaled"], 1)

            scale_feature_tile(("dt",))
            d_ps = full(dve, "dt").rearrange("p (n c) -> p n c", n=NT)[:, :, 0:8]
            V.tensor_tensor(dtr, d_ps, over(row("ssm_dt_bias", 8), 1, NT), ALU.add).then_inc(free_sem("dt"), 1)
            drained(dve, "dt")
            V.scalar_tensor_tensor(out=dta, in0=dtr, scalar=-1.0, in1=dtr, op0=ALU.mult, op1=ALU.max
                                   ).then_inc(S["s_soft_e"], 1)
            dve.wait_ge(S["halo"], 5)
            for i in range(8):
                link(scale_projected(xbc_in[:, i, 3:], "xbc", i))
                conv(xbc[:, i, :], xbc_in[:, i, :], "ssm_conv_w", "ssm_conv_b", i, 8, S["ssm_conv"])
            for j in range(4):
                scale_feature_tile(("z", j))
            dve.wait_ge(S["s_soft_l"], 1)
            link(V.scalar_tensor_tensor(out=dtt, in0=dtr, scalar=0.0, in1=dta, op0=ALU.max, op1=ALU.add))
            V.scalar_tensor_tensor(out=dA, in0=dtt, scalar=-1.0, in1=over(expa, 1, NT), op0=ALU.mult, op1=ALU.mult
                                   ).then_inc(S["da_ready"], 1)
            o = full(dve, "a_cum")
            V.tensor_copy(acum, o[:, 0:64].rearrange("p (a b) -> p a b", a=2)).then_inc(free_sem("a_cum"), 1)
            drained(dve, "a_cum")
            link(V.tensor_tensor(dsx, acum[:, 1, :], acum[:, 0, :], ALU.subtract))
            V.tensor_scalar(nacum, acum[:, 0, :], -1.0, None, ALU.mult).then_inc(S["acum_args"], 1)
            dve.wait_ge(S["acum_exps"], 1)
            a4 = acum[:, 0, :].rearrange("p (n b c) -> p n b c", n=NT, b=2)
            h8 = lambda ap: ap.rearrange("p (c d) -> p c d", d=64)

            def ssd_front(n):
                b = n % 2
                for half in range(2):
                    diag(s_dg[:, half, :], a4[:, n, half, :], S["s_diag"])
                for half in range(2):
                    o = full(dve, "a_row", n, half).rearrange("p (a t) -> p a t", a=4)
                    V.tensor_tensor(s_t[:, half, :].rearrange("p (a t) -> p a t", a=4), o, over(const("add_st"), 1, 4),
                                    ALU.add).then_inc(free_sem("a_row", n, half), 1)
                    drained(dve, "a_row", n, half)
                    dve.sem_inc(S["s_masked"], 1)
                drained(dve, "x_tok", n)
                dt_n = dtt[:, n, :]
                if n >= 2:
                    full(dve, "y_diag", n - 2)
                    full(dve, "s_loc", n - 2)
                link(V.tensor_tensor(h8(xdt[:, b, :]), h8(xs_tok[:, b, :]), over(dt_n, 2, 64), ALU.mult))
                V.tensor_tensor(h8(xds[:, b, :]), h8(xdt[:, b, :]), over(ds_[:, 8 * n:8 * n + 8], 2, 64), ALU.mult
                                ).then_inc(S["xdt_ready"], 1)
                o = full(dve, "cb", n)[:, 0:256].rearrange("p (g t) -> p g t", g=2)
                for half in range(2):
                    dve.wait_ge(S["s_decay"], 2 * n + half + 1)
                    ins = V.tensor_tensor(s_m[:, b, half * 512:(half + 1) * 512].rearrange("p (a t) -> p a t", a=4),
                                          s_w[:, half, :].rearrange("p (a t) -> p a t", a=4), over(o[:, half, :], 1, 4),
                                          ALU.mult)
                    if half == 0:
                        link(ins)
                    else:
                        ins.then_inc(free_sem("cb", n), 1)
                drained(dve, "cb", n)
                dve.sem_inc(S["s_m_ready"], 1)

            mixed = [0]

            def shift(i):
                link(scale_projected(raw[:, i, 1:], "rw", i))
                mixed[0] += 1
                link(V.tensor_tensor(relu_t[:, 1, :], raw[:, i, 0:T], raw[:, i, 1:], ALU.subtract))
                V.scalar_tensor_tensor(out=raw[:, i, 1:], in0=relu_t[:, 1, :], scalar=col_b("rw_mu", i),
                                             in1=raw[:, i, 1:], op0=ALU.mult, op1=ALU.add).then_inc(S["mixed"], 1)
                dve.wait_ge(S["mixed"], mixed[0])

            def ssd_back(n):
                b = n % 2
                y = s_y[:, n, :]
                link(V.tensor_tensor(h8(y), h8(xs_tok[:, b, :]), over(row("ssm_d", 8), 2, 64), ALU.mult))
                o = full(dve, "y_diag", n)
                V.tensor_tensor(y, y, o, ALU.add).then_inc(free_sem("y_diag", n), 1)
                drained(dve, "y_diag", n)
                if n:
                    o = full(dve, "y_off", n)
                    V.tensor_tensor(h8(relu_t[:, 0, :]), h8(o), over(ea[:, 8 * n:8 * n + 8], 2, 64), ALU.mult
                                    ).then_inc(free_sem("y_off", n), 1)
                    drained(dve, "y_off", n)
                    link(V.tensor_tensor(y, y, relu_t[:, 0, :], ALU.add))
                if n == 0:
                    for j in range(4):
                        drained(dve, "z", j)
                V.tensor_tensor(y, y, z_tok[:, n, :], ALU.mult).then_inc(S["z_silu"], 1)
                dve.wait_ge(S["z_silu"], n + 1)
                dve.sem_inc(S["s_yprod"], 1)
                if n < NT - 1:
                    o = full(dve, "s_loc", n)
                    nxt = s_state[:, (n + 1) % 2, :]
                    if n:
                        link(V.tensor_tensor(h8(nxt), h8(s_state[:, b, :]), over(dec[:, 8 * n:8 * n + 8], 2, 64), ALU.mult))
                        V.tensor_tensor(nxt, nxt, o, ALU.add).then_inc(free_sem("s_loc", n), 1)
                    else:
                        V.tensor_copy(nxt, o).then_inc(free_sem("s_loc", n), 1)
                    drained(dve, "s_loc", n)
                    dve.sem_inc(S["s_new"], 1)
            for item in odd_front():
                if item[0] == "ssd_front":
                    ssd_front(item[1])
                elif item[0] == "ssd_back":
                    ssd_back(item[1])
                elif item[0] == "slot" and item[1] >= 14:
                    shift(ODD_SLOTS[item[1] - 1][1][1])
            shift(ODD_SLOTS[-1][1][1])
            V.tensor_scalar(omka, cols_t[:, A_N + B_AT["rw_k_a"]:A_N + B_AT["rw_k_a"] + 4], -1.0, 1.0,
                            ALU.mult, ALU.add).then_inc(S["omka_ready"], 1)
            dve.wait_ge(S["s_root"], 1)
            link(V.reciprocal(gss, gss))
            for n in range(NT):
                for g in range(2):
                    c = slice(g * 256, g * 256 + 256)
                    ins = V.scalar_tensor_tensor(out=s_y[:, n, c], in0=s_y[:, n, c], scalar=gss[:, 2 * n + g:2 * n + g + 1],
                                                 in1=row("ssm_norm", 512)[:, c], op0=ALU.mult, op1=ALU.mult)
                    if (n, g) == (NT - 1, 1):
                        ins.then_inc(S["y_ssm_ready"], 1)
                    else:
                        link(ins)
            drained(dve, "kk_sum")
            link(V.tensor_scalar(rms_t[0:8, :], rms_t[0:8, :], 1e-12, None, ALU.max))
            V.reciprocal(rms_t[0:8, :], rms_t[0:8, :]).then_inc(S["kk_inverted"], 1)
            def running_decay(f):
                b = f % 2
                if f >= 2:
                    dve.wait_ge(S["tilde_kr"], f - 1)
                    dve.wait_ge(S["tilde"], f - 1)
                drained(dve, "decay", f)
                c = cum_now[:, b, :]
                link(V.tensor_tensor_scan(c, const("reset"), decay_s[:, f, :], 0.0, ALU.mult, ALU.add))
                chunked = c.rearrange("p (n t) -> p n t", n=NT)
                mid = c[:, P // 2 - 1::P]
                end = c[:, P - 1::P]
                link(V.tensor_tensor(e_a[:, f, :], end, mid, ALU.subtract))
                link(V.tensor_tensor(e_a[:, f, 0:NT - 1], e_a[:, f, 0:NT - 1], mid[:, 1:NT], ALU.add))
                link(V.tensor_copy(lnm[:, f, 0:NT], mid))
                link(V.tensor_tensor(chunked, chunked, over(lnm[:, f, 0:NT], 2, P), ALU.subtract))
                V.tensor_tensor(cum_before[:, b, :], c, decay_s[:, f, :], ALU.subtract).then_inc(S["cum_args"], 1)

            running_decay(0)
            for f in range(4):
                if f < 3:
                    running_decay(f + 1)
                r_, k_ = raw[:, f, 1:], raw[:, 4 + f, 1:]
                o = full(dve, "kk_inv", f)
                V.tensor_tensor(kk_s[:, f, :], kk_s[:, f, :], o, ALU.mult).then_inc(free_sem("kk_inv", f), 1)
                drained(dve, "kk_inv", f)
                dve.wait_ge(S["k_gained"], f + 1)
                link(V.tensor_tensor(k_, k_, k_gain[:, f, :], ALU.mult))
                link(V.tensor_tensor(a_s[:, f, :], a_s[:, f, :], kk_s[:, f, :], ALU.mult))
                V.scalar_tensor_tensor(out=mats_rk[:, f, :], in0=r_, scalar=col_b("rw_r_k", f), in1=k_, op0=ALU.mult,
                                       op1=ALU.mult).then_inc(S["rk_ready"], 1)
                dve.wait_ge(S["cum_exps"], f + 1)
                link(V.tensor_tensor(b_s[:, f, :], a_s[:, f, :], cum_now[:, f % 2, :], ALU.mult))
                dve.wait_ge(S["rk_ready"], f + 1)
                V.tensor_tensor(k_, k_, cum_now[:, f % 2, :], ALU.mult).then_inc(S["tilde"], 1)
            dve.wait_ge(S["tilde"], 4)
            dve.wait_ge(S["tilde_kr"], 4)
            dve.wait_ge(S["scales"], 1)
            o = full(dve, "sub", 3, 1).rearrange("p (n s) -> p n s", n=NT)
            for q in range(P // SUB):
                rows = slice(q * SUB, (q + 1) * SUB)
                ins = V.tensor_scalar(sub_tok[rows, :, 7::8].rearrange("p s n -> p n s"), o[rows, :, rows], -1.0, None,
                                      ALU.mult)
            ins.then_inc(free_sem("sub", 3, 1), 1)
            V.memset(sub_inv, 0.0)
            for f in range(4):
                for par in range(2):
                    drained(dve, "sub", f, par)
            V.transpose(sub_prob, sub_tok).then_inc(S["sub_turned"], 1)
            dve.wait_ge(S["sub_turned"], 1)
            o = full(dve, "bonus")
            V.tensor_copy(bon, o[:, 0:32].rearrange("p (n c) -> p n c", n=NT)).then_inc(free_sem("bonus"), 1)

            def masked(n, f, par):
                o = full(dve, "mats", n, f, par)
                V.scalar_tensor_tensor(out=mats[:, 2 * f + par].rearrange("p a b -> p (a b)"), in0=o, scalar=HUGE,
                                       in1=const("four"), op0=ALU.min, op1=ALU.mult
                                       ).then_inc(free_sem("mats", n, f, par), 1)

            diagonal = sub_inv.rearrange("p t c -> p (t c)")[:, ::SUB + 1]
            link(V.tensor_copy(diagonal, ones[:, 0:SUB]))
            for s_ in range(SUB - 1):
                rest, width = SUB - 1 - s_, s_ + 1
                tmp = sub_tmp[:, 0:rest * width].rearrange("p (t c) -> p t c", c=width)
                link(V.tensor_tensor(tmp, over(sub_prob[:, s_, s_ + 1:SUB], 2, width),
                                     over(sub_inv[:, s_, 0:width], 1, rest), ALU.mult))
                below = sub_inv[:, s_ + 1:SUB, 0:width]
                V.tensor_tensor(below, below, tmp, ALU.add).then_inc(dve_step, 1)
                steps[0] += 1
                if s_ % 3 == 2 and s_ < 24:
                    masked(0, s_ // 6, s_ // 3 % 2)
                dve.wait_ge(dve_step, steps[0])
            for n in range(NT):
                full(dve, "rv_tok", n)
            V.transpose(inv_rows, sub_inv.rearrange("p t c -> p c t"))
            link(V.transpose(inv_cols, sub_inv))

            def zero_inverses(n):
                if n:
                    full(dve, "u", n - 1)
                V.memset(inv_d, 0.0)
                V.memset(inv_t, 0.0).then_inc(S["inv_zero"], 1)

            def ln_stats(n):
                drained(dve, "y", n)
                y8 = h8(y_rw[:, n, :])
                link(V.tensor_reduce(lnm[:, n, :], y8, AX.X, ALU.add))
                link(V.tensor_scalar(lnm[:, n, :], lnm[:, n, :], 1.0 / 64, None, ALU.mult))
                link(V.tensor_tensor(y8, y8, over(lnm[:, n, :], 2, 64), ALU.subtract))
                link(V.tensor_tensor(t1, y_rw[:, n, :], y_rw[:, n, :], ALU.mult))
                V.tensor_reduce(lnv[:, n, :], h8(t1), AX.X, ALU.add).then_inc(S["ln2_var"], 1)

            def ln_out(n):
                dve.wait_ge(S["ln2_root"], n + 1)
                link(V.reciprocal(lnv[:, n, :], lnv[:, n, :]))
                drained(dve, "g_tok", n)
                drained(dve, "rv_tok", n)
                y = y_rw[:, n, :]
                link(V.tensor_tensor(h8(y), h8(y), over(lnv[:, n, :], 2, 64), ALU.mult))
                link(V.tensor_tensor(y, y, row("rw_ln_w", 512), ALU.mult))
                link(V.tensor_tensor(y, y, row("rw_ln_b", 512), ALU.add))
                link(V.tensor_tensor(h8(t1), h8(v_tok[:, n, :]), over(bon[:, n, :], 2, 64), ALU.mult))
                link(V.tensor_tensor(y, y, t1, ALU.add))
                V.tensor_tensor(y, y, g_tok[:, n, :], ALU.mult).then_inc(S["y_rw_ready"], 1)

            V.memset(inv_p, 0.0)
            zero_inverses(0)
            pairs = over(const("pairs").rearrange("p (i c) -> p i c", c=SUB), 1, 4)
            for n in range(NT):
                def every_second(ap, b):
                    return ap.rearrange("p a (i b c) -> p a i b c", b=2, c=SUB)[:, :, :, b, :]

                def heads4(ap, b):
                    return every_second(ap.rearrange("p (a t) -> p a t", a=4), b)

                for half in range(2):
                    hs = slice(4 * half, 4 * half + 4)
                    o = heads4(full(dve, "pt", n, 0, half), 1)
                    V.tensor_tensor(every_second(inv_p[:, hs, :], 1), o, pairs, ALU.mult
                                    ).then_inc(free_sem("pt", n, 0, half), 1)
                for half in range(2):
                    hs = slice(4 * half, 4 * half + 4)
                    o = heads4(full(dve, "d", n, half), 0)
                    full(dve, "dt_", n, 0, half)
                    dst = every_second(inv_d[:, hs, :], 0)
                    V.tensor_tensor(dst, dst, o, ALU.subtract).then_inc(free_sem("d", n, half), 1)
                    o = heads4(full(dve, "dt_", n, 0, half), 1)
                    dst = every_second(inv_t[:, hs, :], 1)
                    V.tensor_tensor(dst, dst, o, ALU.subtract).then_inc(free_sem("dt_", n, 0, half), 1)
                if n:
                    ln_stats(n - 1)
                    ln_out(n - 1)
                if n < NT - 1:
                    zero_inverses(n + 1)
                    full(dve, "y", n)
                    for hh in range(2):
                        masked(n + 1, hh // 2, hh % 2)
                    o = full(dve, "s_rw", n)
                    if n:
                        link(V.tensor_tensor(s_sum, s_rw[:, n % 2, :], o, ALU.add))
                    else:
                        link(V.tensor_copy(s_sum, o))
                    for f in range(4):
                        c = slice(f * P, (f + 1) * P)
                        ins = V.scalar_tensor_tensor(out=s_rw[:, (n + 1) % 2, c], in0=s_sum[:, c],
                                                     scalar=e_s[:, f, n:n + 1], in1=blocks, op0=ALU.mult, op1=ALU.mult)
                        if f < 3:
                            link(ins)
                        else:
                            ins.then_inc(free_sem("s_rw", n), 1)
                    drained(dve, "s_rw", n)
                    dve.sem_inc(S["s_rw_ready"], 1)
                    for hh in range(2, 8):
                        masked(n + 1, hh // 2, hh % 2)
            ln_stats(NT - 1)
            ln_out(NT - 1)
            project_out(1)
            norm(3)
            mlp(1)
            drained(dve, "norm", 4)
            V.reciprocal(token_root, token_root).then_inc(S["root_inverted"], 1)
            dve.wait_ge(S["root_inverted"], 1)
            for t in range(NT):
                o = full(dve, "result", t, 1)
                V.tensor_scalar(arena[:, t * D + 512:(t + 1) * D], o, token_root[:, t:t + 1], None, ALU.mult
                                ).then_inc(S["x_out_right"], 1)


PARAMS = ["x", "w_up", "w_down", "e_w_in", "e_w_out", "o_w_in", "o_w_out", "rw_w2", "rw_a2", "rw_g2"]


def kernel(**inputs):
    import concourse.bacc as bacc
    from concourse.bass_utils import run_bass_kernel_spmd

    nc = bacc.Bacc("TRN2", target_bir_lowering=False, num_devices=1)
    arrays, dram = {}, {}
    names = PARAMS + [n for n, _ in STACK_A + STACK_B + ROWS]
    data = {n: np.ascontiguousarray(inputs[n]) for n in names}
    data["main_const"] = np.concatenate([np.asarray(a, np.float32) for _, a in MAIN_COLS], 1)
    data["even_const"] = np.concatenate([np.asarray(a, np.float32) for _, a in EVEN_COLS], 1)
    for name, a in data.items():
        arrays[f"in_{name}"] = a
        dram[name] = nc.dram_tensor(f"in_{name}", a.shape, mybir.dt.from_np(a.dtype), kind="ExternalInput").ap()
    out = nc.dram_tensor("out_0", (1, T, D), F32, kind="ExternalOutput").ap()
    trunk(nc, dram, out)
    r = run_bass_kernel_spmd(nc, [arrays], core_ids=[0])
    return r.results[0]["out_0"]
```
